# Optimizing a Trainium2 kernel written in Bass

```python
import math
import jax
import jax.numpy as jnp
from jax import lax
import numpy as np

D_MODEL = 1024
BATCH = 1
SEQ = 1024
DEPTH = 1

CHUNK = 64
Q_BLOCK = 128

DIFF_HEADS = 4
DIFF_DH = 64
DIFF_QK_W = DIFF_HEADS * 2 * DIFF_DH
DIFF_V_W = DIFF_HEADS * 2 * DIFF_DH

GLA_HEADS = 4
GLA_DK = 64
GLA_DV = 128
GLA_QK_W = GLA_HEADS * GLA_DK
GLA_V_W = GLA_HEADS * GLA_DV
GLA_RANK = 16
GLA_GATE_NORM = 16.0

IN_WIDTHS = (DIFF_QK_W, DIFF_QK_W, DIFF_V_W,
             GLA_QK_W, GLA_QK_W, GLA_V_W, GLA_V_W, GLA_RANK,
             D_MODEL, D_MODEL)
IN_WIDTH = sum(IN_WIDTHS)

N_EXPERTS = 32
TOP_K = 4
D_FF = D_MODEL
SWIGLU_LIMIT = 7.0
SWIGLU_ALPHA = 1.702
MOE_BLOCK = 128

N_MOD = 6
EPS = 1e-6

kernel_name = 'hybrid_diffattn_gla_moe_block'

def rmsnorm(x, g):
    xf = x.astype(jnp.float32)
    y = xf * lax.rsqrt(jnp.mean(xf * xf, axis=-1, keepdims=True) + EPS)
    return (y * g.astype(jnp.float32)).astype(x.dtype)

def alibi_slopes(n_heads):
    return jnp.asarray(2.0 ** (-8.0 * np.arange(1, n_heads + 1) / n_heads), dtype=jnp.float32)

def diff_attention(q, k, v, lam):
    S = q.shape[1]
    slopes = alibi_slopes(DIFF_HEADS)
    pos = jnp.arange(S)
    scale = DIFF_DH ** -0.5
    outs = []
    for i in range(S // Q_BLOCK):
        q0 = i * Q_BLOCK
        kv_len = q0 + Q_BLOCK
        qb = q[:, q0:kv_len]
        kb = k[:, :kv_len]
        vb = v[:, :kv_len]
        s = jnp.einsum('bqhpd,bkhpd->bhpqk', qb, kb).astype(jnp.float32) * scale
        qpos = pos[q0:kv_len]
        kpos = pos[:kv_len]
        allowed = (qpos[:, None] // CHUNK) >= (kpos[None, :] // CHUNK)
        dist = jnp.abs(qpos[:, None] - kpos[None, :]).astype(jnp.float32)
        bias = -slopes[:, None, None] * dist
        s = jnp.where(allowed, s + bias[None, :, None], -jnp.inf)
        p = jax.nn.softmax(s, axis=-1)
        a = p[:, :, 0] - lam * p[:, :, 1]
        outs.append(jnp.einsum('bhqk,bkhe->bqhe', a.astype(vb.dtype), vb))
    return jnp.concatenate(outs, axis=1)

def chunked_gla(q, k, v, g):
    B, S, H, DK = q.shape
    DV = v.shape[-1]
    n = S // CHUNK
    f32 = jnp.float32
    q = q.astype(f32).reshape(B, n, CHUNK, H, DK) * (DK ** -0.5)
    k = k.astype(f32).reshape(B, n, CHUNK, H, DK)
    v = v.astype(f32).reshape(B, n, CHUNK, H, DV)
    G = jnp.cumsum(g.astype(f32).reshape(B, n, CHUNK, H, DK), axis=2)
    G_last = G[:, :, -1:]
    q_s = q * jnp.exp(G)
    k_s = k * jnp.exp(-G)
    k_dec = k * jnp.exp(G_last - G)
    causal = jnp.tril(jnp.ones((CHUNK, CHUNK), dtype=bool))
    A = jnp.einsum('bnchk,bnshk->bnhcs', q_s, k_s)
    A = jnp.where(causal, A, 0.0)
    o_intra = jnp.einsum('bnhcs,bnshv->bnchv', A, v)
    dS = jnp.einsum('bnshk,bnshv->bnhkv', k_dec, v)
    decay = jnp.exp(G_last[:, :, 0])

    def step(state, inp):
        d, ds = inp
        return d[..., None] * state + ds, state

    _, S_prev = lax.scan(step, jnp.zeros((B, H, DK, DV), f32),
                         (jnp.moveaxis(decay, 1, 0), jnp.moveaxis(dS, 1, 0)))
    S_prev = jnp.moveaxis(S_prev, 0, 1)
    o_inter = jnp.einsum('bnchk,bnhkv->bnchv', q_s, S_prev)
    return (o_intra + o_inter).reshape(B, S, H, DV)

def moe_ffn(h, w_router, b_router, w_gate_up, b_gate_up, w_down, b_down):
    B, S, D = h.shape
    N = B * S
    hf = h.reshape(N, D)
    logits = (hf @ w_router + b_router).astype(jnp.float32)
    top_vals, top_idx = lax.top_k(logits, TOP_K)
    weights = jax.nn.softmax(top_vals, axis=-1)
    A = N * TOP_K
    e_flat = top_idx.reshape(A)
    w_flat = weights.reshape(A)
    tok_flat = jnp.arange(A, dtype=jnp.int32) // TOP_K
    order = jnp.argsort(e_flat)
    e_sorted = e_flat[order]
    counts = jnp.bincount(e_flat, length=N_EXPERTS)
    starts = jnp.cumsum(counts) - counts
    padded = ((counts + MOE_BLOCK - 1) // MOE_BLOCK) * MOE_BLOCK
    pad_ends = jnp.cumsum(padded)
    pad_starts = pad_ends - padded
    dest = pad_starts[e_sorted] + (jnp.arange(A) - starts[e_sorted])
    NB = -(-A // MOE_BLOCK) + N_EXPERTS
    P = NB * MOE_BLOCK
    tok_buf = jnp.full((P,), N, dtype=jnp.int32).at[dest].set(tok_flat[order])
    w_buf = jnp.zeros((P,), dtype=jnp.float32).at[dest].set(w_flat[order])
    blk_expert = jnp.minimum(
        jnp.searchsorted(pad_ends, jnp.arange(NB) * MOE_BLOCK, side='right'), N_EXPERTS - 1)
    h_pad = jnp.concatenate([hf, jnp.zeros((1, D), hf.dtype)], axis=0)
    xb = h_pad[tok_buf].reshape(NB, MOE_BLOCK, D)

    def expert_block(args):
        x_i, e = args
        gu = x_i @ w_gate_up[e] + b_gate_up[e]
        gate, up = jnp.split(gu, 2, axis=-1)
        gate = jnp.minimum(gate, SWIGLU_LIMIT)
        up = jnp.clip(up, -SWIGLU_LIMIT, SWIGLU_LIMIT)
        act = (up + 1.0) * (gate * jax.nn.sigmoid(SWIGLU_ALPHA * gate))
        return act @ w_down[e] + b_down[e]

    yb = lax.map(expert_block, (xb, blk_expert)).reshape(P, D)
    y = jax.ops.segment_sum(yb * w_buf[:, None].astype(yb.dtype), tok_buf, num_segments=N + 1)[:N]
    return y.reshape(B, S, D)

def hybrid_layer(x, c, layer_idx, w_ada, b_ada, norm1_g, w_in,
                 lambda_q1, lambda_k1, lambda_q2, lambda_k2, diff_norm_g,
                 w_alpha_up, b_alpha, gla_norm_g, w_branch_diff, w_branch_gla, w_out,
                 norm2_g, w_router, b_router, w_gate_up, b_gate_up, w_down, b_down):
    B, S, D = x.shape
    mod = jax.nn.silu(c) @ w_ada + b_ada
    sh1, sc1, gt1, sh2, sc2, gt2 = jnp.split(mod[:, None, :], N_MOD, axis=-1)

    h = rmsnorm(x, norm1_g) * (1.0 + sc1) + sh1
    proj = h @ w_in
    split_at = list(np.cumsum(IN_WIDTHS)[:-1])
    dq, dk, dv, gq, gk, gv, gr, g_lr, gate_a, gate_b = jnp.split(proj, split_at, axis=-1)

    lambda_init = 0.8 - 0.6 * math.exp(-0.3 * layer_idx)
    lam = (jnp.exp(jnp.sum(lambda_q1 * lambda_k1)) - jnp.exp(jnp.sum(lambda_q2 * lambda_k2))
           + lambda_init).astype(jnp.float32)
    o_a = diff_attention(dq.reshape(B, S, DIFF_HEADS, 2, DIFF_DH),
                         dk.reshape(B, S, DIFF_HEADS, 2, DIFF_DH),
                         dv.reshape(B, S, DIFF_HEADS, 2 * DIFF_DH), lam)
    o_a = (rmsnorm(o_a, diff_norm_g) * (1.0 - lambda_init)).reshape(B, S, DIFF_V_W)

    log_alpha = jax.nn.log_sigmoid((g_lr @ w_alpha_up + b_alpha).astype(jnp.float32)) / GLA_GATE_NORM
    o_b = chunked_gla(gq.reshape(B, S, GLA_HEADS, GLA_DK),
                      gk.reshape(B, S, GLA_HEADS, GLA_DK),
                      gv.reshape(B, S, GLA_HEADS, GLA_DV),
                      log_alpha.reshape(B, S, GLA_HEADS, GLA_DK)).astype(x.dtype)
    o_b = rmsnorm(o_b, gla_norm_g).reshape(B, S, GLA_V_W) * jax.nn.silu(gr)

    merged = (jax.nn.sigmoid(gate_a) * (o_a @ w_branch_diff)
              + jax.nn.sigmoid(gate_b) * (o_b @ w_branch_gla))
    x = x + gt1 * (merged @ w_out)

    h2 = rmsnorm(x, norm2_g) * (1.0 + sc2) + sh2
    x = x + gt2 * moe_ffn(h2, w_router, b_router, w_gate_up, b_gate_up, w_down, b_down)
    return x

def setup_inputs(seed: int = 0) -> dict:
    key = jax.random.key(seed)
    ks = jax.random.split(key, 26)
    f32 = jnp.float32
    L, D, E, F = DEPTH, D_MODEL, N_EXPERTS, D_FF

    def nrm(k, shape, scale):
        return jax.random.normal(k, shape, f32) * scale

    return {
        'x': nrm(ks[0], (BATCH, SEQ, D), 1.0),
        'c': nrm(ks[1], (BATCH, D), 1.0),
        'w_ada': nrm(ks[2], (L, D, N_MOD * D), D ** -0.5),
        'b_ada': nrm(ks[3], (L, N_MOD * D), 0.02),
        'norm1_g': 1.0 + nrm(ks[4], (L, D), 0.1),
        'w_in': nrm(ks[5], (L, D, IN_WIDTH), D ** -0.5),
        'lambda_q1': nrm(ks[6], (L, DIFF_DH), 0.1),
        'lambda_k1': nrm(ks[7], (L, DIFF_DH), 0.1),
        'lambda_q2': nrm(ks[8], (L, DIFF_DH), 0.1),
        'lambda_k2': nrm(ks[9], (L, DIFF_DH), 0.1),
        'diff_norm_g': 1.0 + nrm(ks[10], (L, 2 * DIFF_DH), 0.1),
        'w_alpha_up': nrm(ks[11], (L, GLA_RANK, GLA_QK_W), GLA_RANK ** -0.5),
        'b_alpha': nrm(ks[12], (L, GLA_QK_W), 0.1),
        'gla_norm_g': 1.0 + nrm(ks[13], (L, GLA_DV), 0.1),
        'w_branch_diff': nrm(ks[14], (L, DIFF_V_W, D), DIFF_V_W ** -0.5),
        'w_branch_gla': nrm(ks[15], (L, GLA_V_W, D), GLA_V_W ** -0.5),
        'w_out': nrm(ks[16], (L, D, D), D ** -0.5),
        'norm2_g': 1.0 + nrm(ks[17], (L, D), 0.1),
        'w_router': nrm(ks[18], (L, D, E), D ** -0.5),
        'b_router': nrm(ks[19], (L, E), 0.01),
        'w_gate_up': nrm(ks[20], (L, E, D, 2 * F), D ** -0.5),
        'b_gate_up': nrm(ks[21], (L, E, 2 * F), 0.01),
        'w_down': nrm(ks[22], (L, E, F, D), F ** -0.5),
        'b_down': nrm(ks[23], (L, E, D), 0.01),
        'final_norm_g': 1.0 + nrm(ks[24], (D,), 0.1),
    }

def reference(x, c, w_ada, b_ada, norm1_g, w_in, lambda_q1, lambda_k1, lambda_q2, lambda_k2,
              diff_norm_g, w_alpha_up, b_alpha, gla_norm_g, w_branch_diff, w_branch_gla, w_out,
              norm2_g, w_router, b_router, w_gate_up, b_gate_up, w_down, b_down, final_norm_g):
    for l in range(DEPTH):
        x = hybrid_layer(x, c, l, w_ada[l], b_ada[l], norm1_g[l], w_in[l],
                         lambda_q1[l], lambda_k1[l], lambda_q2[l], lambda_k2[l], diff_norm_g[l],
                         w_alpha_up[l], b_alpha[l], gla_norm_g[l], w_branch_diff[l], w_branch_gla[l],
                         w_out[l], norm2_g[l], w_router[l], b_router[l], w_gate_up[l],
                         b_gate_up[l], w_down[l], b_down[l])
    return rmsnorm(x, final_norm_g)


_drawn_inputs = setup_inputs


def setup_inputs(seed=0):
    import zlib

    import numpy as np

    out = dict(_drawn_inputs(seed))
    spreads = {}
    factors = {'lambda_q1': 125.968,
     'lambda_k2': 142.472,
     'b_gate_up': 8.0,
     'b_down': 8.0,
     'lambda_k1': 5.047}
    for name, (base, spread) in spreads.items():
        noise = np.random.default_rng([zlib.crc32(name.encode()), seed]).standard_normal(out[name].shape)
        drawn = base * np.exp(spread * noise) if base else spread * noise
        out[name] = jnp.asarray(drawn.astype(out[name].dtype))
    for name, factor in factors.items():
        out[name] = (out[name] * factor).astype(out[name].dtype)
    return out
```

```python
from contextlib import ExitStack

import concourse.bass as bass
from concourse import mybir

F32 = mybir.dt.float32
F32R = mybir.dt.float32r
I32 = mybir.dt.int32
U32 = mybir.dt.uint32
ALU = mybir.AluOpType
ACT = mybir.ActivationFunctionType
AX = mybir.AxisListType.X

P = 128
D = 1024
SEQ = 1024
KT = D // P
NT = SEQ // P
CHUNK = 64
HEADS = 4
DH = 64
DV = 128
RANK = 16
NE = 32
TOPK = 4
FF = 1024
EPS = 1e-6
LIMIT = 7.0
ALPHA = 1.702
LAMBDA_INIT = 0.2
MASKED = -1.0e30
N = 512

SLOTS = 2
GROUP = SLOTS * P
MAX_ROUNDS = SEQ * TOPK // GROUP + NE
LIST = SEQ
NO_ROW = 8191
CH = 4
FC = FF // CH
FIRST_K = 6


PASSED = []


def wait_apart(eng, sem, value):
    eng.wait_ge(sem, value)
    eng.sem_inc(PASSED[0], 1)


class Count:

    def __init__(self, eng, sem, base=0):
        self.eng, self.sem, self.base, self.n = eng, sem, base, 0

    def inc(self, ins):
        self.n += 1
        return ins.then_inc(self.sem, 1)

    def wait(self):
        self.eng.wait_ge(self.sem, self.base + self.n)

    def step(self, ins):
        self.inc(ins)
        self.wait()


class Memory:
    pass


def three(pe, out, a, w, first, last):
    pe.matmul(out, a[0], w[0], start=first, stop=False)
    pe.matmul(out, a[0], w[1], start=False, stop=False)
    return pe.matmul(out, a[1], w[0], start=False, stop=last)


def phase_modulate(nc, m):
    sem, sb = m.sem, m.scoped
    with ExitStack() as ctx:
        crow = sb(ctx, "crow", [P, KT], F32)
        csig = sb(ctx, "csig", [P, KT], F32)
        csil = sb(ctx, "csil", [P, KT], F32)
        wada = sb(ctx, "wada", [P, 4, 2 * D], F32)
        part = sb(ctx, "part", [P, 6 * D], F32)
        ones = sb(ctx, "ones_mod", [P, P], F32)
        g1 = sb(ctx, "g1", [P, D], F32)
        g2 = sb(ctx, "g2", [P, D], F32)
        xt = sb(ctx, "xt", [P, 2, D], F32)
        sq = sb(ctx, "sq0", [P, D], F32)
        ht = sb(ctx, "ht", [P, 2, D], F32)
        st = sb(ctx, "st0", [P, NT, 4], F32)
        pm = m.psum(ctx, "pm", [P, 2, N])
        pt = m.psum(ctx, "pt0", [P, 2, D])
        mod = m.mod

        small_in = sem("m_small_in")
        wada_in = [sem(f"m_wada_in{i}") for i in range(4)]
        x_in = [sem(f"m_x_in{i}") for i in range(2)]
        csig_done = sem("m_csig")
        part_done = sem("m_part")
        bcast_done = sem("m_bcast")
        mod_done = sem("m_mod")
        vec = sem("m_vec")
        sumsq_done = sem("m_sumsq")
        root_done = sem("m_root")
        x_used = sem("m_x_used")
        h_done = sem("m_h")
        turned = sem("m_turned")
        hi_done = sem("m_hi")
        lo_done = sem("m_lo")
        const_done = sem("m_const")

        block = ctx.enter_context(nc.Block())

        @block.sync
        def _(sp):
            sp.dma_start(crow[:], m.c_.rearrange("a (k p) -> p (a k)", p=P), allow_slow_non_contiguous=True).then_inc(small_in, 16)
            sp.dma_start(mod[:], m.b_ada[:, 0:5 * D].to_broadcast([P, 5 * D])).then_inc(small_in, 16)
            sp.dma_start(m.gate2[:], m.b_ada[:, 5 * D:6 * D].to_broadcast([P, D])).then_inc(small_in, 16)
            sp.dma_start(g1[:], m.norm1_g.to_broadcast([P, D])).then_inc(small_in, 16)
            sp.dma_start(g2[:], m.norm2_g.to_broadcast([P, D])).then_inc(small_in, 16)
            for j, g in enumerate((m.diff_norm_g, m.gla_norm_g)):
                sp.dma_start(m.cols[:, j:j + 1], g.rearrange("a p -> p a"), allow_slow_non_contiguous=True).then_inc(small_in, 16)
            for g in range(3):
                for k in range(KT):
                    i = g * KT + k
                    if i >= 4:
                        sp.wait_ge(part_done, i - 3)
                    sp.dma_start(wada[:, i % 4, :], m.w_ada[0, k * P:(k + 1) * P, g * 2 * D:(g + 1) * 2 * D]).then_inc(wada_in[i % 4], 16)

        @block.scalar
        def _(act):
            for t in range(2):
                act.dma_start(xt[:, t], m.x[0, t * P:(t + 1) * P, :]).then_inc(x_in[t], 16)
            act.wait_ge(small_in, 112)
            act.activation(csig[:], crow[:], ACT.Sigmoid).then_inc(csig_done, 1)
            act.wait_ge(const_done, 3)
            for t in range(NT):
                act.wait_ge(x_in[t % 2], 16 * (t // 2 + 1))
                if t:
                    act.wait_ge(sumsq_done, t)
                act.activation(sq[:], xt[:, t % 2], ACT.Square, accum_out=st[:, t, 0:1]).then_inc(sumsq_done, 1)
                act.wait_ge(sumsq_done, t + 1)
                act.activation(st[:, t, 1:2], st[:, t, 0:1], ACT.Sqrt, scale=1.0 / D, bias=m.eps[:, 0:1]).then_inc(root_done, 1)
                act.wait_ge(turned, t + 1)
                act.activation(m.hTH[:, :, t * P:(t + 1) * P], pt[:, t % 2].rearrange("p (k n) -> p k n", k=KT), ACT.Copy).then_inc(hi_done, 1)
                if t + 2 < NT:
                    act.wait_ge(x_used, t + 1)
                    act.dma_start(xt[:, t % 2], m.x[0, (t + 2) * P:(t + 3) * P, :]).then_inc(x_in[t % 2], 16)

        @block.gpsimd
        def _(pool):
            pool.memset(m.ident[:], 0.0).then_inc(const_done, 1)
            pool.wait_ge(const_done, 1)
            pool.affine_select(out=m.ident[:], in_=m.ident[:], compare_op=ALU.not_equal, fill=1.0, base=0,
                               pattern=[[-1, P]], channel_multiplier=1).then_inc(const_done, 1)
            pool.memset(m.eps[:], EPS).then_inc(const_done, 1)

        def low(t, dve):
            dve.wait_ge(hi_done, t + 1)
            cols = slice(t * P, (t + 1) * P)
            dve.tensor_tensor(m.hTL[:, :, cols], pt[:, t % 2].rearrange("p (k n) -> p k n", k=KT), m.hTH[:, :, cols].bitcast(F32), ALU.subtract).then_inc(lo_done, 1)

        @block.vector
        def _(dve):
            v = Count(dve, vec)
            v.step(dve.memset(ones[:], 1.0))
            dve.wait_ge(csig_done, 1)
            v.step(dve.tensor_tensor(csil[:], crow[:], csig[:], ALU.mult))
            v.step(dve.tensor_scalar(m.cols[:, 0:1], m.cols[:, 0:1], 1.0 - LAMBDA_INIT, None, ALU.mult))
            for g in range(3):
                cols = part[:, g * 2 * D:(g + 1) * 2 * D]
                for k in range(KT):
                    i = g * KT + k
                    dve.wait_ge(wada_in[i % 4], 16 * (i // 4 + 1))
                    if k == 0:
                        ins = dve.tensor_scalar(cols, wada[:, i % 4], csil[:, k:k + 1], None, ALU.mult)
                    else:
                        dve.wait_ge(part_done, i)
                        ins = dve.scalar_tensor_tensor(out=cols, in0=wada[:, i % 4], scalar=csil[:, k:k + 1], in1=cols,
                                                       op0=ALU.mult, op1=ALU.add)
                    ins.then_inc(part_done, 1)
                for j in range(4):
                    n = g * 4 + j
                    dve.wait_ge(bcast_done, n + 1)
                    to = mod[:, n * N:(n + 1) * N] if n < 10 else m.gate2[:, (n - 10) * N:(n - 9) * N]
                    dve.tensor_tensor(to, pm[:, n % 2], to, ALU.add).then_inc(mod_done, 1)
                if g == 0:
                    dve.wait_ge(mod_done, 4)
                    v.step(dve.scalar_tensor_tensor(out=mod[:, D:2 * D], in0=mod[:, D:2 * D], scalar=1.0, in1=g1[:], op0=ALU.add, op1=ALU.mult))
            dve.wait_ge(mod_done, 12)
            v.step(dve.scalar_tensor_tensor(out=mod[:, 4 * D:5 * D], in0=mod[:, 4 * D:5 * D], scalar=1.0, in1=g2[:], op0=ALU.add, op1=ALU.mult))
            for t in range(NT):
                h = ht[:, t % 2]
                dve.wait_ge(root_done, t + 1)
                v.step(dve.reciprocal(st[:, t, 2:3], st[:, t, 1:2]))
                if t >= 2:
                    dve.wait_ge(turned, t - 1)
                dve.scalar_tensor_tensor(out=h, in0=xt[:, t % 2], scalar=st[:, t, 2:3], in1=mod[:, D:2 * D], op0=ALU.mult, op1=ALU.mult).then_inc(x_used, 1)
                dve.wait_ge(x_used, t + 1)
                dve.tensor_tensor(h, h, mod[:, 0:D], ALU.add).then_inc(h_done, 1)
                if t >= 1:
                    low(t - 1, dve)
            low(NT - 1, dve)

        @block.tensor
        def _(pe):
            pe.wait_ge(vec, 1)
            for g in range(3):
                pe.wait_ge(part_done, (g + 1) * KT)
                for j in range(4):
                    n = g * 4 + j
                    if n >= 2:
                        pe.wait_ge(mod_done, n - 1)
                    pe.matmul(pm[:, n % 2], ones[:], part[:, n * N:(n + 1) * N], start=True, stop=True).then_inc(bcast_done, 1)
            pe.wait_ge(const_done, 2)
            for t in range(NT):
                pe.wait_ge(h_done, t + 1)
                if t >= 2:
                    pe.wait_ge(lo_done, t - 1)
                for k in range(KT):
                    ins = pe.transpose(pt[:, t % 2, k * P:(k + 1) * P], ht[:, t % 2, k * P:(k + 1) * P], m.ident[:])
                ins.then_inc(turned, 1)


UNITS = 8
CHUNKS = 10


def phase_project(nc, m):
    sem, sb = m.sem, m.scoped
    with ExitStack() as ctx:
        raw = sb(ctx, "win_raw", [P, 2, KT, N], F32)
        wH = sb(ctx, "win_hi", [P, 2, KT, N], F32R)
        wL = sb(ctx, "win_lo", [P, 2, KT, N], F32R)
        outb = sb(ctx, "out_stage", [P, 4, N], F32)
        ps = m.psum(ctx, "ps1", [P, 4, N])
        raw_in = [sem(f"p_raw_in{i}") for i in range(2)]
        hi = sem("p_hi")
        lo = sem("p_lo")
        unit = sem("p_unit")
        evac = sem("p_evac")
        stored = [sem(f"p_stored{i}") for i in range(4)]
        block = ctx.enter_context(nc.Block())

        groups = [(0, 4, True, False, 2 * N, m.by_token), (4, 2, False, False, 0, m.qkT),
                  (6, 4, False, True, 6 * N + RANK, m.gatesT)]
        columns = [c + i * N for _, count, _, _, c, _ in groups for i in range(count)] + [6 * N]

        def chunk_pairs(eng, body):
            for first, count, by_token, gated, _, dest in groups:
                if count > 2:
                    with eng.Fori(0, count // 2) as i:
                        for b in range(2):
                            body(first + 2 * i + b, b, by_token, gated, dest, 2 * i + b)
                else:
                    for b in range(2):
                        body(first + b, b, by_token, gated, dest, b)

        @block.gpsimd
        def _(pool):
            w = m.w_in[0].rearrange("(k p) n -> p k n", p=P)
            for q, col in enumerate(columns):
                if q >= 2:
                    pool.wait_ge(lo, (q - 1) * KT)
                pool.dma_start(raw[:, q % 2], w[:, :, col:col + N]).then_inc(raw_in[q % 2], 16)

        @block.sync
        def _(sp):
            for i in range(4):
                sp.sem_inc(stored[i], 16)

            def body(q, b, by_token, gated, dest, j):
                for x in range(UNITS):
                    sp.wait_ge(evac, q * UNITS + x + 5)
                    if by_token:
                        to = dest[bass.ds(j, 1), x * P:(x + 1) * P, :]
                    else:
                        to = dest[bass.ds(j, 1), (x // 2) * P:(x // 2 + 1) * P, (x % 2) * N:(x % 2 + 1) * N]
                    sp.dma_start(to.rearrange("a p n -> p (a n)"), outb[:, x % 4]).then_inc(stored[x % 4], 16)

            chunk_pairs(sp, body)
            for x in range(2):
                sp.wait_ge(evac, CHUNKS * UNITS + x + 5)
                sp.dma_start(m.lrT[:, x * N:(x + 1) * N], outb[0:RANK, x]).then_inc(stored[x], 16)
            for i in range(4):
                sp.wait_ge(stored[i], 16 * (2 * CHUNKS + 1 + (i < 2)))

        @block.scalar
        def _(act):
            def piece(q, b, k):
                act.wait_ge(raw_in[b], 8 * (q - b) + 16)
                act.activation(wH[:, b, k], raw[:, b, k], ACT.Copy).then_inc(hi, 1)

            for k in range(KT):
                piece(0, 0, k)

            def body(q, b, by_token, gated, dest, j):
                for x in range(UNITS):
                    if x == 0:
                        act.wait_ge(unit, (q + 1) * UNITS)
                    piece(q + 1, 1 - b, x)
                    act.wait_ge(unit, q * UNITS + x + 1 + UNITS)
                    act.wait_ge(stored[x % 4], q * 32 + x // 4 * 16 + 16)
                    act.activation(outb[:, x % 4], ps[:, x % 4], ACT.Sigmoid if gated else ACT.Copy).then_inc(evac, 1)

            chunk_pairs(act, body)
            for x in range(2):
                act.wait_ge(unit, CHUNKS * UNITS + x + 1 + UNITS)
                act.wait_ge(stored[x], CHUNKS * 32 + 16)
                act.activation(outb[:, x], ps[:, x], ACT.Copy).then_inc(evac, 1)

        @block.vector
        def _(dve):
            def piece(q, b, k):
                dve.wait_ge(hi, q * KT + k + 1)
                dve.tensor_tensor(wL[:, b, k], raw[:, b, k], wH[:, b, k].bitcast(F32), ALU.subtract).then_inc(lo, 1)

            for k in range(KT):
                piece(0, 0, k)

            def body(q, b, by_token, gated, dest, j):
                dve.wait_ge(unit, (q + 1) * UNITS)
                for x in range(UNITS):
                    piece(q + 1, 1 - b, x)

            chunk_pairs(dve, body)

        @block.tensor
        def _(pe):
            pe.sem_inc(unit, UNITS)
            pe.sem_inc(evac, 4)

            def tile_of(u, b, x, by_token):
                pe.wait_ge(evac, u + 1)
                for k in range(KT):
                    if by_token:
                        a = (m.hTH[:, k, x * P:(x + 1) * P], m.hTL[:, k, x * P:(x + 1) * P])
                        w = (wH[:, b, k], wL[:, b, k])
                    else:
                        mt, half = x // 2, x % 2
                        a = (wH[:, b, k, mt * P:(mt + 1) * P], wL[:, b, k, mt * P:(mt + 1) * P])
                        w = (m.hTH[:, k, half * N:(half + 1) * N], m.hTL[:, k, half * N:(half + 1) * N])
                    ins = three(pe, ps[:, x % 4], a, w, k == 0, k == KT - 1)
                ins.then_inc(unit, 1)

            def body(q, b, by_token, gated, dest, j):
                pe.wait_ge(lo, (q + 1) * KT)
                for x in range(UNITS):
                    tile_of(q * UNITS + x, b, x, by_token)

            chunk_pairs(pe, body)
            pe.wait_ge(lo, (CHUNKS + 1) * KT)
            for x in range(2):
                tile_of(CHUNKS * UNITS + x, 0, x, False)


def phase_gla(nc, m):
    sem, sb = m.sem, m.scoped
    with ExitStack() as ctx:
        qk = sb(ctx, "g_qk", [P, 2, 2, 256], F32)
        gv = sb(ctx, "g_v", [P, 2, HEADS, DV], F32)
        gr = sb(ctx, "g_r", [P, 2, N], F32)
        lr = sb(ctx, "g_lr", [RANK, 2, P], F32)
        wup = sb(ctx, "g_wup", [RANK, 256], F32)
        bal = sb(ctx, "g_bal", [P, 256], F32)
        upto = sb(ctx, "g_upto", [P, P], F32)
        past = sb(ctx, "g_past", [P, P], F32)
        whole = sb(ctx, "g_whole", [P, 2], F32)
        allowed = sb(ctx, "g_allowed", [P, 2, P], I32)
        allowf = sb(ctx, "g_allowf", [P, P], F32)
        zb = sb(ctx, "g_zb", [P, 2, 256], F32)
        la = sb(ctx, "g_la", [P, 256], F32)
        ex = sb(ctx, "g_ex", [P, 3, 256], F32)
        dec = sb(ctx, "g_dec", [P, 4], F32)
        qs = sb(ctx, "g_qs", [P, 3, 256], F32)
        qsT = sb(ctx, "g_qsT", [P, 4, P], F32)
        att = sb(ctx, "g_att", [P, 2, 2, P], F32)
        er = sb(ctx, "g_er", [P, N], F32)
        state = sb(ctx, "g_state", [P, 2, DV], F32)
        sq = sb(ctx, "g_sq", [P, DV], F32)
        nrm = sb(ctx, "g_nrm", [P, 3, 4], F32)
        on = sb(ctx, "g_on", [P, HEADS, DV], F32)
        pG = m.psum(ctx, "pG", [P, 2, 256])
        pz = m.psum(ctx, "pz", [P, N])
        pT = m.psum(ctx, "pT", [P, 4, P])
        pA = m.psum(ctx, "pA", [P, 2, 4, P])
        pO = m.psum(ctx, "pO", [P, 2, 4, P])
        pS = m.psum(ctx, "pS", [P, 4, P])

        once_in = sem("g_once_in")
        tile_in = [sem(f"g_tile_in{i}") for i in range(2)]
        consts = sem("g_consts")
        z_done = sem("g_z")
        abs_done = sem("g_abs")
        soft_done = sem("g_soft")
        la_done = sem("g_la_done")
        sums_done = sem("g_sums")
        exp_done = sem("g_exp")
        er_done = sem("g_er_done")
        scaled_done = sem("g_scaled")
        turned = sem("g_turned")
        qsT_done = sem("g_qsT_done")
        scores = sem("g_scores")
        masked = sem("g_masked")
        delta = sem("g_delta")
        state_done = sem("g_state_done")
        out_done = sem("g_out")
        sumsq = sem("g_sumsq")
        rstd = sem("g_rstd")
        normed = sem("g_normed")
        turned_o = sem("g_turned_o")
        hi = sem("g_hi")
        lo = sem("g_lo")
        vec = sem("g_vec")
        actc = sem("g_act")
        block = ctx.enter_context(nc.Block())

        def tiles(eng, body):
            with eng.Fori(0, NT // 2) as i:
                for b in range(2):
                    body(2 * i + b, b)

        @block.sync
        def _(sp):
            sp.dma_start(wup[:], m.w_alpha_up[0]).then_inc(once_in, 16)
            sp.dma_start(bal[:], m.b_alpha.to_broadcast([P, 256])).then_inc(once_in, 16)
            sp.sem_inc(lo, 2)

            def body(t, b):
                sp.wait_ge(lo, t + 1)
                rows = bass.ds(t * P, P)
                sp.dma_start(qk[:, b].rearrange("p a n -> p (a n)"), m.by_token[1, rows, :]).then_inc(tile_in[b], 16)
                sp.dma_start(gv[:, b].rearrange("p h n -> p (h n)"), m.by_token[2, rows, :]).then_inc(tile_in[b], 16)
                sp.dma_start(gr[:, b], m.by_token[3, rows, :]).then_inc(tile_in[b], 16)
                sp.dma_start(lr[:, b], m.lrT[:, rows]).then_inc(tile_in[b], 16)

            tiles(sp, body)

        @block.gpsimd
        def _(pool):
            c = Count(pool, consts)
            c.step(pool.memset(upto[:], 1.0 / 16))
            c.step(pool.memset(past[:], 1.0 / 16))
            c.step(pool.memset(allowf[:], 1.0))
            for j in range(2):
                c.step(pool.memset(whole[:, j:j + 1], 1.0 / 16))
            for j in range(2):
                cols = slice(j * CHUNK, (j + 1) * CHUNK)
                for tile, w in ((upto[:, cols], CHUNK), (past[:, cols], CHUNK), (allowf[:, cols], CHUNK), (whole[:, j:j + 1], 1)):
                    c.step(pool.affine_select(out=tile, in_=tile, compare_op=ALU.is_ge, fill=0.0, base=-j * CHUNK,
                                              pattern=[[0, w]], channel_multiplier=1))
                    c.step(pool.affine_select(out=tile, in_=tile, compare_op=ALU.is_gt, fill=0.0, base=(j + 1) * CHUNK,
                                              pattern=[[0, w]], channel_multiplier=-1))
            c.step(pool.affine_select(out=upto[:], in_=upto[:], compare_op=ALU.is_ge, fill=0.0, base=0, pattern=[[1, P]], channel_multiplier=-1))
            c.step(pool.affine_select(out=allowf[:], in_=allowf[:], compare_op=ALU.is_ge, fill=0.0, base=0, pattern=[[1, P]], channel_multiplier=-1))
            c.step(pool.affine_select(out=past[:], in_=past[:], compare_op=ALU.is_gt, fill=0.0, base=0, pattern=[[-1, P]], channel_multiplier=1))
            for j in range(2):
                c.inc(pool.tensor_copy(allowed[:, j], allowf[:]))
            m.g_consts = c.n

        @block.tensor
        def _(pe):
            def body(t, b):
                c = t + 1
                pe.wait_ge(tile_in[b], 32 * (t - b) + 64)
                pe.wait_ge(la_done, c)
                pe.matmul(pz[:, 0:256], lr[:, b], wup[:], start=True, stop=True).then_inc(z_done, 1)
                pe.wait_ge(la_done, c + 1)
                pe.matmul(pG[:, 0], upto[:], la[:], start=True, stop=True)
                pe.matmul(pG[:, 1], past[:], la[:], start=True, stop=True)
                for h2 in range(2):
                    ins = pe.matmul(pz[:, 256 + 2 * h2:258 + 2 * h2], la[:, h2 * P:(h2 + 1) * P], whole[:], start=True, stop=True)
                ins.then_inc(sums_done, 1)
                pe.wait_ge(scaled_done, 3 * c + 1)
                for j in range(4):
                    ins = pe.transpose(pT[:, j], qs[:, j // 2, (j % 2) * P:(j % 2 + 1) * P], m.ident[:])
                ins.then_inc(turned, 1)
                pe.wait_ge(qsT_done, c)
                for h in range(HEADS):
                    r = slice((h % 2) * DH, (h % 2 + 1) * DH)
                    ins = pe.matmul(pA[:, h % 2, h // 2], qsT[r, 2 + h // 2], qsT[r, h // 2], start=True, stop=True)
                ins.then_inc(scores, 1)
                pe.wait_ge(masked, 2 * c + 2)
                for h in range(HEADS):
                    pe.matmul(pO[:, h % 2, h // 2], att[:, h % 2, h // 2], gv[:, b, h], start=(h < 2), stop=False, skip_group_check=True)
                for j in range(2):
                    k = 2 * t + j
                    rows = slice(j * CHUNK, (j + 1) * CHUNK)
                    wait_apart(pe, state_done, 2 * k + 2)
                    for h in range(HEADS):
                        r = slice((h % 2) * DH, (h % 2 + 1) * DH)
                        pe.matmul(pO[rows, h % 2, h // 2], qsT[r, h // 2, rows], state[r, h // 2], start=False, stop=(h >= 2), skip_group_check=True)
                    for h in range(HEADS):
                        r = slice((h % 2) * DH, (h % 2 + 1) * DH)
                        ins = pe.matmul(pS[r, h // 2], qs[rows, 2, h * DH:(h + 1) * DH], gv[rows, b, h], start=True, stop=True)
                    ins.then_inc(delta, 1)
                pe.wait_ge(normed, 4 * c + 1)
                for h in range(HEADS):
                    ins = pe.transpose(pT[:, h], on[:, h], m.ident[:])
                ins.then_inc(turned_o, 1)

            pe.wait_ge(once_in, 32)
            pe.wait_ge(consts, m.g_consts)
            tiles(pe, body)

        @block.scalar
        def _(act):
            act.wait_ge(once_in, 32)

            def body(t, b):
                c = t + 1
                act.wait_ge(abs_done, c)
                act.activation(zb[:, 1], zb[:, 1], ACT.Exp, scale=-1.0).then_inc(actc, 1)
                act.wait_ge(actc, 2 * t + 1)
                act.activation(zb[:, 1], zb[:, 1], ACT.Ln, bias=1.0).then_inc(soft_done, 1)
                act.wait_ge(tile_in[b], 32 * (t - b) + 64)
                act.wait_ge(normed, 4 * c - 3)
                act.activation(er[:], gr[:, b], ACT.Exp, scale=-1.0).then_inc(er_done, 1)
                act.wait_ge(sums_done, c)
                act.wait_ge(scaled_done, 3 * t + 1)
                act.activation(ex[:, 0], pG[:, 0], ACT.Exp)
                act.activation(ex[:, 1], pG[:, 0], ACT.Exp, scale=-1.0)
                act.activation(ex[:, 2], pG[:, 1], ACT.Exp)
                act.activation(dec[:], pz[:, 256:260], ACT.Exp).then_inc(exp_done, 1)
                act.wait_ge(turned, c)
                act.activation(qsT[:], pT[:], ACT.Copy).then_inc(qsT_done, 1)
                act.wait_ge(delta, 2 * c)
                for h in range(HEADS):
                    if h:
                        act.wait_ge(sumsq, 4 * t + h)
                    act.activation(sq[:], pO[:, h % 2, h // 2], ACT.Square, accum_out=nrm[:, 0, h:h + 1]).then_inc(sumsq, 1)
                act.wait_ge(sumsq, 4 * c)
                act.activation(nrm[:, 1], nrm[:, 0], ACT.Ln, scale=1.0 / DV, bias=m.eps[:, 0:1]).then_inc(actc, 1)
                act.wait_ge(actc, 2 * t + 2)
                act.activation(nrm[:, 2], nrm[:, 1], ACT.Exp, scale=-0.5).then_inc(rstd, 1)
                act.wait_ge(turned_o, c)
                act.activation(m.oTH[:, HEADS:2 * HEADS, bass.ds(t * P, P)], pT[:], ACT.Copy, scale=m.cols[:, 1:2]).then_inc(hi, 1)

            tiles(act, body)

        @block.vector
        def _(dve):
            v = Count(dve, vec)
            dve.wait_ge(once_in, 32)
            v.step(dve.memset(att[:], 0.0))
            dve.memset(state[:], 0.0).then_inc(state_done, 2)
            dve.sem_inc(la_done, 1)
            dve.sem_inc(masked, 2)
            dve.sem_inc(scaled_done, 1)
            dve.sem_inc(normed, 1)
            dve.wait_ge(consts, m.g_consts)
            start = v.n

            def body(t, b):
                c = t + 1
                v = Count(dve, vec, start + PER * t)
                dve.wait_ge(z_done, c)
                v.step(dve.tensor_tensor(zb[:, 0], pz[:, 0:256], bal[:], ALU.add))
                dve.scalar_tensor_tensor(out=zb[:, 1], in0=zb[:, 0], scalar=-1.0, in1=zb[:, 0], op0=ALU.mult, op1=ALU.max).then_inc(abs_done, 1)
                dve.wait_ge(soft_done, c)
                dve.scalar_tensor_tensor(out=la[:], in0=zb[:, 0], scalar=0.0, in1=zb[:, 1], op0=ALU.min, op1=ALU.subtract).then_inc(la_done, 1)
                dve.wait_ge(er_done, c)
                v.step(dve.tensor_scalar(er[:], er[:], 1.0, None, ALU.add))
                v.step(dve.reciprocal(er[:], er[:]))
                v.step(dve.tensor_tensor(er[:], er[:], gr[:, b], ALU.mult))
                dve.wait_ge(exp_done, c)
                dve.scalar_tensor_tensor(out=qs[:, 0], in0=qk[:, b, 0], scalar=DH ** -0.5, in1=ex[:, 0], op0=ALU.mult, op1=ALU.mult).then_inc(scaled_done, 1)
                for j in range(2):
                    dve.tensor_tensor(qs[:, 1 + j], qk[:, b, 1], ex[:, 1 + j], ALU.mult).then_inc(scaled_done, 1)
                wait_apart(dve, scores, c)
                for j in range(2):
                    dve.copy_predicated(att[:, j], allowed[:], pA[:, j, 0:2]).then_inc(masked, 1)
                for j in range(2):
                    dve.wait_ge(delta, 2 * t + j + 1)
                    for h2 in range(2):
                        dve.scalar_tensor_tensor(out=state[:, h2], in0=state[:, h2], scalar=dec[:, 2 * h2 + j:2 * h2 + j + 1], in1=pS[:, h2],
                                                 op0=ALU.mult, op1=ALU.add).then_inc(state_done, 1)
                dve.wait_ge(rstd, c)
                for h in range(HEADS):
                    dve.scalar_tensor_tensor(out=on[:, h], in0=pO[:, h % 2, h // 2], scalar=nrm[:, 2, h:h + 1], in1=er[:, h * DV:(h + 1) * DV],
                                             op0=ALU.mult, op1=ALU.mult).then_inc(normed, 1)
                dve.wait_ge(hi, c)
                cols = bass.ds(t * P, P)
                dve.scalar_tensor_tensor(out=m.oTL[:, HEADS:2 * HEADS, cols], in0=pT[:], scalar=m.cols[:, 1:2],
                                         in1=m.oTH[:, HEADS:2 * HEADS, cols].bitcast(F32), op0=ALU.mult, op1=ALU.subtract).then_inc(lo, 1)
                assert v.n == PER, v.n

            PER = 4
            tiles(dve, body)


def phase_attention(nc, m):
    sem, sb = m.sem, m.scoped
    with ExitStack() as ctx:
        qT = sb(ctx, "a_qT", [P, 2, SEQ], F32)
        kT = sb(ctx, "a_kT", [P, 2, SEQ], F32)
        vh = sb(ctx, "a_v", [P, 2, NT, DV], F32)
        disti = sb(ctx, "a_disti", [P, SEQ], I32)
        dist = sb(ctx, "a_dist", [P, SEQ], F32)
        bias = sb(ctx, "a_bias", [P, 2, SEQ], F32)
        lam4 = sb(ctx, "a_lam4", [P, 4, DH], F32)
        lam = sb(ctx, "a_lam", [P, 8], F32)
        lamt = sb(ctx, "a_lamt", [P, DH], F32)
        pr = sb(ctx, "a_pr", [P, 2, 2, SEQ], F32)
        mx = sb(ctx, "a_mx", [P, 2, 2], F32)
        nb = sb(ctx, "a_nb", [P, 2, 2], F32)
        sm = sb(ctx, "a_sm", [P, 2, 2], F32)
        ri = sb(ctx, "a_ri", [P, 2, 2], F32)
        at = sb(ctx, "a_at", [P, SEQ], F32)
        aT = sb(ctx, "a_aT", [P, SEQ], F32)
        sq = sb(ctx, "a_sq", [P, DV], F32)
        nrm = sb(ctx, "a_nrm", [P, 4], F32)
        on = sb(ctx, "a_on", [P, DV], F32)
        pS = m.psum(ctx, "paS", [P, 2, SEQ])
        pT = m.psum(ctx, "paT", [P, SEQ])
        pO = m.psum(ctx, "paO", [P, 4, P])
        pQ = m.psum(ctx, "paQ", [P, 4, P])

        once_in = sem("a_once_in")
        head_in = [sem(f"a_head_in{i}") for i in range(2)]
        dist_done = sem("a_dist_done")
        bias_done = sem("a_bias_done")
        lam_done = sem("a_lam_done")
        lame_done = sem("a_lame")
        score = sem("a_score")
        biased = sem("a_biased")
        negmax = sem("a_negmax")
        exped = sem("a_exped")
        mixed = sem("a_mixed")
        vec = sem("a_vec")
        turned = sem("a_turned")
        aT_done = sem("a_aT_done")
        pv = sem("a_pv")
        sumsq = sem("a_sumsq")
        logd = sem("a_logd")
        rstd = sem("a_rstd")
        normed = sem("a_normed")
        turned_o = sem("a_turned_o")
        hi = sem("a_hi")
        lo = sem("a_lo")
        block = ctx.enter_context(nc.Block())
        U = 2 * NT

        def head_pairs(eng, body):
            with eng.Fori(0, HEADS // 2) as i:
                body(i)

        @block.sync
        def _(sp):
            for j, w in enumerate((m.lambda_q1, m.lambda_k1, m.lambda_q2, m.lambda_k2)):
                sp.dma_start(lam4[:, j], w.to_broadcast([P, DH])).then_inc(once_in, 16)

            sp.sem_inc(lo, U)

            def body(i):
                for b in range(2):
                    sp.wait_ge(lo, U * i + (b + 1) * NT)
                    rows = bass.ds((2 * i + b) * P, P)
                    sp.dma_start(qT[:, b], m.qkT[0, rows, :]).then_inc(head_in[b], 16)
                    sp.dma_start(kT[:, b], m.qkT[1, rows, :]).then_inc(head_in[b], 16)
                    sp.dma_start(vh[:, b], m.by_token[0].rearrange("(t p) n -> p t n", p=P)[:, :, rows]).then_inc(head_in[b], 16)

            head_pairs(sp, body)

        @block.gpsimd
        def _(pool):
            pool.iota(disti[:], [[1, SEQ]], base=-(SEQ - P), channel_multiplier=-1).then_inc(dist_done, 1)
            pool.wait_ge(bias_done, 2)
            tail = bias[0:CHUNK, :, SEQ - CHUNK:SEQ]
            pool.memset(tail, MASKED).then_inc(bias_done, 1)

        def of(b, i):
            return b * NT + i

        @block.tensor
        def _(pe):
            def score_of(i0, b, i):
                u = of(b, i) + U * i0
                L = (i + 1) * P
                if i == 0:
                    pe.wait_ge(head_in[b], 48 * (i0 + 1))
                pe.wait_ge(biased, 2 * u + 2)
                for p in range(2):
                    r = slice(p * DH, (p + 1) * DH)
                    for c in range(0, L, N):
                        w = min(N, L - c)
                        ins = pe.matmul(pS[:, p, c:c + w], qT[r, b, i * P:(i + 1) * P], kT[r, b, c:c + w], start=True, stop=True)
                    ins.then_inc(score, 1)

            def value_of(i0, b, i):
                u = of(b, i) + U * i0
                pe.wait_ge(mixed, u + 1)
                pe.wait_ge(aT_done, u + 1)
                for c in range(i + 1):
                    ins = pe.transpose(pT[:, c * P:(c + 1) * P], at[:, c * P:(c + 1) * P], m.ident[:])
                ins.then_inc(turned, 1)
                pe.wait_ge(aT_done, u + 2)
                pe.wait_ge(normed, u + 1)
                for c in range(i + 1):
                    ins = pe.matmul(pO[:, 0], aT[:, c * P:(c + 1) * P], vh[:, b, c], start=(c == 0), stop=(c == i))
                ins.then_inc(pv, 1)

            def out_of(i0, b, i):
                u = of(b, i) + U * i0
                pe.wait_ge(normed, u + 2)
                pe.wait_ge(lo, u + U)
                pe.transpose(pQ[:, 0], on[:], m.ident[:]).then_inc(turned_o, 1)

            pe.sem_inc(biased, 2)

            def body(i0):
                seq = [(b, i) for b in range(2) for i in range(NT)]
                for n in range(U + 2):
                    if n < U:
                        score_of(i0, *seq[n])
                    if n >= 2:
                        out_of(i0, *seq[n - 2])
                    if 1 <= n <= U:
                        value_of(i0, *seq[n - 1])

            head_pairs(pe, body)

        @block.vector
        def _(dve):
            v = Count(dve, vec)
            dve.sem_inc(normed, 1)
            dve.wait_ge(dist_done, 1)
            v.step(dve.tensor_copy(dist[:], disti[:]))
            v.step(dve.scalar_tensor_tensor(out=dist[:], in0=dist[:], scalar=-1.0, in1=dist[:], op0=ALU.mult, op1=ALU.max))
            for h in range(2):
                slope = 2.0 ** (-8.0 * (h + 1) / HEADS)
                dve.tensor_scalar(bias[:, h], dist[:], -slope * DH ** 0.5, None, ALU.mult).then_inc(bias_done, 1)
            dve.wait_ge(once_in, 64)
            for j in range(2):
                v.step(dve.tensor_tensor(lamt[:], lam4[:, 2 * j], lam4[:, 2 * j + 1], ALU.mult))
                v.step(dve.reduce_sum(lam[:, j:j + 1], lamt[:], axis=AX))
            dve.sem_inc(lam_done, 1)
            dve.wait_ge(lame_done, 1)
            v.step(dve.tensor_tensor(lam[:, 4:5], lam[:, 3:4], lam[:, 2:3], ALU.subtract))
            v.step(dve.tensor_scalar(lam[:, 5:6], lam[:, 4:5], -LAMBDA_INIT, None, ALU.add))
            dve.wait_ge(bias_done, 3)
            start = v.n

            def body(i0):
                v = Count(dve, vec, start + PER * i0)

                def bias_of(b, i):
                    u = of(b, i) + U * i0
                    L = (i + 1) * P
                    s = i % 2
                    table = bias[:, b, SEQ - L:SEQ]
                    for p in range(2):
                        wait_apart(dve, score, 2 * u + p + 1)
                        dve.tensor_tensor_reduce(out=pr[:, s, p, 0:L], in0=pS[:, p, 0:L], in1=table, scale=1.0, scalar=-3.0e38,
                                                 op0=ALU.add, op1=ALU.max, accum_out=mx[:, s, p:p + 1]).then_inc(biased, 1)
                    dve.wait_ge(biased, 2 * u + 4)
                    dve.tensor_scalar(nb[:, s], mx[:, s], -DH ** -0.5, None, ALU.mult).then_inc(negmax, 1)

                def mix_of(b, i):
                    u = of(b, i) + U * i0
                    L = (i + 1) * P
                    s = i % 2
                    dve.wait_ge(exped, 2 * u + 2)
                    v.step(dve.reciprocal(ri[:, s], sm[:, s]))
                    v.step(dve.tensor_tensor(ri[:, s, 1:2], ri[:, s, 1:2], lam[:, 5:6], ALU.mult))
                    dve.wait_ge(turned, u + 1)
                    v.step(dve.tensor_scalar(at[:, 0:L], pr[:, s, 0, 0:L], ri[:, s, 0:1], None, ALU.mult))
                    dve.scalar_tensor_tensor(out=at[:, 0:L], in0=pr[:, s, 1, 0:L], scalar=ri[:, s, 1:2], in1=at[:, 0:L],
                                             op0=ALU.mult, op1=ALU.add).then_inc(mixed, 1)

                def norm_of(b, i):
                    u = of(b, i) + U * i0
                    dve.wait_ge(rstd, u + 1)
                    dve.wait_ge(turned_o, u + 1)
                    dve.tensor_scalar(on[:], pO[:, 0], nrm[:, 2:3], None, ALU.mult).then_inc(normed, 1)

                def low_of(b, i):
                    u = of(b, i) + U * i0
                    dve.wait_ge(hi, u + 1)
                    at_ = (slice(None), bass.ds(2 * i0 + b, 1), slice(i * P, (i + 1) * P))
                    dve.scalar_tensor_tensor(out=m.oTL[at_].rearrange("p a n -> p (a n)"), in0=pQ[:, 0], scalar=m.cols[:, 0:1],
                                             in1=m.oTH[at_].bitcast(F32).rearrange("p a n -> p (a n)"), op0=ALU.mult, op1=ALU.subtract).then_inc(lo, 1)

                seq = [(b, i) for b in range(2) for i in range(NT)]
                for n in range(U + 3):
                    if n < U:
                        bias_of(*seq[n])
                    if 1 <= n <= U:
                        mix_of(*seq[n - 1])
                    if 2 <= n <= U + 1:
                        norm_of(*seq[n - 2])
                    if n >= 3:
                        low_of(*seq[n - 3])
                v.step(dve.tensor_scalar(bias[:], bias[:], 2.0 ** (-16.0 / HEADS), None, ALU.mult))
                assert v.n == PER, v.n

            PER = 3 * U + 1
            head_pairs(dve, body)

        @block.scalar
        def _(act):
            act.wait_ge(lam_done, 1)
            act.activation(lam[:, 2:4], lam[:, 0:2], ACT.Exp).then_inc(lame_done, 1)
            act.sem_inc(aT_done, 1)
            act.sem_inc(turned, 1)
            act.sem_inc(turned_o, 1)

            def body(i0):
                def exp_of(b, i):
                    u = of(b, i) + U * i0
                    L = (i + 1) * P
                    s = i % 2
                    act.wait_ge(negmax, u + 1)
                    for p in range(2):
                        act.activation(pr[:, s, p, 0:L], pr[:, s, p, 0:L], ACT.Exp, bias=nb[:, s, p:p + 1], scale=DH ** -0.5,
                                       accum_out=sm[:, s, p:p + 1]).then_inc(exped, 1)

                def copy_of(b, i):
                    u = of(b, i) + U * i0
                    act.wait_ge(turned, u + 2)
                    act.wait_ge(pv_free, u + 1)
                    act.activation(aT[:, 0:(i + 1) * P], pT[:, 0:(i + 1) * P], ACT.Copy).then_inc(aT_done, 1)

                def root_of(b, i):
                    u = of(b, i) + U * i0
                    act.wait_ge(pv, u + 2)
                    act.activation(sq[:], pO[:, 0], ACT.Square, accum_out=nrm[:, 0:1]).then_inc(sumsq, 1)
                    act.wait_ge(sumsq, u + 1)
                    act.activation(nrm[:, 1:2], nrm[:, 0:1], ACT.Ln, scale=1.0 / DV, bias=m.eps[:, 0:1]).then_inc(logd, 1)
                    act.wait_ge(logd, u + 1)
                    act.activation(nrm[:, 2:3], nrm[:, 1:2], ACT.Exp, scale=-0.5).then_inc(rstd, 1)

                def high_of(b, i):
                    u = of(b, i) + U * i0
                    act.wait_ge(turned_o, u + 2)
                    to = m.oTH[:, bass.ds(2 * i0 + b, 1), i * P:(i + 1) * P].rearrange("p a n -> p (a n)")
                    act.activation(to, pQ[:, 0], ACT.Copy, scale=m.cols[:, 0:1]).then_inc(hi, 1)

                seq = [(b, i) for b in range(2) for i in range(NT)]
                for n in range(U + 3):
                    if n < U:
                        exp_of(*seq[n])
                    if 1 <= n <= U:
                        copy_of(*seq[n - 1])
                        root_of(*seq[n - 1])
                    if 2 <= n <= U + 1:
                        high_of(*seq[n - 2])

            pv_free = pv
            act.sem_inc(pv, 1)
            head_pairs(act, body)


def phase_merge(nc, m):
    sem, sb = m.sem, m.scoped
    with ExitStack() as ctx:
        raw = sb(ctx, "wb_raw", [P, 2, 2, HEADS, P], F32)
        wH = sb(ctx, "wb_hi", [P, 2, 2 * HEADS, P], F32R)
        wL = sb(ctx, "wb_lo", [P, 2, 2 * HEADS, P], F32R)
        gate = sb(ctx, "gate_in", [P, 2, 2, SEQ], F32)
        tmp = sb(ctx, "merge_tmp", [P, 2, N], F32)
        mg = sb(ctx, "merge_out", [P, 2, N], F32)
        ps = m.psum(ctx, "ps3", [P, 2, 2, N])
        raw_in = [sem(f"b_raw_in{i}") for i in range(2)]
        gate_in = [sem(f"b_gate_in{i}") for i in range(2)]
        whi = sem("b_whi")
        wlo = sem("b_wlo")
        unit = sem("b_unit")
        scaled = sem("b_scaled")
        summed = sem("b_summed")
        hi = sem("b_hi")
        lo = sem("b_lo")
        block = ctx.enter_context(nc.Block())

        def tiles(eng, body):
            with eng.Fori(0, KT // 2) as i:
                for b in range(2):
                    body(2 * i + b, b)

        @block.sync
        def _(sp):
            sp.sem_inc(wlo, 2)
            sp.sem_inc(lo, 4)

            def body(q, b):
                sp.wait_ge(wlo, q + 1)
                cols = bass.ds(q * P, P)
                for j, w in enumerate((m.w_branch_diff, m.w_branch_gla)):
                    sp.dma_start(raw[:, b, j], w[0].rearrange("(k p) n -> p k n", p=P)[:, :, cols]).then_inc(raw_in[b], 16)
                sp.wait_ge(lo, 2 * q + 2)
                for j in range(2):
                    sp.dma_start(gate[:, b, j], m.gatesT.rearrange("(j a) r n -> j (a r) n", j=2)[j, cols, :]).then_inc(gate_in[b], 16)

            tiles(sp, body)

        @block.scalar
        def _(act):
            act.sem_inc(unit, 4)

            def body(q, b):
                act.wait_ge(raw_in[b], 16 * (q - b) + 32)
                act.wait_ge(unit, 2 * q + 2)
                act.activation(wH[:, b].rearrange("p k n -> p (k n)"), raw[:, b].rearrange("p j k n -> p (j k n)"), ACT.Copy).then_inc(whi, 1)
                for half in range(2):
                    u = 2 * q + half
                    act.wait_ge(summed, u + 1)
                    act.activation(m.mTH[:, bass.ds(q, 1), half * N:(half + 1) * N].rearrange("p a n -> p (a n)"), mg[:, half], ACT.Copy).then_inc(hi, 1)

            tiles(act, body)

        @block.vector
        def _(dve):
            def body(q, b):
                dve.wait_ge(whi, q + 1)
                dve.tensor_tensor(wL[:, b].rearrange("p k n -> p (k n)"), raw[:, b].rearrange("p j k n -> p (j k n)"),
                                  wH[:, b].bitcast(F32).rearrange("p k n -> p (k n)"), ALU.subtract).then_inc(wlo, 1)
                dve.wait_ge(gate_in[b], 16 * (q - b) + 32)
                for half in range(2):
                    u = 2 * q + half
                    cols = slice(half * N, (half + 1) * N)
                    dve.wait_ge(unit, u + 5)
                    for j in range(2):
                        dve.tensor_tensor(tmp[:, j], ps[:, half, j], gate[:, b, j, cols], ALU.mult).then_inc(scaled, 1)
                    dve.wait_ge(scaled, 2 * u + 6)
                    dve.tensor_tensor(mg[:, half], tmp[:, 0], tmp[:, 1], ALU.add).then_inc(summed, 1)
                    dve.wait_ge(hi, u + 1)
                    to = (slice(None), bass.ds(q, 1), cols)
                    dve.tensor_tensor(m.mTL[to].rearrange("p a n -> p (a n)"), mg[:, half], m.mTH[to].bitcast(F32).rearrange("p a n -> p (a n)"), ALU.subtract).then_inc(lo, 1)

            tiles(dve, body)

        @block.tensor
        def _(pe):
            pe.sem_inc(scaled, 4)

            def body(q, b):
                pe.wait_ge(wlo, q + 3)
                for half in range(2):
                    u = 2 * q + half
                    pe.wait_ge(scaled, 2 * u + 2)
                    cols = slice(half * N, (half + 1) * N)
                    for j in range(2):
                        for k in range(HEADS):
                            kk = j * HEADS + k
                            ins = three(pe, ps[:, half, j], (wH[:, b, kk], wL[:, b, kk]), (m.oTH[:, kk, cols], m.oTL[:, kk, cols]), k == 0, k == HEADS - 1)
                    ins.then_inc(unit, 1)

            tiles(pe, body)


def phase_out(nc, m):
    sem, sb = m.sem, m.scoped
    with ExitStack() as ctx:
        raw = sb(ctx, "wo_raw", [P, 2, D], F32)
        wH = sb(ctx, "wo_hi", [P, KT, D], F32R)
        wL = sb(ctx, "wo_lo", [P, KT, D], F32R)
        xt = sb(ctx, "o_x", [P, 2, D], F32)
        x2 = sb(ctx, "o_x2", [P, 2, D], F32)
        h2 = sb(ctx, "o_h2", [P, 2, D], F32)
        h2T = sb(ctx, "o_h2T", [P, D], F32)
        sq = sb(ctx, "o_sq", [P, D], F32)
        nrm = sb(ctx, "o_nrm", [P, NT, 4], F32)
        wr = sb(ctx, "o_wr", [P, KT, NE], F32)
        br = sb(ctx, "o_br", [P, NE], F32)
        ps = m.psum(ctx, "ps4", [P, 2, D])
        pT = m.psum(ctx, "pT4", [P, D])
        pL = m.psum(ctx, "pL4", [P, N])
        once_in = sem("o_once_in")
        raw_in = [sem(f"o_raw_in{i}") for i in range(2)]
        x_in = [sem(f"o_x_in{i}") for i in range(2)]
        whi = sem("o_whi")
        wlo = sem("o_wlo")
        unit = sem("o_unit")
        resid = sem("o_resid")
        added = sem("o_added")
        sumsq = sem("o_sumsq")
        logd = sem("o_logd")
        rstd = sem("o_rstd")
        norm = sem("o_norm")
        h2_done = sem("o_h2_done")
        turned = sem("o_turned")
        h2T_done = sem("o_h2T_done")
        logit = sem("o_logit")
        logit_out = sem("o_logit_out")
        stored = [sem(f"o_stored{i}") for i in range(2)]
        block = ctx.enter_context(nc.Block())

        @block.sync
        def _(sp):
            for k in range(KT):
                if k >= 2:
                    sp.wait_ge(wlo, k - 1)
                sp.dma_start(raw[:, k % 2], m.w_out[0, k * P:(k + 1) * P, :]).then_inc(raw_in[k % 2], 16)
                if k < 2:
                    sp.dma_start(xt[:, k], m.x[0, k * P:(k + 1) * P, :]).then_inc(x_in[k], 16)
            sp.dma_start(wr[:], m.w_router[0].rearrange("(k p) n -> p k n", p=P)).then_inc(once_in, 16)
            sp.dma_start(br[:], m.b_router.to_broadcast([P, NE])).then_inc(once_in, 16)
            for t in range(NT):
                rows = slice(t * P, (t + 1) * P)
                sp.wait_ge(added, t + 1)
                sp.dma_start(m.x2[rows, :], x2[:, t % 2]).then_inc(stored[t % 2], 16)
                if t + 2 < NT:
                    sp.dma_start(xt[:, t % 2], m.x[0, (t + 2) * P:(t + 3) * P, :]).then_inc(x_in[t % 2], 16)
                sp.wait_ge(h2_done, t + 1)
                sp.dma_start(m.h2[rows, :], h2[:, t % 2]).then_inc(stored[t % 2], 16)
            for b in range(2):
                sp.wait_ge(stored[b], 32 * (NT // 2))

        @block.scalar
        def _(act):
            for k in range(KT):
                act.wait_ge(raw_in[k % 2], 16 * (k // 2 + 1))
                act.activation(wH[:, k], raw[:, k % 2], ACT.Copy).then_inc(whi, 1)
            for t in range(NT):
                act.wait_ge(added, t + 1)
                act.activation(sq[:], x2[:, t % 2], ACT.Square, accum_out=nrm[:, t, 0:1]).then_inc(sumsq, 1)
                act.wait_ge(sumsq, t + 1)
                act.activation(nrm[:, t, 1:2], nrm[:, t, 0:1], ACT.Ln, scale=1.0 / D, bias=m.eps[:, 0:1]).then_inc(logd, 1)
                act.wait_ge(logd, t + 1)
                act.activation(nrm[:, t, 2:3], nrm[:, t, 1:2], ACT.Exp, scale=-0.5).then_inc(rstd, 1)
                act.wait_ge(turned, t + 1)
                if t:
                    act.wait_ge(logit, t)
                act.activation(h2T[:], pT[:], ACT.Copy).then_inc(h2T_done, 1)

        @block.vector
        def _(dve):
            for k in range(KT):
                dve.wait_ge(whi, k + 1)
                dve.tensor_tensor(wL[:, k], raw[:, k % 2], wH[:, k].bitcast(F32), ALU.subtract).then_inc(wlo, 1)
            dve.wait_ge(once_in, 32)
            for t in range(NT):
                b = t % 2
                dve.wait_ge(unit, t + 1)
                dve.wait_ge(x_in[b], 16 * (t // 2 + 1))
                if t >= 2:
                    dve.wait_ge(stored[b], 32 * (t // 2))
                dve.tensor_tensor(x2[:, b], ps[:, b], m.mod[:, 2 * D:3 * D], ALU.mult).then_inc(resid, 1)
                dve.wait_ge(resid, t + 1)
                dve.tensor_tensor(x2[:, b], x2[:, b], xt[:, b], ALU.add).then_inc(added, 1)
                dve.wait_ge(rstd, t + 1)
                dve.scalar_tensor_tensor(out=h2[:, b], in0=x2[:, b], scalar=nrm[:, t, 2:3], in1=m.mod[:, 4 * D:5 * D], op0=ALU.mult, op1=ALU.mult).then_inc(norm, 1)
                dve.wait_ge(norm, t + 1)
                dve.tensor_tensor(h2[:, b], h2[:, b], m.mod[:, 3 * D:4 * D], ALU.add).then_inc(h2_done, 1)
                dve.wait_ge(logit, t + 1)
                dve.tensor_tensor(m.logits[:, t], pL[:, 0:NE], br[:], ALU.add).then_inc(logit_out, 1)

        @block.tensor
        def _(pe):
            def product(t):
                if t >= 2:
                    pe.wait_ge(resid, t - 1)
                rows = slice(t * P, (t + 1) * P)
                for half in range(2):
                    cols = slice(half * N, (half + 1) * N)
                    for k in range(KT):
                        if t == 0 and half == 0:
                            pe.wait_ge(wlo, k + 1)
                        ins = three(pe, ps[:, t % 2, cols], (m.mTH[:, k, rows], m.mTL[:, k, rows]), (wH[:, k, cols], wL[:, k, cols]), k == 0, k == KT - 1)
                ins.then_inc(unit, 1)

            def route(t):
                pe.wait_ge(h2_done, t + 1)
                if t:
                    pe.wait_ge(h2T_done, t)
                    pe.wait_ge(logit_out, t)
                for k in range(KT):
                    ins = pe.transpose(pT[:, k * P:(k + 1) * P], h2[:, t % 2, k * P:(k + 1) * P], m.ident[:])
                ins.then_inc(turned, 1)
                pe.wait_ge(h2T_done, t + 1)
                for k in range(KT):
                    ins = pe.matmul(pL[:, 0:NE], h2T[:, k * P:(k + 1) * P], wr[:, k], start=(k == 0), stop=(k == KT - 1))
                ins.then_inc(logit, 1)

            pe.wait_ge(once_in, 32)
            for t in range(NT + 1):
                if t < NT:
                    product(t)
                if t:
                    route(t - 1)


def phase_route(nc, m):
    sem, sb = m.sem, m.scoped
    ROWS = MAX_ROUNDS + 2
    with ExitStack() as ctx:
        top = sb(ctx, "r_top", [P, NT, 8], F32)
        idx = sb(ctx, "r_idx", [P, NT, 8], U32)
        idf = sb(ctx, "r_idf", [P, NT, 8], F32)
        sh = sb(ctx, "r_sh", [P, NT, TOPK], F32)
        tot = sb(ctx, "r_tot", [P, NT], F32)
        eidi = sb(ctx, "r_eidi", [P, NE], I32)
        eid = sb(ctx, "r_eid", [P, NE], F32)
        hot = sb(ctx, "r_hot", [P, TOPK, NT, NE], F32)
        mask = sb(ctx, "r_mask", [P, NT, NE], F32)
        before = sb(ctx, "r_before", [P, P], F32)
        ones = sb(ctx, "r_ones", [P, P], F32)
        rank = sb(ctx, "r_rank", [P, NT, NE], F32)
        tmp = sb(ctx, "r_tmp", [P, TOPK, NT, NE], F32)
        slot = sb(ctx, "r_slot", [P, TOPK, NT], F32)
        slotu = sb(ctx, "r_slotu", [P, TOPK, NT], U32)
        entry = sb(ctx, "r_entry", [P, TOPK, NT, 2], I32)
        pads = sb(ctx, "r_pads", [P, NE * LIST // P, 2], I32)
        cnt = sb(ctx, "r_cnt", [NE, 8], F32)
        cnti = sb(ctx, "r_cnti", [NE, 4], I32)
        rid = sb(ctx, "r_rid", [NE, ROWS], F32)
        ridi = sb(ctx, "r_ridi", [NE, ROWS], I32)
        pidi = sb(ctx, "r_pidi", [NE, 1], I32)
        pid = sb(ctx, "r_pid", [NE, 1], F32)
        rh = sb(ctx, "r_rh", [NE, 2, ROWS], F32)
        rv = sb(ctx, "r_rv", [NE, 4, ROWS], F32)
        row = sb(ctx, "r_row", [1, 4, ROWS], F32)
        row2 = sb(ctx, "r_row2", [1, 8, ROWS], F32)
        pr = m.psum(ctx, "pr5", [P, NT, NE])
        pc = m.psum(ctx, "pc5", [P, 4, P])
        pw = m.psum(ctx, "pw5", [P, N])
        ptab = m.psum(ctx, "pt5", [P, N])
        vec = sem("r_vec")
        pad_set = sem("r_pad_set")
        pool_set = sem("r_pool_set")
        cast = sem("r_cast")
        exped = sem("r_exped")
        shifted = sem("r_shifted")
        masked = sem("r_masked")
        ranked = sem("r_ranked")
        ranks_out = sem("r_ranks_out")
        counted = sem("r_counted")
        cum_in = sem("r_cum_in")
        cummed = sem("r_cummed")
        rows_in = sem("r_rows_in")
        rows_out = sem("r_rows_out")
        weighed = sem("r_weighed")
        wc_out = sem("r_wc_out")
        slots = sem("r_slots")
        padded = sem("r_padded")
        listed = sem("r_listed")
        block = ctx.enter_context(nc.Block())

        @block.gpsimd
        def _(pool):
            c = Count(pool, pool_set)
            c.step(pool.memset(pads[:, :, 0:1], 0))
            pool.memset(pads[:, :, 1:2], NO_ROW).then_inc(pad_set, 1)
            pool.wait_ge(pad_set, 1)
            pool.dma_start(m.lists.rearrange("(p n) c -> p n c", p=P), pads[:]).then_inc(padded, 16)
            c.step(pool.iota(eidi[:], [[1, NE]], base=0, channel_multiplier=0))
            c.step(pool.iota(ridi[:], [[1, ROWS]], base=0, channel_multiplier=0))
            c.step(pool.iota(pidi[:], [[0, 1]], base=0, channel_multiplier=1))
            c.step(pool.iota(entry[:, :, :, 0], [[0, TOPK], [P, NT]], base=0, channel_multiplier=1))
            c.step(pool.iota(entry[:, :, :, 1], [[1, TOPK], [P * TOPK, NT]], base=0, channel_multiplier=TOPK))
            c.step(pool.memset(ones[:], 1.0))
            c.step(pool.memset(before[:], 1.0))
            c.step(pool.affine_select(out=before[:], in_=before[:], compare_op=ALU.is_gt, fill=0.0, base=0, pattern=[[1, P]], channel_multiplier=-1))
            pool.wait_ge(slots, 1)
            pool.wait_ge(padded, 16)
            for k in range(TOPK):
                for t in range(NT):
                    pool.indirect_dma_start(out=m.lists[:, :], out_offset=bass.IndirectOffsetOnAxis(ap=slotu[:, k, t:t + 1], axis=0),
                                            in_=entry[:, k, t, :], in_offset=None).then_inc(listed, 16)
            pool.wait_ge(listed, 16 * TOPK * NT)

        @block.scalar
        def _(act):
            act.wait_ge(shifted, 1)
            act.activation(sh[:], sh[:], ACT.Exp).then_inc(exped, 1)

        @block.tensor
        def _(pe):
            pe.wait_ge(pool_set, 9)
            pe.wait_ge(masked, 1)
            for t in range(NT):
                for s in range(t):
                    pe.matmul(pr[:, t], ones[:], mask[:, s], start=(s == 0), stop=False)
                ins = pe.matmul(pr[:, t], before[:], mask[:, t], start=(t == 0), stop=True)
            ins.then_inc(ranked, 1)
            for t in range(NT):
                ins = pe.matmul(pc[0:NE, 0, 0:1], mask[:, t], ones[:, 0:1], start=(t == 0), stop=(t == NT - 1))
            ins.then_inc(counted, 1)
            pe.wait_ge(cum_in, 1)
            pe.matmul(pw[0:NE, 0:4], before[0:NE, 0:NE], cnt[:, 0:4], start=True, stop=True).then_inc(cummed, 1)
            pe.wait_ge(rows_in, 1)
            for j in range(4):
                ins = pe.matmul(ptab[0:1, j * ROWS:(j + 1) * ROWS], ones[0:NE, 0:1], rv[:, j], start=True, stop=True)
            pe.matmul(ptab[0:1, 4 * ROWS:4 * ROWS + 1], ones[0:NE, 0:1], cnt[:, 0:1], start=True, stop=True).then_inc(rows_out, 1)
            for t in range(NT):
                pe.wait_ge(weighed, t + 1)
                pe.transpose(pc[0:NE, 1], tmp[:, 0, t], m.ident[:]).then_inc(wc_out, 1)

        @block.vector
        def _(dve):
            v = Count(dve, vec)
            dve.wait_ge(pool_set, 9)
            v.step(dve.tensor_copy(eid[:], eidi[:]))
            v.step(dve.tensor_copy(rid[:], ridi[:]))
            v.step(dve.tensor_copy(pid[:], pidi[:]))
            for t in range(NT):
                v.step(dve.max(top[:, t], m.logits[:, t]))
                v.step(dve.max_index(idx[:, t], top[:, t], m.logits[:, t]))
            v.step(dve.tensor_copy(idf[:], idx[:]))
            for t in range(NT):
                ins = dve.tensor_scalar(sh[:, t], top[:, t, 0:TOPK], top[:, t, 0:1], None, ALU.subtract)
            ins.then_inc(shifted, 1)
            for k in range(TOPK):
                for t in range(NT):
                    v.inc(dve.tensor_scalar(hot[:, k, t], eid[:], idf[:, t, k:k + 1], None, ALU.is_equal))
            v.wait()
            v.step(dve.tensor_tensor(mask[:], hot[:, 0], hot[:, 1], ALU.add))
            v.step(dve.tensor_tensor(mask[:], mask[:], hot[:, 2], ALU.add))
            dve.tensor_tensor(mask[:], mask[:], hot[:, 3], ALU.add).then_inc(masked, 1)
            dve.wait_ge(exped, 1)
            v.step(dve.reduce_sum(tot[:], sh[:], axis=AX))
            v.step(dve.reciprocal(tot[:], tot[:]))
            for t in range(NT):
                v.inc(dve.tensor_scalar(m.wtop[:, t], sh[:, t], tot[:, t:t + 1], None, ALU.mult))
            dve.wait_ge(counted, 1)
            c = cnt
            v.step(dve.tensor_scalar(c[:, 4:5], pc[0:NE, 0, 0:1], 1.0, None, ALU.max))
            v.step(dve.tensor_scalar(c[:, 5:6], c[:, 4:5], GROUP / 2 - 0.5, 1.0 / GROUP, ALU.add, ALU.mult))
            v.step(dve.tensor_scalar(c[:, 6:7], c[:, 4:5], P / 2 - 0.5, 1.0 / P, ALU.add, ALU.mult))
            v.step(dve.tensor_copy(cnti[:, 0:2], c[:, 5:7]))
            v.step(dve.tensor_copy(c[:, 0:2], cnti[:, 0:2]))
            v.step(dve.tensor_copy(c[:, 2:4], cnti[:, 0:2]))
            dve.sem_inc(cum_in, 1)
            dve.wait_ge(cummed, 1)
            v.step(dve.tensor_copy(c[:, 4:6], pw[0:NE, 0:2]))
            v.step(dve.tensor_tensor(c[:, 6:7], c[:, 4:5], c[:, 0:1], ALU.add))
            v.step(dve.tensor_scalar(rh[:, 0], rid[:], c[:, 4:5], None, ALU.is_ge))
            v.step(dve.tensor_scalar(rh[:, 1], rid[:], c[:, 6:7], None, ALU.is_lt))
            v.step(dve.tensor_tensor(rh[:, 0], rh[:, 0], rh[:, 1], ALU.mult))
            v.step(dve.tensor_scalar(rh[:, 1], rid[:], c[:, 4:5], None, ALU.subtract))
            v.step(dve.tensor_scalar(rv[:, 0], rh[:, 0], pid[:, 0:1], None, ALU.mult))
            v.step(dve.tensor_tensor(rv[:, 1], rh[:, 0], rh[:, 1], ALU.mult))
            v.step(dve.tensor_scalar(rv[:, 2], rh[:, 0], c[:, 1:2], None, ALU.mult))
            v.step(dve.tensor_scalar(rv[:, 3], rh[:, 0], c[:, 5:6], None, ALU.mult))
            dve.sem_inc(rows_in, 1)
            dve.wait_ge(rows_out, 1)
            v.step(dve.tensor_copy(row[:].rearrange("p a n -> p (a n)"), ptab[0:1, 0:4 * ROWS]))
            v.step(dve.tensor_copy(row2[:, 0], row[:, 0]))
            v.step(dve.tensor_scalar(row2[:, 4], row[:, 1], float(GROUP), None, ALU.mult))
            v.step(dve.scalar_tensor_tensor(out=row2[:, 1], in0=row[:, 0], scalar=float(LIST), in1=row2[:, 4], op0=ALU.mult, op1=ALU.add))
            v.step(dve.scalar_tensor_tensor(out=row2[:, 5], in0=row[:, 1], scalar=-2.0, in1=row[:, 2], op0=ALU.mult, op1=ALU.add))
            v.step(dve.tensor_scalar(row2[:, 2], row2[:, 5], 2.0, None, ALU.is_ge))
            v.step(dve.scalar_tensor_tensor(out=row2[:, 6], in0=row[:, 1], scalar=2.0, in1=row[:, 3], op0=ALU.mult, op1=ALU.add))
            v.step(dve.tensor_scalar(row2[:, 3], row2[:, 6], 4.0, None, ALU.mult))
            for j in range(4):
                v.inc(dve.tensor_copy(m.table[:, :, j], row2[:, j]))
            v.step(dve.tensor_copy(m.rounds[:], ptab[0:1, 4 * ROWS:4 * ROWS + 1]))
            dve.wait_ge(ranked, 1)
            v.step(dve.tensor_copy(rank[:], pr[:]))
            for k in range(TOPK):
                v.inc(dve.tensor_tensor(tmp[:, k], hot[:, k], rank[:], ALU.mult))
            v.wait()
            for k in range(TOPK):
                v.inc(dve.reduce_sum(slot[:, k], tmp[:, k], axis=AX))
            v.wait()
            for k in range(TOPK):
                v.inc(dve.scalar_tensor_tensor(out=slot[:, k], in0=idf[:, :, k], scalar=float(LIST), in1=slot[:, k], op0=ALU.mult, op1=ALU.add))
            v.wait()
            dve.tensor_copy(slotu[:], slot[:]).then_inc(slots, 1)
            for t in range(NT):
                v.inc(dve.tensor_scalar(tmp[:, 0, t], hot[:, 0, t], m.wtop[:, t, 0:1], None, ALU.mult))
            v.wait()
            for k in range(1, TOPK):
                for t in range(NT):
                    ins = dve.scalar_tensor_tensor(out=tmp[:, 0, t], in0=hot[:, k, t], scalar=m.wtop[:, t, k:k + 1], in1=tmp[:, 0, t], op0=ALU.mult, op1=ALU.add)
                    v.inc(ins)
                v.wait()
            dve.sem_inc(weighed, 1)
            for t in range(NT):
                dve.wait_ge(wc_out, t + 1)
                dve.tensor_copy(m.wcT[:, t], pc[0:NE, 1]).then_inc(weighed, 1)


def phase_experts(nc, m):
    sem, sb = m.sem, m.scoped
    KD = FC // P
    QG = 4
    with ExitStack() as ctx:
        gu_raw = sb(ctx, "e_gu_raw", [P, 2, KT, 2, FC], F32)
        gu_hi = sb(ctx, "e_gu_hi", [P, 2, KT, 2 * FC], F32R)
        gu_lo = sb(ctx, "e_gu_lo", [P, 2, KT, 2 * FC], F32R)
        dn_raw = sb(ctx, "e_dn_raw", [P, 2, KD, D], F32)
        dn_hi = sb(ctx, "e_dn_hi", [P, 2, KD, D], F32R)
        dn_lo = sb(ctx, "e_dn_lo", [P, 2, KD, D], F32R)
        bias = sb(ctx, "e_bias", [P, 2, 2, FC], F32)
        rows = sb(ctx, "e_rows", [P, SLOTS, 2], I32)
        dest = sb(ctx, "e_dest", [P, 2, SLOTS], I32)
        xg = sb(ctx, "e_xg", [P, SLOTS, D], F32)
        xT = sb(ctx, "e_xT", [P, SLOTS, KT, P], F32)
        x_hi = sb(ctx, "e_x_hi", [P, SLOTS, KT, P], F32R)
        x_lo = sb(ctx, "e_x_lo", [P, SLOTS, KT, P], F32R)
        gb = sb(ctx, "e_gb", [P, 2, FC], F32)
        sg = sb(ctx, "e_sg", [P, FC], F32)
        av = sb(ctx, "e_act", [P, FC], F32)
        a_hi = sb(ctx, "e_a_hi", [P, KD, P], F32R)
        a_lo = sb(ctx, "e_a_lo", [P, KD, P], F32R)
        ys = sb(ctx, "e_y", [P, D], F32)
        warm = sb(ctx, "e_warm", [P, 1], F32)
        p_gu = m.psum(ctx, "e_pgu", [P, 2, 2, FC])
        p_dn = m.psum(ctx, "e_pdn", [P, SLOTS, D])
        p_at = m.psum(ctx, "e_pat", [P, N])
        p_xt = m.psum(ctx, "e_pxt", [P, N])

        gu_in = [[sem(f"e_gu_in{i}{half}") for half in range(2)] for i in range(2)]
        dn_in = [sem(f"e_dn_in{i}") for i in range(2)]
        bias_in = [sem(f"e_bias_in{i}") for i in range(2)]
        gu_hi_done = sem("e_gu_hi_done")
        gu_lo_done = sem("e_gu_lo_done")
        dn_hi_done = sem("e_dn_hi_done")
        dn_lo_done = sem("e_dn_lo_done")
        hidden = sem("e_hidden")
        x_half_used = sem("e_x_half_used")
        with_bias = sem("e_with_bias")
        clamped = sem("e_clamped")
        up_clamped = sem("e_up_clamped")
        sigm = sem("e_sigmoid")
        gated = sem("e_gated")
        activated = sem("e_activated")
        a_turned = sem("e_a_turned")
        a_hi_done = sem("e_a_hi_done")
        a_lo_done = sem("e_a_lo_done")
        dn_done = sem("e_dn_done")
        x_hi_done = sem("e_x_hi_done")
        x_lo_done = sem("e_x_lo_done")
        x1_hi_done = sem("e_x1_hi_done")
        x1_lo_done = sem("e_x1_lo_done")
        gathered = [sem(f"e_gathered{i}") for i in range(SLOTS)]
        x_turned = sem("e_x_turned")
        xT_done = sem("e_xT_done")
        rows_in = sem("e_rows_in")
        dest_kept = sem("e_dest_kept")
        y_out = sem("e_y_out")
        scattered = sem("e_scattered")
        block = ctx.enter_context(nc.Block())

        w_gu = m.w_gate_up[0].rearrange("e (k p) (g n) -> e p k g n", p=P, g=2)
        w_dn = m.w_down[0].rearrange("e (k p) n -> e p k n", p=P)
        b_gu = m.b_gate_up[0].rearrange("e (g n) -> e g n", g=2)

        def entry(eng, r, j, top):
            return eng.value_load(m.table[0:1, bass.ds(r, 1), j:j + 1].rearrange("p a b -> p (a b)"), min_val=0, max_val=top)

        def expert_of(eng, r):
            return entry(eng, r, 0, NE - 1)

        def rounds(eng, body):
            n = eng.value_load(m.rounds[0:1, 0:1], min_val=1, max_val=MAX_ROUNDS)
            with eng.Fori(0, n) as r:
                U = eng.snap(entry(eng, r, 3, 4 * (MAX_ROUNDS * SLOTS)))
                two = entry(eng, r, 2, 1)
                with eng.If(two > 0):
                    body(r, U, True)
                with eng.Else():
                    body(r, U, False)
            return eng.snap(entry(eng, n - 1, 3, 4 * (MAX_ROUNDS * SLOTS)) + 4 + 4 * entry(eng, n - 1, 2, 1)), n

        def units(two):
            slots = (1, 0) if two else (0,)
            seq = [(c, s) for c in range(CH) for s in slots]
            for l, (c, s) in enumerate(seq):
                yield l, c, s, s == 0, seq[l - 1]

        def after_first(eng, r, l, body):
            if l == 0:
                with eng.If(r > 0):
                    body()
            else:
                body()

        @block.sync
        def _(sp):
            def gu(e, c, b, half):
                k = slice(half * (KT // 2), (half + 1) * (KT // 2))
                for g in range(2):
                    src = w_gu[bass.ds(e, 1), :, k, g, c * FC:(c + 1) * FC].rearrange("a p k n -> p (a k) n")
                    sp.dma_start(gu_raw[:, b, k, g], src).then_inc(gu_in[b][half], 16)

            def dn(e, c, b):
                sp.dma_start(dn_raw[:, b], w_dn[bass.ds(e, 1), :, c * KD:(c + 1) * KD, :].rearrange("a p k n -> p (a k) n")).then_inc(dn_in[b], 16)

            def bs(e, c, b):
                sp.dma_start(bias[:, b], b_gu[bass.ds(e, 1), :, c * FC:(c + 1) * FC].to_broadcast([P, 2, FC])).then_inc(bias_in[b], 16)

            e0 = expert_of(sp, 0)
            for half in range(2):
                gu(e0, 0, 0, half)
            bs(e0, 0, 0)
            for half in range(2):
                gu(e0, 1, 1, half)
            dn(e0, 0, 0)
            dn(e0, 1, 1)
            for half in range(2):
                wait_apart(sp, gu_lo_done, (half + 1) * QG // 2)
                gu(e0, 2, 0, half)

            def body(r, U, two):
                here, there = expert_of(sp, r), expert_of(sp, r + 1)
                q4 = sp.snap(4 * r)
                for c in range(CH):
                    wait_apart(sp, with_bias, U + c * (1 + two) + 2)
                    bs(here if c < 3 else there, (c + 1) % CH, (c + 1) % 2)
                    for half in range(2):
                        wait_apart(sp, gu_lo_done, QG * q4 + QG * (c + 1) + (half + 1) * QG // 2)
                        gu(here if c == 0 else there, (c + 3) % CH, (c + 1) % 2, half)
                    wait_apart(sp, dn_lo_done, KD * q4 + KD * (c + 1))
                    dn(here if c < 2 else there, (c + 2) % CH, c % 2)

            rounds(sp, body)
            n = sp.value_load(m.rounds[0:1, 0:1], min_val=1, max_val=MAX_ROUNDS)
            for half in range(2):
                wait_apart(sp, gu_in[0][half], 64 * n + 64)
                wait_apart(sp, gu_in[1][half], 64 * n + 32)
            for b in range(2):
                wait_apart(sp, dn_in[b], 32 * n + 16)
            wait_apart(sp, bias_in[0], 32 * n + 16)
            wait_apart(sp, bias_in[1], 32 * n)

        @block.gpsimd
        def _(pool):
            def fetch(r):
                at = entry(pool, r, 1, NE * LIST - GROUP)
                pool.dma_start(rows[:], m.lists[bass.ds(at, GROUP), :].rearrange("(s p) c -> p s c", p=P)).then_inc(rows_in, 16)

            def gather(s):
                pool.indirect_dma_start(out=xg[:, s], out_offset=None, in_=m.h2[:, :],
                                        in_offset=bass.IndirectOffsetOnAxis(ap=rows[:, s, 0:1].bitcast(U32), axis=0)).then_inc(gathered[s], 16)

            def scatter(s, blocks):
                wait_apart(pool, y_out, blocks + 2)
                pool.indirect_dma_start(out=m.y4[:, :], out_offset=bass.IndirectOffsetOnAxis(ap=dest[:, 0, s:s + 1].bitcast(U32), axis=0),
                                        in_=ys[:], in_offset=None, bounds_check=SEQ * TOPK - 1, oob_is_err=False).then_inc(scattered, 16)

            pool.dma_start(rows[:], m.lists[0:GROUP, :].rearrange("(s p) c -> p s c", p=P)).then_inc(scattered, 16)
            wait_apart(pool, scattered, 16)
            fetch(0)
            wait_apart(pool, rows_in, 16)
            gather(1)
            gather(0)
            for s in range(SLOTS):
                wait_apart(pool, gathered[s], 16)
            pool.tensor_copy(dest[:, 1], rows[:, :, 1]).then_inc(dest_kept, 1)
            wait_apart(pool, dest_kept, 1)
            fetch(1)

            def body(r, U, two):
                B = pool.snap(U // 4)
                wait_apart(pool, rows_in, 16 * r + 32)
                wait_apart(pool, x_turned, 4 * r + 4)
                gather(1)
                gather(0)
                with pool.If(r > 0):
                    scatter(0, B)
                    wait_apart(pool, scattered, 16 * B + 16)
                pool.tensor_copy(dest[:, 0], dest[:, 1]).then_inc(dest_kept, 1)
                for s in range(SLOTS):
                    wait_apart(pool, gathered[s], 16 * r + 32)
                wait_apart(pool, dest_kept, 2 * r + 2)
                pool.tensor_copy(dest[:, 1], rows[:, :, 1]).then_inc(dest_kept, 1)
                wait_apart(pool, dest_kept, 2 * r + 3)
                fetch(r + 2)
                if two:
                    scatter(1, B + 1)

            total, n = rounds(pool, body)
            B = pool.snap(total // 4)
            scatter(0, B)
            wait_apart(pool, scattered, 16 * B + 16)
            for s in range(SLOTS):
                wait_apart(pool, gathered[s], 16 * n + 16)
            wait_apart(pool, rows_in, 16 * n + 32)

        @block.tensor
        def _(pe):
            pe.sem_inc(hidden, 2)
            pe.sem_inc(x_half_used, 1)
            pe.sem_inc(dn_done, 2)
            pe.sem_inc(y_out, 2)

            def turn_x(r, i):
                count = 4 * r + i
                if i % 2 == 0:
                    pe.wait_ge(gathered[1 - i // 2], 16 * r + 16)
                pe.wait_ge(xT_done, count + 1)
                for k in range(4):
                    kk = 4 * (i % 2) + k
                    ins = pe.transpose(p_xt[:, k * P:(k + 1) * P], xg[:, 1 - i // 2, kk * P:(kk + 1) * P], m.ident[:])
                ins.then_inc(x_turned, 1)

            def turn_a(n):
                pe.wait_ge(activated, n + 1)
                pe.wait_ge(a_lo_done, n + 1)
                for k in range(KD):
                    ins = pe.transpose(p_at[:, k * P:(k + 1) * P], av[:, k * P:(k + 1) * P], m.ident[:])
                ins.then_inc(a_turned, 1)

            def down(n, q, blocks, c, s):
                pe.wait_ge(a_lo_done, n + 2)
                pe.wait_ge(dn_lo_done, KD * q + KD)
                if c == 0:
                    pe.wait_ge(y_out, blocks)
                for half in range(2):
                    cols = slice(half * N, (half + 1) * N)
                    for k in range(KD):
                        ins = three(pe, p_dn[:, s, cols], (a_hi[:, k], a_lo[:, k]), (dn_hi[:, c % 2, k, cols], dn_lo[:, c % 2, k, cols]),
                                    c == 0 and k == 0, c == CH - 1 and k == KD - 1)
                ins.then_inc(dn_done, 1)

            for i in range(4):
                turn_x(0, i)

            def body(r, U, two):
                B = pe.snap(U // 4)
                q4 = pe.snap(4 * r)
                for l, c, s, last, (pc, ps) in units(two):
                    n = U + l
                    pe.wait_ge(with_bias, n + 1)
                    if c == 0 and s == 1:
                        pe.wait_ge(x1_lo_done, r + 1)
                    for k in range(KT):
                        if c == 0 and s == 0 and k % (KT // 2) == 0:
                            pe.wait_ge(x_lo_done, 2 * r + 2 * k // KT + 1)
                        if k == (FIRST_K if l else 3):
                            after_first(pe, r, l, lambda: turn_a(n - 1))
                        if k == FIRST_K and s == 0 and c >= 2:
                            turn_x(r + 1, 2 * c - 3)
                        if (s == 1 or not two) and k % 2 == 0:
                            pe.wait_ge(gu_lo_done, QG * q4 + QG * c + k // 2 + 1)
                        ins = three(pe, p_gu[:, l % 2].rearrange("p g n -> p (g n)"), (x_hi[:, s, k], x_lo[:, s, k]),
                                    (gu_hi[:, c % 2, k], gu_lo[:, c % 2, k]), k == 0, k == KT - 1)
                        if c == CH - 1 and last and k == KT // 2 - 1:
                            ins.then_inc(x_half_used, 1)
                    ins.then_inc(hidden, 1)
                    after_first(pe, r, l, lambda: down(n - 1, q4 + (pc if l else -1), B + 2, pc, ps))
                    if s == 0 and c in (1, 2):
                        turn_x(r + 1, 2 * c - 2)

            total, n = rounds(pe, body)
            turn_a(total - 1)
            down(total - 1, 4 * n - 1, 0, CH - 1, 0)

        @block.scalar
        def _(act):
            def gu_piece(r, c, j):
                b = c % 2
                if j % 2 == 0:
                    act.wait_ge(gu_in[b][j // 2], 64 * r + 32 * (c // 2) + 32)
                act.activation(gu_hi[:, b, 2 * j:2 * j + 2], gu_raw[:, b, 2 * j:2 * j + 2].rearrange("p k g n -> p k (g n)"), ACT.Copy).then_inc(gu_hi_done, 1)

            def dn_piece(r, c, j):
                b = c % 2
                if j == 0:
                    act.wait_ge(dn_in[b], 32 * r + 16 * (c // 2) + 16)
                act.activation(dn_hi[:, b, j], dn_raw[:, b, j], ACT.Copy).then_inc(dn_hi_done, 1)

            def stage_x(r, i):
                count = 4 * r + i
                act.wait_ge(x_turned, count + 1)
                act.activation(xT[:, 1 - i // 2, 4 * (i % 2):4 * (i % 2) + 4].rearrange("p k n -> p (k n)"), p_xt[:], ACT.Copy).then_inc(xT_done, 1)

            def sigmoid(n):
                act.wait_ge(clamped, n + 1)
                act.activation(sg[:], gb[:, 0], ACT.Sigmoid, scale=ALPHA).then_inc(sigm, 1)

            def high_x(r, half):
                act.wait_ge(xT_done, 4 * r + 4 + half)
                k = slice(half * (KT // 2), (half + 1) * (KT // 2))
                act.activation(x_hi[:, 0, k], xT[:, 0, k], ACT.Copy).then_inc(x_hi_done, 1)

            def high_x1(r):
                act.wait_ge(xT_done, 4 * r + 3)
                act.activation(x_hi[:, 1], xT[:, 1], ACT.Copy).then_inc(x1_hi_done, 1)

            def high_a(n):
                act.wait_ge(a_turned, n + 1)
                act.wait_ge(dn_done, n + 2)
                act.activation(a_hi[:].rearrange("p k n -> p (k n)"), p_at[:, 0:FC], ACT.Copy).then_inc(a_hi_done, 1)

            def evacuate(n, s, blocks):
                act.wait_ge(dn_done, n + 3)
                act.wait_ge(scattered, 16 * blocks + 16)
                act.activation(ys[:], p_dn[:, s], ACT.Copy).then_inc(y_out, 1)

            act.sem_inc(xT_done, 1)
            for j in range(QG):
                gu_piece(0, 0, j)
            for i in range(4):
                stage_x(0, i)
            high_x1(0)
            high_x(0, 0)
            high_x(0, 1)

            def body(r, U, two):
                B = act.snap(U // 4)
                act.activation(warm[:], m.eps[:], ACT.Sigmoid)
                for l, c, s, last, (pc, ps) in units(two):
                    n = U + l
                    nc_, nr = ((c + 1) % CH, r + (c == CH - 1))
                    if not two:
                        todo = [("g", 0), ("g", 1), ("g", 2), ("g", 3), ("d", 0), ("d", 1)]
                    elif s == 1:
                        todo = [("g", 0), ("d", 0), ("d", 1)]
                    else:
                        todo = [("g", 1), ("g", 2), ("g", 3)]
                    if s == 1 or not two:
                        act.wait_ge(hidden, n + 2)

                    def piece():
                        if todo:
                            kind, j = todo.pop(0)
                            if kind == "d":
                                if j == 0:
                                    act.wait_ge(dn_done, n + 1)
                                dn_piece(r, c, j)
                            else:
                                gu_piece(nr, nc_, j)

                    piece()
                    if l:
                        sigmoid(n - 1)
                        piece()
                        piece()
                    after_first(act, r, l, lambda: high_a(n - 1))
                    if s == 0 and c >= 2:
                        stage_x(r + 1, 2 * c - 3)
                    if (c, s) == ((CH - 1, 0) if two else (CH - 2, 0)):
                        high_x1(r + 1)
                    if (c, s) == (CH - 1, 0):
                        act.wait_ge(x_half_used, r + 2)
                        high_x(r + 1, 0)
                        piece()
                        act.wait_ge(hidden, n + 3)
                        high_x(r + 1, 1)
                        sigmoid(n)
                    if l == 1:
                        after_first(act, r, 0, lambda: evacuate(n - 2, 0, B - 1))
                    while todo:
                        piece()
                    if s == 0 and c in (1, 2):
                        if c == 1:
                            act.wait_ge(x1_lo_done, r + 1)
                        stage_x(r + 1, 2 * c - 2)
                if two:
                    evacuate(n - 1, 1, B)

            total, n = rounds(act, body)
            high_a(total - 1)
            evacuate(total - 1, 0, act.snap(total // 4) - 1)

        @block.vector
        def _(dve):
            def gu_piece(count, c, j):
                b = c % 2
                dve.wait_ge(gu_hi_done, count + 1)
                dve.tensor_tensor(gu_lo[:, b, 2 * j:2 * j + 2], gu_raw[:, b, 2 * j:2 * j + 2].rearrange("p k g n -> p k (g n)"),
                                  gu_hi[:, b, 2 * j:2 * j + 2].bitcast(F32), ALU.subtract).then_inc(gu_lo_done, 1)

            def dn_piece(count, c, j):
                b = c % 2
                dve.wait_ge(dn_hi_done, count + 1)
                dve.tensor_tensor(dn_lo[:, b, j], dn_raw[:, b, j], dn_hi[:, b, j].bitcast(F32), ALU.subtract).then_inc(dn_lo_done, 1)

            def with_biases(n, c, parity, in_count):
                dve.wait_ge(hidden, n + 3)
                dve.wait_ge(bias_in[c % 2], in_count)
                dve.tensor_tensor(gb[:], p_gu[:, parity], bias[:, c % 2], ALU.add).then_inc(with_bias, 1)
                dve.wait_ge(with_bias, n + 3)
                dve.tensor_scalar(gb[:, 0], gb[:, 0], LIMIT, None, ALU.min).then_inc(clamped, 1)
                dve.tensor_scalar(gb[:, 1], gb[:, 1], -LIMIT, LIMIT, ALU.max, ALU.min).then_inc(up_clamped, 1)

            def activate(n):
                dve.wait_ge(sigm, n + 1)
                dve.tensor_tensor(sg[:], gb[:, 0], sg[:], ALU.mult).then_inc(gated, 1)
                dve.wait_ge(gated, n + 1)
                dve.wait_ge(up_clamped, n + 1)
                dve.scalar_tensor_tensor(out=av[:], in0=gb[:, 1], scalar=1.0, in1=sg[:], op0=ALU.add, op1=ALU.mult).then_inc(activated, 1)

            def low_x1(r):
                dve.wait_ge(x1_hi_done, r + 1)
                dve.tensor_tensor(x_lo[:, 1], xT[:, 1], x_hi[:, 1].bitcast(F32), ALU.subtract).then_inc(x1_lo_done, 1)

            def low_x(r, half):
                k = slice(half * (KT // 2), (half + 1) * (KT // 2))
                dve.wait_ge(x_hi_done, 2 * r + half + 1)
                dve.tensor_tensor(x_lo[:, 0, k], xT[:, 0, k], x_hi[:, 0, k].bitcast(F32), ALU.subtract).then_inc(x_lo_done, 1)

            def low_a(n):
                dve.wait_ge(a_hi_done, n + 1)
                dve.tensor_tensor(a_lo[:].rearrange("p k n -> p (k n)"), p_at[:, 0:FC], a_hi[:].rearrange("p k n -> p (k n)").bitcast(F32),
                                  ALU.subtract).then_inc(a_lo_done, 1)

            dve.sem_inc(with_bias, 2)
            dve.sem_inc(a_lo_done, 1)
            for j in range(QG):
                gu_piece(j, 0, j)
            low_x1(0)
            low_x(0, 0)
            low_x(0, 1)

            def body(r, U, two):
                for l, c, s, last, (pc, ps) in units(two):
                    n = U + l
                    if not two:
                        todo = [("g", 0), ("g", 1), ("g", 2), ("g", 3), ("d", 0), ("d", 1)]
                    elif s == 1:
                        todo = [("g", 0), ("d", 0), ("d", 1)]
                    else:
                        todo = [("g", 1), ("g", 2), ("g", 3)]

                    def piece():
                        if todo:
                            kind, j = todo.pop(0)
                            if kind == "d":
                                dn_piece(8 * r + KD * c + j, c, j)
                            else:
                                gu_piece(16 * r + QG * (c + 1) + j, c + 1, j)

                    if l:
                        with_biases(n - 1, pc, (l - 1) % 2, 32 * r + 16 * (pc // 2) + 16)
                    piece()
                    if l:
                        activate(n - 1)
                        piece()
                    after_first(dve, r, l, lambda: low_a(n - 1))
                    if (c, s) == ((CH - 1, 0) if two else (CH - 2, 0)):
                        low_x1(r + 1)
                    if (c, s) == (CH - 1, 0):
                        low_x(r + 1, 0)
                        with_biases(n, c, l % 2, 32 * r + 32)
                        low_x(r + 1, 1)
                        activate(n)
                    while todo:
                        piece()

            total, n = rounds(dve, body)
            low_a(total - 1)


def phase_combine(nc, m):
    sem, sb = m.sem, m.scoped
    with ExitStack() as ctx:
        y = sb(ctx, "c_y", [P, 2, TOPK, D], F32)
        x2 = sb(ctx, "c_x2", [P, 2, D], F32)
        bd = sb(ctx, "c_bd", [NE, D], F32)
        gf = sb(ctx, "c_gf", [P, D], F32)
        acc = sb(ctx, "c_acc", [P, 2, D], F32)
        res = sb(ctx, "c_res", [P, 2, D], F32)
        sq = sb(ctx, "c_sq", [P, D], F32)
        nrm = sb(ctx, "c_nrm", [P, NT, 4], F32)
        ps = m.psum(ctx, "ps7", [P, 2, D])
        once_in = sem("c_once_in")
        y_in = [sem(f"c_y_in{i}") for i in range(2)]
        biased = sem("c_biased")
        weighed = sem("c_weighed")
        summed = sem("c_summed")
        gated = sem("c_gated")
        x3 = sem("c_x3")
        sumsq = sem("c_sumsq")
        logd = sem("c_logd")
        rstd = sem("c_rstd")
        done = sem("c_done")
        out_done = [sem(f"c_out{i}") for i in range(2)]
        block = ctx.enter_context(nc.Block())

        @block.sync
        def _(sp):
            sp.dma_start(bd[:], m.b_down[0]).then_inc(once_in, 16)
            sp.dma_start(gf[:], m.final_g.rearrange("(a d) -> a d", a=1).to_broadcast([P, D])).then_inc(once_in, 16)
            for t in range(NT):
                b = t % 2
                if t >= 2:
                    sp.wait_ge(x3, t - 1)
                sp.dma_start(y[:, b], m.y4.rearrange("(t p k) n -> t p k n", p=P, k=TOPK)[t]).then_inc(y_in[b], 16)
                sp.dma_start(x2[:, b], m.x2[t * P:(t + 1) * P, :]).then_inc(y_in[b], 16)

        @block.tensor
        def _(pe):
            pe.wait_ge(once_in, 32)
            for t in range(NT):
                if t >= 2:
                    pe.wait_ge(weighed, TOPK * (t - 2) + 1)
                for half in range(2):
                    cols = slice(half * N, (half + 1) * N)
                    ins = pe.matmul(ps[:, t % 2, cols], m.wcT[:, t], bd[:, cols], start=True, stop=True)
                ins.then_inc(biased, 1)

        @block.vector
        def _(dve):
            dve.wait_ge(once_in, 32)
            for t in range(NT):
                b = t % 2
                dve.wait_ge(y_in[b], 32 * (t // 2 + 1))
                dve.wait_ge(biased, t + 1)
                for k in range(TOPK):
                    if k:
                        dve.wait_ge(weighed, TOPK * t + k)
                    dve.scalar_tensor_tensor(out=acc[:, b], in0=y[:, b, k], scalar=m.wtop[:, t, k:k + 1], in1=acc[:, b] if k else ps[:, b],
                                             op0=ALU.mult, op1=ALU.add).then_inc(weighed, 1)
                dve.wait_ge(weighed, TOPK * (t + 1))
                dve.tensor_tensor(acc[:, b], acc[:, b], m.gate2[:], ALU.mult).then_inc(gated, 1)
                dve.wait_ge(gated, t + 1)
                dve.tensor_tensor(acc[:, b], acc[:, b], x2[:, b], ALU.add).then_inc(x3, 1)
                dve.wait_ge(rstd, t + 1)
                if t >= 2:
                    dve.wait_ge(out_done[b], 16 * (t // 2))
                dve.scalar_tensor_tensor(out=res[:, b], in0=acc[:, b], scalar=nrm[:, t, 2:3], in1=gf[:], op0=ALU.mult, op1=ALU.mult).then_inc(done, 1)

        @block.scalar
        def _(act):
            for t in range(NT):
                b = t % 2
                act.wait_ge(x3, t + 1)
                act.activation(sq[:], acc[:, b], ACT.Square, accum_out=nrm[:, t, 0:1]).then_inc(sumsq, 1)
                act.wait_ge(sumsq, t + 1)
                act.activation(nrm[:, t, 1:2], nrm[:, t, 0:1], ACT.Ln, scale=1.0 / D, bias=m.eps[:, 0:1]).then_inc(logd, 1)
                act.wait_ge(logd, t + 1)
                act.activation(nrm[:, t, 2:3], nrm[:, t, 1:2], ACT.Exp, scale=-0.5).then_inc(rstd, 1)
                act.wait_ge(done, t + 1)
                act.dma_start(m.out[0, t * P:(t + 1) * P, :], res[:, b]).then_inc(out_done[b], 16)
            for b in range(2):
                act.wait_ge(out_done[b], 16 * (NT // 2))


def build(nc, x, c, w_ada, b_ada, norm1_g, w_in, lambda_q1, lambda_k1, lambda_q2, lambda_k2, diff_norm_g, w_alpha_up, b_alpha,
          gla_norm_g, w_branch_diff, w_branch_gla, w_out, norm2_g, w_router, b_router, w_gate_up, b_gate_up, w_down, b_down,
          final_norm_g, out):
    with ExitStack() as ctx:
        m = Memory()
        m.x, m.c_, m.w_ada, m.b_ada, m.norm1_g, m.w_in = x, c, w_ada, b_ada, norm1_g, w_in
        m.lambda_q1, m.lambda_k1, m.lambda_q2, m.lambda_k2 = lambda_q1, lambda_k1, lambda_q2, lambda_k2
        m.diff_norm_g, m.w_alpha_up, m.b_alpha, m.gla_norm_g = diff_norm_g, w_alpha_up, b_alpha, gla_norm_g
        m.w_branch_diff, m.w_branch_gla, m.w_out, m.norm2_g = w_branch_diff, w_branch_gla, w_out, norm2_g
        m.w_router, m.b_router, m.w_gate_up, m.b_gate_up = w_router, b_router, w_gate_up, b_gate_up
        m.w_down, m.b_down, m.final_g, m.out = w_down, b_down, final_norm_g, out

        def dram(name, shape, dt=F32):
            return nc.dram_tensor(name, shape, dt, kind="Internal").ap()

        m.by_token = dram("proj_by_token", [4, SEQ, N])
        m.qkT = dram("qk_transposed", [2, N, SEQ])
        m.gatesT = dram("gates_transposed", [4, N, SEQ])
        m.lrT = dram("low_rank_transposed", [RANK, SEQ])
        m.x2 = dram("residual", [SEQ, D])
        m.h2 = dram("ffn_input", [SEQ, D])
        m.lists = dram("expert_lists", [NE * LIST, 2], I32)
        m.y4 = dram("expert_rows", [SEQ * TOPK, D])

        PASSED[:] = [nc.alloc_semaphore("passed")]
        phase_sems = []

        def sem(name):
            phase_sems.append(nc.alloc_semaphore(name))
            return phase_sems[-1]

        def end_phase():
            nc.clear_and_free_semaphores(phase_sems)
            phase_sems.clear()
            nc.all_engine_barrier()

        m.sem = sem
        m.scoped = lambda c, name, shape, dt: c.enter_context(nc.sbuf_tensor(name, shape, dt))
        m.psum = lambda c, name, shape: c.enter_context(nc.psum_tensor(name, shape, F32))
        sb = lambda name, shape, dt: m.scoped(ctx, name, shape, dt)
        m.gate2 = sb("gate2", [P, D], F32)
        m.ident = sb("ident", [P, P], F32)
        m.eps = sb("eps", [P, 1], F32)
        m.cols = sb("norm_cols", [P, 2], F32)
        m.logits = sb("logits", [P, NT, NE], F32)
        m.wtop = sb("top_weights", [P, NT, TOPK], F32)
        m.wcT = sb("weights_transposed", [NE, NT, P], F32)
        m.table = sb("rounds", [1, MAX_ROUNDS + 2, 4], I32)
        m.rounds = sb("round_count", [1, 1], I32)

        vectors = ExitStack()
        m.mod = m.scoped(vectors, "mod", [P, 5 * D], F32)
        with ExitStack() as scope:
            m.hTH = m.scoped(scope, "hT_hi", [P, KT, SEQ], F32R)
            m.hTL = m.scoped(scope, "hT_lo", [P, KT, SEQ], F32R)
            phase_modulate(nc, m)
            end_phase()
            phase_project(nc, m)
            end_phase()
        with ExitStack() as merged:
            with ExitStack() as scope:
                m.oTH = scope.enter_context(nc.sbuf_tensor("oT_hi", [P, 2 * HEADS, SEQ], F32R, side="right"))
                m.oTL = scope.enter_context(nc.sbuf_tensor("oT_lo", [P, 2 * HEADS, SEQ], F32R, side="right"))
                phase_gla(nc, m)
                end_phase()
                phase_attention(nc, m)
                end_phase()
                m.mTH = m.scoped(merged, "mergedT_hi", [P, KT, SEQ], F32R)
                m.mTL = m.scoped(merged, "mergedT_lo", [P, KT, SEQ], F32R)
                phase_merge(nc, m)
                end_phase()
            phase_out(nc, m)
            end_phase()
        vectors.close()
        phase_route(nc, m)
        end_phase()
        phase_experts(nc, m)
        end_phase()
        phase_combine(nc, m)


_INS = ["x", "c", "w_ada", "b_ada", "norm1_g", "w_in", "lambda_q1", "lambda_k1", "lambda_q2", "lambda_k2", "diff_norm_g",
        "w_alpha_up", "b_alpha", "gla_norm_g", "w_branch_diff", "w_branch_gla", "w_out", "norm2_g", "w_router", "b_router",
        "w_gate_up", "b_gate_up", "w_down", "b_down", "final_norm_g"]


def kernel(**inputs):
    import numpy as _np
    import concourse.bacc as _bacc
    from concourse import mybir as _mybir
    from concourse.bass_utils import run_bass_kernel_spmd as _run

    nc = _bacc.Bacc("TRN2", target_bir_lowering=False, num_devices=1)
    arrays, args = {}, []
    for name in _INS:
        a = _np.ascontiguousarray(inputs[name])
        arrays[f"in_{name}_dram"] = a
        args.append(nc.dram_tensor(f"in_{name}_dram", a.shape, _mybir.dt.from_np(a.dtype), kind="ExternalInput").ap())
    args.append(nc.dram_tensor("out_0_dram", (1, SEQ, D), _mybir.dt.float32, kind="ExternalOutput").ap())
    build(nc, *args)
    r = _run(nc, [arrays], core_ids=[0])
    return r.results[0]["out_0_dram"]
```

```python
from contextlib import ExitStack

import concourse.bass as bass
from concourse import mybir

F32 = mybir.dt.float32
F32R = mybir.dt.float32r
I32 = mybir.dt.int32
U32 = mybir.dt.uint32
ALU = mybir.AluOpType
ACT = mybir.ActivationFunctionType
AX = mybir.AxisListType.X

P = 128
D = 1024
SEQ = 1024
KT = D // P
NT = SEQ // P
CHUNK = 64
HEADS = 4
DH = 64
DV = 128
RANK = 16
NE = 32
TOPK = 4
FF = 1024
EPS = 1e-6
LIMIT = 7.0
ALPHA = 1.702
LAMBDA_INIT = 0.2
MASKED = -1.0e30
N = 512

SLOTS = 2
GROUP = SLOTS * P
MAX_ROUNDS = SEQ * TOPK // GROUP + NE
LIST = SEQ
NO_ROW = 8191
CH = 4
FC = FF // CH
FIRST_K = 6


PASSED = []


def wait_apart(eng, sem, value):
    eng.wait_ge(sem, value)
    eng.sem_inc(PASSED[0], 1)


class Count:

    def __init__(self, eng, sem, base=0):
        self.eng, self.sem, self.base, self.n = eng, sem, base, 0

    def inc(self, ins):
        self.n += 1
        return ins.then_inc(self.sem, 1)

    def wait(self):
        self.eng.wait_ge(self.sem, self.base + self.n)

    def step(self, ins):
        self.inc(ins)
        self.wait()


class Memory:
    pass


def three(pe, out, a, w, first, last):
    pe.matmul(out, a[0], w[0], start=first, stop=False)
    pe.matmul(out, a[0], w[1], start=False, stop=False)
    return pe.matmul(out, a[1], w[0], start=False, stop=last)


def phase_modulate(nc, m):
    sem, sb = m.sem, m.scoped
    with ExitStack() as ctx:
        crow = sb(ctx, "crow", [P, KT], F32)
        csig = sb(ctx, "csig", [P, KT], F32)
        csil = sb(ctx, "csil", [P, KT], F32)
        wada = sb(ctx, "wada", [P, 4, 2 * D], F32)
        part = sb(ctx, "part", [P, 6 * D], F32)
        ones = sb(ctx, "ones_mod", [P, P], F32)
        g1 = sb(ctx, "g1", [P, D], F32)
        g2 = sb(ctx, "g2", [P, D], F32)
        xt = sb(ctx, "xt", [P, 2, D], F32)
        sq = sb(ctx, "sq0", [P, D], F32)
        ht = sb(ctx, "ht", [P, 2, D], F32)
        st = sb(ctx, "st0", [P, NT, 4], F32)
        pm = m.psum(ctx, "pm", [P, 2, N])
        pt = m.psum(ctx, "pt0", [P, 2, D])
        mod = m.mod

        small_in = sem("m_small_in")
        wada_in = [sem(f"m_wada_in{i}") for i in range(4)]
        x_in = [sem(f"m_x_in{i}") for i in range(2)]
        csig_done = sem("m_csig")
        part_done = sem("m_part")
        bcast_done = sem("m_bcast")
        mod_done = sem("m_mod")
        vec = sem("m_vec")
        sumsq_done = sem("m_sumsq")
        root_done = sem("m_root")
        x_used = sem("m_x_used")
        h_done = sem("m_h")
        turned = sem("m_turned")
        hi_done = sem("m_hi")
        lo_done = sem("m_lo")
        const_done = sem("m_const")

        block = ctx.enter_context(nc.Block())

        @block.sync
        def _(sp):
            sp.dma_start(crow[:], m.c_.rearrange("a (k p) -> p (a k)", p=P), allow_slow_non_contiguous=True).then_inc(small_in, 16)
            sp.dma_start(mod[:], m.b_ada[:, 0:5 * D].to_broadcast([P, 5 * D])).then_inc(small_in, 16)
            sp.dma_start(m.gate2[:], m.b_ada[:, 5 * D:6 * D].to_broadcast([P, D])).then_inc(small_in, 16)
            sp.dma_start(g1[:], m.norm1_g.to_broadcast([P, D])).then_inc(small_in, 16)
            sp.dma_start(g2[:], m.norm2_g.to_broadcast([P, D])).then_inc(small_in, 16)
            for j, g in enumerate((m.diff_norm_g, m.gla_norm_g)):
                sp.dma_start(m.cols[:, j:j + 1], g.rearrange("a p -> p a"), allow_slow_non_contiguous=True).then_inc(small_in, 16)
            for g in range(3):
                for k in range(KT):
                    i = g * KT + k
                    if i >= 4:
                        sp.wait_ge(part_done, i - 3)
                    sp.dma_start(wada[:, i % 4, :], m.w_ada[0, k * P:(k + 1) * P, g * 2 * D:(g + 1) * 2 * D]).then_inc(wada_in[i % 4], 16)

        @block.scalar
        def _(act):
            for t in range(2):
                act.dma_start(xt[:, t], m.x[0, t * P:(t + 1) * P, :]).then_inc(x_in[t], 16)
            act.wait_ge(small_in, 112)
            act.activation(csig[:], crow[:], ACT.Sigmoid).then_inc(csig_done, 1)
            act.wait_ge(const_done, 3)
            for t in range(NT):
                act.wait_ge(x_in[t % 2], 16 * (t // 2 + 1))
                if t:
                    act.wait_ge(sumsq_done, t)
                act.activation(sq[:], xt[:, t % 2], ACT.Square, accum_out=st[:, t, 0:1]).then_inc(sumsq_done, 1)
                act.wait_ge(sumsq_done, t + 1)
                act.activation(st[:, t, 1:2], st[:, t, 0:1], ACT.Sqrt, scale=1.0 / D, bias=m.eps[:, 0:1]).then_inc(root_done, 1)
                act.wait_ge(turned, t + 1)
                act.activation(m.hTH[:, :, t * P:(t + 1) * P], pt[:, t % 2].rearrange("p (k n) -> p k n", k=KT), ACT.Copy).then_inc(hi_done, 1)
                if t + 2 < NT:
                    act.wait_ge(x_used, t + 1)
                    act.dma_start(xt[:, t % 2], m.x[0, (t + 2) * P:(t + 3) * P, :]).then_inc(x_in[t % 2], 16)

        @block.gpsimd
        def _(pool):
            pool.memset(m.ident[:], 0.0).then_inc(const_done, 1)
            pool.wait_ge(const_done, 1)
            pool.affine_select(out=m.ident[:], in_=m.ident[:], compare_op=ALU.not_equal, fill=1.0, base=0,
                               pattern=[[-1, P]], channel_multiplier=1).then_inc(const_done, 1)
            pool.memset(m.eps[:], EPS).then_inc(const_done, 1)

        def low(t, dve):
            dve.wait_ge(hi_done, t + 1)
            cols = slice(t * P, (t + 1) * P)
            dve.tensor_tensor(m.hTL[:, :, cols], pt[:, t % 2].rearrange("p (k n) -> p k n", k=KT), m.hTH[:, :, cols].bitcast(F32), ALU.subtract).then_inc(lo_done, 1)

        @block.vector
        def _(dve):
            v = Count(dve, vec)
            v.step(dve.memset(ones[:], 1.0))
            dve.wait_ge(csig_done, 1)
            v.step(dve.tensor_tensor(csil[:], crow[:], csig[:], ALU.mult))
            v.step(dve.tensor_scalar(m.cols[:, 0:1], m.cols[:, 0:1], 1.0 - LAMBDA_INIT, None, ALU.mult))

            def modulate(t):
                h = ht[:, t % 2]
                dve.wait_ge(root_done, t + 1)
                v.step(dve.reciprocal(st[:, t, 2:3], st[:, t, 1:2]))
                if t >= 2:
                    dve.wait_ge(turned, t - 1)
                dve.scalar_tensor_tensor(out=h, in0=xt[:, t % 2], scalar=st[:, t, 2:3], in1=mod[:, D:2 * D], op0=ALU.mult, op1=ALU.mult).then_inc(x_used, 1)
                dve.wait_ge(x_used, t + 1)
                dve.tensor_tensor(h, h, mod[:, 0:D], ALU.add).then_inc(h_done, 1)
                if t >= 1:
                    low(t - 1, dve)

            for g in range(3):
                cols = part[:, g * 2 * D:(g + 1) * 2 * D]
                for k in range(KT):
                    i = g * KT + k
                    dve.wait_ge(wada_in[i % 4], 16 * (i // 4 + 1))
                    if k == 0:
                        ins = dve.tensor_scalar(cols, wada[:, i % 4], csil[:, k:k + 1], None, ALU.mult)
                    else:
                        dve.wait_ge(part_done, i)
                        ins = dve.scalar_tensor_tensor(out=cols, in0=wada[:, i % 4], scalar=csil[:, k:k + 1], in1=cols,
                                                       op0=ALU.mult, op1=ALU.add)
                    ins.then_inc(part_done, 1)
                    if g and k % 2:
                        modulate((g - 1) * NT // 2 + k // 2)
                for j in range(4):
                    n = g * 4 + j
                    dve.wait_ge(bcast_done, n + 1)
                    to = mod[:, n * N:(n + 1) * N] if n < 10 else m.gate2[:, (n - 10) * N:(n - 9) * N]
                    dve.tensor_tensor(to, pm[:, n % 2], to, ALU.add).then_inc(mod_done, 1)
                if g == 0:
                    dve.wait_ge(mod_done, 4)
                    v.step(dve.scalar_tensor_tensor(out=mod[:, D:2 * D], in0=mod[:, D:2 * D], scalar=1.0, in1=g1[:], op0=ALU.add, op1=ALU.mult))
            dve.wait_ge(mod_done, 12)
            v.step(dve.scalar_tensor_tensor(out=mod[:, 4 * D:5 * D], in0=mod[:, 4 * D:5 * D], scalar=1.0, in1=g2[:], op0=ALU.add, op1=ALU.mult))
            low(NT - 1, dve)

        @block.tensor
        def _(pe):

            def turn(t):
                pe.wait_ge(h_done, t + 1)
                if t >= 2:
                    pe.wait_ge(lo_done, t - 1)
                for k in range(KT):
                    ins = pe.transpose(pt[:, t % 2, k * P:(k + 1) * P], ht[:, t % 2, k * P:(k + 1) * P], m.ident[:])
                ins.then_inc(turned, 1)

            pe.wait_ge(vec, 1)
            pe.wait_ge(const_done, 2)
            for g in range(3):
                if g:
                    for t in range((g - 1) * NT // 2, g * NT // 2):
                        turn(t)
                pe.wait_ge(part_done, (g + 1) * KT)
                for j in range(4):
                    n = g * 4 + j
                    if n >= 2:
                        pe.wait_ge(mod_done, n - 1)
                    pe.matmul(pm[:, n % 2], ones[:], part[:, n * N:(n + 1) * N], start=True, stop=True).then_inc(bcast_done, 1)

UNITS = 8
CHUNKS = 10


def phase_project(nc, m):
    sem, sb = m.sem, m.scoped
    with ExitStack() as ctx:
        raw = sb(ctx, "win_raw", [P, 2, KT, N], F32)
        wH = sb(ctx, "win_hi", [P, 2, KT, N], F32R)
        wL = sb(ctx, "win_lo", [P, 2, KT, N], F32R)
        outb = sb(ctx, "out_stage", [P, 4, N], F32)
        ps = m.psum(ctx, "ps1", [P, 4, N])
        raw_in = [sem(f"p_raw_in{i}") for i in range(2)]
        hi = sem("p_hi")
        lo = sem("p_lo")
        unit = sem("p_unit")
        evac = sem("p_evac")
        stored = [sem(f"p_stored{i}") for i in range(4)]
        block = ctx.enter_context(nc.Block())

        groups = [(0, 4, True, False, 2 * N, m.by_token), (4, 2, False, False, 0, m.qkT),
                  (6, 4, False, True, 6 * N + RANK, m.gatesT)]
        columns = [c + i * N for _, count, _, _, c, _ in groups for i in range(count)] + [6 * N]

        def chunk_pairs(eng, body):
            for first, count, by_token, gated, _, dest in groups:
                if count > 2:
                    with eng.Fori(0, count // 2) as i:
                        for b in range(2):
                            body(first + 2 * i + b, b, by_token, gated, dest, 2 * i + b)
                else:
                    for b in range(2):
                        body(first + b, b, by_token, gated, dest, b)

        @block.gpsimd
        def _(pool):
            w = m.w_in[0].rearrange("(k p) n -> p k n", p=P)
            for q, col in enumerate(columns):
                if q >= 2:
                    pool.wait_ge(lo, (q - 1) * KT)
                pool.dma_start(raw[:, q % 2], w[:, :, col:col + N]).then_inc(raw_in[q % 2], 16)

        @block.sync
        def _(sp):
            for i in range(4):
                sp.sem_inc(stored[i], 16)

            def body(q, b, by_token, gated, dest, j):
                for x in range(UNITS):
                    sp.wait_ge(evac, q * UNITS + x + 5)
                    if by_token:
                        to = dest[bass.ds(j, 1), x * P:(x + 1) * P, :]
                    else:
                        to = dest[bass.ds(j, 1), (x // 2) * P:(x // 2 + 1) * P, (x % 2) * N:(x % 2 + 1) * N]
                    sp.dma_start(to.rearrange("a p n -> p (a n)"), outb[:, x % 4]).then_inc(stored[x % 4], 16)

            chunk_pairs(sp, body)
            for x in range(2):
                sp.wait_ge(evac, CHUNKS * UNITS + x + 5)
                sp.dma_start(m.lrT[:, x * N:(x + 1) * N], outb[0:RANK, x]).then_inc(stored[x], 16)
            for i in range(4):
                sp.wait_ge(stored[i], 16 * (2 * CHUNKS + 1 + (i < 2)))

        @block.scalar
        def _(act):
            def piece(q, b, k):
                act.wait_ge(raw_in[b], 8 * (q - b) + 16)
                act.activation(wH[:, b, k], raw[:, b, k], ACT.Copy).then_inc(hi, 1)

            for k in range(KT):
                piece(0, 0, k)

            def body(q, b, by_token, gated, dest, j):
                for x in range(UNITS):
                    if x == 0:
                        act.wait_ge(unit, (q + 1) * UNITS)
                    piece(q + 1, 1 - b, x)
                    act.wait_ge(unit, q * UNITS + x + 1 + UNITS)
                    act.wait_ge(stored[x % 4], q * 32 + x // 4 * 16 + 16)
                    act.activation(outb[:, x % 4], ps[:, x % 4], ACT.Sigmoid if gated else ACT.Copy).then_inc(evac, 1)

            chunk_pairs(act, body)
            for x in range(2):
                act.wait_ge(unit, CHUNKS * UNITS + x + 1 + UNITS)
                act.wait_ge(stored[x], CHUNKS * 32 + 16)
                act.activation(outb[:, x], ps[:, x], ACT.Copy).then_inc(evac, 1)

        @block.vector
        def _(dve):
            def piece(q, b, k):
                dve.wait_ge(hi, q * KT + k + 1)
                dve.tensor_tensor(wL[:, b, k], raw[:, b, k], wH[:, b, k].bitcast(F32), ALU.subtract).then_inc(lo, 1)

            for k in range(KT):
                piece(0, 0, k)

            def body(q, b, by_token, gated, dest, j):
                dve.wait_ge(unit, (q + 1) * UNITS)
                for x in range(UNITS):
                    piece(q + 1, 1 - b, x)

            chunk_pairs(dve, body)

        @block.tensor
        def _(pe):
            pe.sem_inc(unit, UNITS)
            pe.sem_inc(evac, 4)

            def tile_of(u, b, x, by_token):
                pe.wait_ge(evac, u + 1)
                for k in range(KT):
                    if by_token:
                        a = (m.hTH[:, k, x * P:(x + 1) * P], m.hTL[:, k, x * P:(x + 1) * P])
                        w = (wH[:, b, k], wL[:, b, k])
                    else:
                        mt, half = x // 2, x % 2
                        a = (wH[:, b, k, mt * P:(mt + 1) * P], wL[:, b, k, mt * P:(mt + 1) * P])
                        w = (m.hTH[:, k, half * N:(half + 1) * N], m.hTL[:, k, half * N:(half + 1) * N])
                    ins = three(pe, ps[:, x % 4], a, w, k == 0, k == KT - 1)
                ins.then_inc(unit, 1)

            def body(q, b, by_token, gated, dest, j):
                pe.wait_ge(lo, (q + 1) * KT)
                for x in range(UNITS):
                    tile_of(q * UNITS + x, b, x, by_token)

            chunk_pairs(pe, body)
            pe.wait_ge(lo, (CHUNKS + 1) * KT)
            for x in range(2):
                tile_of(CHUNKS * UNITS + x, 0, x, False)


def phase_gla(nc, m):
    sem, sb = m.sem, m.scoped
    with ExitStack() as ctx:
        qk = sb(ctx, "g_qk", [P, 2, 2, 256], F32)
        gv = sb(ctx, "g_v", [P, 2, HEADS, DV], F32)
        gr = sb(ctx, "g_r", [P, 2, N], F32)
        lr = sb(ctx, "g_lr", [RANK, 2, P], F32)
        wup = sb(ctx, "g_wup", [RANK, 256], F32)
        bal = sb(ctx, "g_bal", [P, 256], F32)
        upto = sb(ctx, "g_upto", [P, P], F32)
        past = sb(ctx, "g_past", [P, P], F32)
        whole = sb(ctx, "g_whole", [P, 2], F32)
        allowed = sb(ctx, "g_allowed", [P, 2, P], I32)
        allowf = sb(ctx, "g_allowf", [P, P], F32)
        zb = sb(ctx, "g_zb", [P, 2, 256], F32)
        la = sb(ctx, "g_la", [P, 256], F32)
        ex = sb(ctx, "g_ex", [P, 3, 256], F32)
        dec = sb(ctx, "g_dec", [P, 2, 4], F32)
        qs = sb(ctx, "g_qs", [P, 3, 256], F32)
        qsT = sb(ctx, "g_qsT", [P, 4, P], F32)
        att = sb(ctx, "g_att", [P, 2, 2, P], F32)
        er = sb(ctx, "g_er", [P, 2, N], F32)
        state = sb(ctx, "g_state", [P, 2, DV], F32)
        sq = sb(ctx, "g_sq", [P, DV], F32)
        nrm = sb(ctx, "g_nrm", [P, 3, 4], F32)
        on = sb(ctx, "g_on", [P, HEADS, DV], F32)
        pG = m.psum(ctx, "pG", [P, 2, 256])
        pz = m.psum(ctx, "pz", [P, N])
        pT = m.psum(ctx, "pT", [P, 4, P])
        pA = m.psum(ctx, "pA", [P, 2, 4, P])
        pO = m.psum(ctx, "pO", [P, 2, 4, P])
        pS = m.psum(ctx, "pS", [P, 4, P])

        once_in = sem("g_once_in")
        tile_in = [sem(f"g_tile_in{i}") for i in range(2)]
        v_in = [sem(f"g_v_in{i}") for i in range(2)]
        consts = sem("g_consts")
        z_done = sem("g_z")
        abs_done = sem("g_abs")
        soft_done = sem("g_soft")
        la_done = sem("g_la_done")
        sums_done = sem("g_sums")
        exp_done = sem("g_exp")
        er_done = sem("g_er_done")
        scaled_done = sem("g_scaled")
        turned = sem("g_turned")
        qsT_done = sem("g_qsT_done")
        scores = sem("g_scores")
        masked = sem("g_masked")
        delta = sem("g_delta")
        state_done = sem("g_state_done")
        out_done = sem("g_out")
        sumsq = sem("g_sumsq")
        rstd = sem("g_rstd")
        normed = sem("g_normed")
        turned_o = sem("g_turned_o")
        hi = sem("g_hi")
        lo = sem("g_lo")
        vec = sem("g_vec")
        exp_abs = sem("g_exp_abs")
        logd = sem("g_logd")
        block = ctx.enter_context(nc.Block())

        def tiles(eng, step):
            step(0, 0, None, None)
            with eng.Fori(0, NT // 2 - 1) as i:
                for b in range(2):
                    step(2 * i + b + 1, 1 - b, 2 * i + b, b)
            step(NT - 1, 1, NT - 2, 0)
            step(None, None, NT - 1, 1)

        @block.sync
        def _(sp):
            sp.dma_start(wup[:], m.w_alpha_up[0]).then_inc(once_in, 16)
            sp.dma_start(bal[:], m.b_alpha.to_broadcast([P, 256])).then_inc(once_in, 16)

            def load(t, b):
                rows = bass.ds(t * P, P)
                sp.dma_start(lr[:, b], m.lrT[:, rows]).then_inc(tile_in[b], 16)
                sp.dma_start(qk[:, b].rearrange("p a n -> p (a n)"), m.by_token[1, rows, :]).then_inc(tile_in[b], 16)
                sp.dma_start(gr[:, b], m.by_token[3, rows, :]).then_inc(tile_in[b], 16)

            def load_v(t, b):
                sp.dma_start(gv[:, b].rearrange("p h n -> p (h n)"), m.by_token[2, bass.ds(t * P, P), :]).then_inc(v_in[b], 16)

            for b in range(2):
                load(b, b)
                load_v(b, b)
            with sp.Fori(1, NT // 2) as i:
                for b in range(2):
                    t = 2 * i + b
                    sp.wait_ge(scaled_done, 3 * t - 2)
                    load(t, b)
                    sp.wait_ge(lo, t)
                    load_v(t, b)

        @block.gpsimd
        def _(pool):
            c = Count(pool, consts)
            c.step(pool.memset(upto[:], 1.0 / 16))
            c.step(pool.memset(past[:], 1.0 / 16))
            c.step(pool.memset(allowf[:], 1.0))
            for j in range(2):
                c.step(pool.memset(whole[:, j:j + 1], 1.0 / 16))
            for j in range(2):
                cols = slice(j * CHUNK, (j + 1) * CHUNK)
                for tile, w in ((upto[:, cols], CHUNK), (past[:, cols], CHUNK), (allowf[:, cols], CHUNK), (whole[:, j:j + 1], 1)):
                    c.step(pool.affine_select(out=tile, in_=tile, compare_op=ALU.is_ge, fill=0.0, base=-j * CHUNK,
                                              pattern=[[0, w]], channel_multiplier=1))
                    c.step(pool.affine_select(out=tile, in_=tile, compare_op=ALU.is_gt, fill=0.0, base=(j + 1) * CHUNK,
                                              pattern=[[0, w]], channel_multiplier=-1))
            c.step(pool.affine_select(out=upto[:], in_=upto[:], compare_op=ALU.is_ge, fill=0.0, base=0, pattern=[[1, P]], channel_multiplier=-1))
            c.step(pool.affine_select(out=allowf[:], in_=allowf[:], compare_op=ALU.is_ge, fill=0.0, base=0, pattern=[[1, P]], channel_multiplier=-1))
            c.step(pool.affine_select(out=past[:], in_=past[:], compare_op=ALU.is_gt, fill=0.0, base=0, pattern=[[-1, P]], channel_multiplier=1))
            for j in range(2):
                c.inc(pool.tensor_copy(allowed[:, j], allowf[:]))
            m.g_consts = c.n

        @block.tensor
        def _(pe):
            def decays(a, b):
                pe.wait_ge(tile_in[b], 24 * (a - b) + 48)
                pe.wait_ge(la_done, a + 1)
                pe.matmul(pz[:, 0:256], lr[:, b], wup[:], start=True, stop=True).then_inc(z_done, 1)

            def sums(a):
                pe.wait_ge(la_done, a + 2)
                pe.matmul(pG[:, 0], upto[:], la[:], start=True, stop=True)
                pe.matmul(pG[:, 1], past[:], la[:], start=True, stop=True)
                for h2 in range(2):
                    ins = pe.matmul(pz[:, 256 + 2 * h2:258 + 2 * h2], la[:, h2 * P:(h2 + 1) * P], whole[:], start=True, stop=True)
                ins.then_inc(sums_done, 1)

            def turn(a):
                pe.wait_ge(scaled_done, 3 * a + 4)
                for j in range(4):
                    ins = pe.transpose(pT[:, j], qs[:, j // 2, (j % 2) * P:(j % 2 + 1) * P], m.ident[:])
                ins.then_inc(turned, 1)

            def score(a):
                pe.wait_ge(qsT_done, a + 1)
                for h in range(HEADS):
                    r = slice((h % 2) * DH, (h % 2 + 1) * DH)
                    ins = pe.matmul(pA[:, h % 2, h // 2], qsT[r, 2 + h // 2], qsT[r, h // 2], start=True, stop=True)
                ins.then_inc(scores, 1)

            def within(t, b):
                pe.wait_ge(v_in[b], 8 * (t - b) + 16)
                pe.wait_ge(masked, 2 * t + 4)
                pe.wait_ge(lo, t + 1)
                for h in range(HEADS):
                    pe.matmul(pO[:, h % 2, h // 2], att[:, h % 2, h // 2], gv[:, b, h], start=(h < 2), stop=False, skip_group_check=True)

            def between(t, b, j):
                rows = slice(j * CHUNK, (j + 1) * CHUNK)
                wait_apart(pe, state_done, 2 * (2 * t + j) + 2)
                for h in range(HEADS):
                    r = slice((h % 2) * DH, (h % 2 + 1) * DH)
                    pe.matmul(pO[rows, h % 2, h // 2], qsT[r, h // 2, rows], state[r, h // 2], start=False, stop=(h >= 2), skip_group_check=True)
                for h in range(HEADS):
                    r = slice((h % 2) * DH, (h % 2 + 1) * DH)
                    ins = pe.matmul(pS[r, h // 2], qs[rows, 2, h * DH:(h + 1) * DH], gv[rows, b, h], start=True, stop=True)
                ins.then_inc(delta, 1)

            def turn_out(t):
                pe.wait_ge(normed, 4 * t + 9)
                for h in range(HEADS):
                    ins = pe.transpose(pO[:, 0, h], on[:, h], m.ident[:])
                ins.then_inc(turned_o, 1)

            def step(a, ab, t, tb):
                if a is not None:
                    decays(a, ab)
                if t is not None:
                    within(t, tb)
                    between(t, tb, 0)
                if a is not None:
                    sums(a)
                if t is not None:
                    between(t, tb, 1)
                if a is not None:
                    turn(a)
                if t is not None:
                    turn_out(t)
                if a is not None:
                    score(a)

            pe.sem_inc(lo, 1)
            pe.wait_ge(once_in, 32)
            pe.wait_ge(consts, m.g_consts)
            tiles(pe, step)

        @block.scalar
        def _(act):
            act.wait_ge(once_in, 32)

            def softplus(a):
                act.wait_ge(abs_done, a + 1)
                act.activation(zb[:, 1], zb[:, 1], ACT.Exp, scale=-1.0).then_inc(exp_abs, 1)
                act.wait_ge(exp_abs, a + 1)
                act.activation(zb[:, 1], zb[:, 1], ACT.Ln, bias=1.0).then_inc(soft_done, 1)

            def swish(a, b):
                act.wait_ge(tile_in[b], 24 * (a - b) + 48)
                act.wait_ge(normed, 4 * a + 1)
                act.activation(er[:, b], gr[:, b], ACT.Exp, scale=-1.0).then_inc(er_done, 1)

            def decay_exps(a, b):
                act.wait_ge(sums_done, a + 1)
                act.wait_ge(scaled_done, 3 * a + 1)
                act.activation(ex[:, 0], pG[:, 0], ACT.Exp)
                act.activation(ex[:, 1], pG[:, 0], ACT.Exp, scale=-1.0)
                act.activation(ex[:, 2], pG[:, 1], ACT.Exp)
                act.activation(dec[:, b], pz[:, 256:260], ACT.Exp).then_inc(exp_done, 1)

            def copy_turned(a):
                act.wait_ge(turned, a + 1)
                act.activation(qsT[:], pT[:], ACT.Copy).then_inc(qsT_done, 1)

            def roots(t):
                act.wait_ge(delta, 2 * t + 2)
                for h in range(HEADS):
                    if h:
                        act.wait_ge(sumsq, 4 * t + h)
                    act.activation(sq[:], pO[:, h % 2, h // 2], ACT.Square, accum_out=nrm[:, 0, h:h + 1]).then_inc(sumsq, 1)
                act.wait_ge(sumsq, 4 * t + 4)
                act.activation(nrm[:, 1], nrm[:, 0], ACT.Ln, scale=1.0 / DV, bias=m.eps[:, 0:1]).then_inc(logd, 1)
                act.wait_ge(logd, t + 1)
                act.activation(nrm[:, 2], nrm[:, 1], ACT.Exp, scale=-0.5).then_inc(rstd, 1)

            def high(t):
                act.wait_ge(turned_o, t + 1)
                act.activation(m.oTH[:, HEADS:2 * HEADS, bass.ds(t * P, P)], pO[:, 0], ACT.Copy, scale=m.cols[:, 1:2]).then_inc(hi, 1)

            def step(a, ab, t, tb):
                if a is not None:
                    softplus(a)
                    swish(a, ab)
                    decay_exps(a, ab)
                if t is not None:
                    roots(t)
                if a is not None:
                    copy_turned(a)
                if t is not None:
                    high(t)

            tiles(act, step)

        @block.vector
        def _(dve):
            v = Count(dve, vec)
            dve.wait_ge(once_in, 32)
            v.step(dve.memset(att[:], 0.0))
            dve.memset(state[:], 0.0).then_inc(state_done, 2)
            dve.sem_inc(la_done, 1)
            dve.sem_inc(masked, 2)
            dve.sem_inc(scaled_done, 1)
            dve.sem_inc(normed, 5)
            dve.wait_ge(consts, m.g_consts)
            start = v.n
            PER = 4

            def biased(a):
                v = Count(dve, vec, start + PER * a)
                dve.wait_ge(z_done, a + 1)
                v.step(dve.tensor_tensor(zb[:, 0], pz[:, 0:256], bal[:], ALU.add))
                dve.scalar_tensor_tensor(out=zb[:, 1], in0=zb[:, 0], scalar=-1.0, in1=zb[:, 0], op0=ALU.mult, op1=ALU.max).then_inc(abs_done, 1)

            def log_alpha(a):
                dve.wait_ge(soft_done, a + 1)
                dve.scalar_tensor_tensor(out=la[:], in0=zb[:, 0], scalar=0.0, in1=zb[:, 1], op0=ALU.min, op1=ALU.subtract).then_inc(la_done, 1)

            def swish(a, b):
                v = Count(dve, vec, start + PER * a + 1)
                dve.wait_ge(er_done, a + 1)
                v.step(dve.tensor_scalar(er[:, b], er[:, b], 1.0, None, ALU.add))
                v.step(dve.reciprocal(er[:, b], er[:, b]))
                v.step(dve.tensor_tensor(er[:, b], er[:, b], gr[:, b], ALU.mult))

            def scale(a, b):
                dve.wait_ge(exp_done, a + 1)
                dve.scalar_tensor_tensor(out=qs[:, 0], in0=qk[:, b, 0], scalar=DH ** -0.5, in1=ex[:, 0], op0=ALU.mult, op1=ALU.mult).then_inc(scaled_done, 1)
                for j in range(2):
                    dve.tensor_tensor(qs[:, 1 + j], qk[:, b, 1], ex[:, 1 + j], ALU.mult).then_inc(scaled_done, 1)

            def mask(a):
                wait_apart(dve, scores, a + 1)
                for j in range(2):
                    dve.copy_predicated(att[:, j], allowed[:], pA[:, j, 0:2]).then_inc(masked, 1)

            def update(t, b, j):
                dve.wait_ge(delta, 2 * t + j + 1)
                for h2 in range(2):
                    dve.scalar_tensor_tensor(out=state[:, h2], in0=state[:, h2], scalar=dec[:, b, 2 * h2 + j:2 * h2 + j + 1], in1=pS[:, h2],
                                             op0=ALU.mult, op1=ALU.add).then_inc(state_done, 1)

            def norm(t, b):
                dve.wait_ge(rstd, t + 1)
                for h in range(HEADS):
                    dve.scalar_tensor_tensor(out=on[:, h], in0=pO[:, h % 2, h // 2], scalar=nrm[:, 2, h:h + 1], in1=er[:, b, h * DV:(h + 1) * DV],
                                             op0=ALU.mult, op1=ALU.mult).then_inc(normed, 1)

            def low(t):
                dve.wait_ge(hi, t + 1)
                cols = bass.ds(t * P, P)
                dve.scalar_tensor_tensor(out=m.oTL[:, HEADS:2 * HEADS, cols], in0=pO[:, 0], scalar=m.cols[:, 1:2],
                                         in1=m.oTH[:, HEADS:2 * HEADS, cols].bitcast(F32), op0=ALU.mult, op1=ALU.subtract).then_inc(lo, 1)

            def step(a, ab, t, tb):
                if a is not None:
                    biased(a)
                if t is not None:
                    update(t, tb, 0)
                if a is not None:
                    log_alpha(a)
                    swish(a, ab)
                if t is not None:
                    update(t, tb, 1)
                if a is not None:
                    scale(a, ab)
                if t is not None:
                    norm(t, tb)
                if a is not None:
                    mask(a)
                if t is not None:
                    low(t)

            tiles(dve, step)


def phase_attention(nc, m):
    sem, sb = m.sem, m.scoped
    G = 4
    with ExitStack() as ctx:
        qT = sb(ctx, "a_qT", [P, 2, SEQ], F32)
        kT = sb(ctx, "a_kT", [P, 2, SEQ], F32)
        vh = sb(ctx, "a_v", [P, 2, NT, DV], F32)
        disti = sb(ctx, "a_disti", [P, SEQ], I32)
        dist = sb(ctx, "a_dist", [P, SEQ], F32)
        bias = sb(ctx, "a_bias", [P, 2, SEQ], F32)
        lam4 = sb(ctx, "a_lam4", [P, 4, DH], F32)
        lam = sb(ctx, "a_lam", [P, 8], F32)
        lamt = sb(ctx, "a_lamt", [P, DH], F32)
        pr = sb(ctx, "a_pr", [P, 2, 2, SEQ], F32)
        mx = sb(ctx, "a_mx", [P, 2, 2], F32)
        nb = sb(ctx, "a_nb", [P, 2, 2], F32)
        sm = sb(ctx, "a_sm", [P, 2, 2], F32)
        ri = sb(ctx, "a_ri", [P, 2, 2], F32)
        at = sb(ctx, "a_at", [P, SEQ], F32)
        aT = sb(ctx, "a_aT", [P, SEQ], F32)
        sq = sb(ctx, "a_sq", [P, DV], F32)
        kept = sb(ctx, "a_kept", [P, 2 * NT, DV], F32)
        nrm = sb(ctx, "a_nrm", [P, 3, 2 * NT], F32)
        on = sb(ctx, "a_on", [P, 2, G, DV], F32)
        pS = m.psum(ctx, "paS", [P, 2, SEQ])
        pT = m.psum(ctx, "paT", [P, SEQ])
        pO = m.psum(ctx, "paO", [P, 4, P])
        pQ = m.psum(ctx, "paQ", [P, 4, P])

        once_in = sem("a_once_in")
        head_in = [sem(f"a_head_in{i}") for i in range(2)]
        dist_done = sem("a_dist_done")
        bias_done = sem("a_bias_done")
        lam_done = sem("a_lam_done")
        lame_done = sem("a_lame")
        score = sem("a_score")
        biased = sem("a_biased")
        negmax = sem("a_negmax")
        exped = sem("a_exped")
        mixed = sem("a_mixed")
        vec = sem("a_vec")
        turned = sem("a_turned")
        aT_done = sem("a_aT_done")
        pv = sem("a_pv")
        kept_done = sem("a_kept_done")
        sumsq = sem("a_sumsq")
        logd = sem("a_logd")
        rstd = sem("a_rstd")
        normed = sem("a_normed")
        turned_o = sem("a_turned_o")
        hi = sem("a_hi")
        lo = sem("a_lo")
        block = ctx.enter_context(nc.Block())
        U = 2 * NT

        def head_pairs(eng, body):
            with eng.Fori(0, HEADS // 2) as i:
                body(i)

        @block.sync
        def _(sp):
            for j, w in enumerate((m.lambda_q1, m.lambda_k1, m.lambda_q2, m.lambda_k2)):
                sp.dma_start(lam4[:, j], w.to_broadcast([P, DH])).then_inc(once_in, 16)

            sp.sem_inc(pv, U)

            def body(i):
                for b in range(2):
                    sp.wait_ge(pv, U * i + (b + 1) * NT)
                    rows = bass.ds((2 * i + b) * P, P)
                    sp.dma_start(qT[:, b], m.qkT[0, rows, :]).then_inc(head_in[b], 16)
                    sp.dma_start(kT[:, b], m.qkT[1, rows, :]).then_inc(head_in[b], 16)
                    sp.dma_start(vh[:, b], m.by_token[0].rearrange("(t p) n -> p t n", p=P)[:, :, rows]).then_inc(head_in[b], 16)

            head_pairs(sp, body)

        @block.gpsimd
        def _(pool):
            pool.iota(disti[:], [[1, SEQ]], base=-(SEQ - P), channel_multiplier=-1).then_inc(dist_done, 1)
            pool.wait_ge(bias_done, 2)
            tail = bias[0:CHUNK, :, SEQ - CHUNK:SEQ]
            pool.memset(tail, MASKED).then_inc(bias_done, 1)

        def of(b, i):
            return b * NT + i

        @block.tensor
        def _(pe):
            def score_of(i0, b, i):
                u = of(b, i) + U * i0
                L = (i + 1) * P
                if i == 0:
                    pe.wait_ge(head_in[b], 48 * (i0 + 1))
                pe.wait_ge(biased, 2 * u + 2)
                for p in range(2):
                    r = slice(p * DH, (p + 1) * DH)
                    for c in range(0, L, N):
                        w = min(N, L - c)
                        ins = pe.matmul(pS[:, p, c:c + w], qT[r, b, i * P:(i + 1) * P], kT[r, b, c:c + w], start=True, stop=True)
                    ins.then_inc(score, 1)

            def turn_of(i0, b, i):
                u = of(b, i) + U * i0
                pe.wait_ge(mixed, u + 1)
                pe.wait_ge(aT_done, u + 1)
                for c in range(i + 1):
                    ins = pe.transpose(pT[:, c * P:(c + 1) * P], at[:, c * P:(c + 1) * P], m.ident[:])
                ins.then_inc(turned, 1)

            def value_of(i0, b, i):
                u = of(b, i) + U * i0
                pe.wait_ge(aT_done, u + 2)
                pe.wait_ge(kept_done, u + 1)
                for c in range(i + 1):
                    ins = pe.matmul(pO[:, 0], aT[:, c * P:(c + 1) * P], vh[:, b, c], start=(c == 0), stop=(c == i))
                ins.then_inc(pv, 1)

            def turn_out(i0, g):
                pe.wait_ge(normed, U // G * i0 + g + 1)
                pe.wait_ge(lo, U // G * i0 + g + 1)
                for j in range(G):
                    ins = pe.transpose(pQ[:, j], on[:, g % 2, j], m.ident[:])
                ins.then_inc(turned_o, 1)

            pe.sem_inc(biased, 2)
            pe.sem_inc(kept_done, 1)
            pe.sem_inc(lo, 1)

            def body(i0):
                seq = [(b, i) for b in range(2) for i in range(NT)]
                for n in range(U + 1):
                    if n < U:
                        score_of(i0, *seq[n])
                    if n >= 1:
                        turn_of(i0, *seq[n - 1])
                        value_of(i0, *seq[n - 1])
                for g in range(U // G):
                    turn_out(i0, g)

            head_pairs(pe, body)

        @block.vector
        def _(dve):
            v = Count(dve, vec)
            dve.wait_ge(dist_done, 1)
            v.step(dve.tensor_copy(dist[:], disti[:]))
            v.step(dve.scalar_tensor_tensor(out=dist[:], in0=dist[:], scalar=-1.0, in1=dist[:], op0=ALU.mult, op1=ALU.max))
            for h in range(2):
                slope = 2.0 ** (-8.0 * (h + 1) / HEADS)
                dve.tensor_scalar(bias[:, h], dist[:], -slope * DH ** 0.5, None, ALU.mult).then_inc(bias_done, 1)
            dve.wait_ge(once_in, 64)
            for j in range(2):
                v.step(dve.tensor_tensor(lamt[:], lam4[:, 2 * j], lam4[:, 2 * j + 1], ALU.mult))
                v.step(dve.reduce_sum(lam[:, j:j + 1], lamt[:], axis=AX))
            dve.sem_inc(lam_done, 1)
            dve.wait_ge(lame_done, 1)
            v.step(dve.tensor_tensor(lam[:, 4:5], lam[:, 3:4], lam[:, 2:3], ALU.subtract))
            v.step(dve.tensor_scalar(lam[:, 5:6], lam[:, 4:5], -LAMBDA_INIT, None, ALU.add))
            dve.wait_ge(bias_done, 3)
            start = v.n

            def body(i0):
                v = Count(dve, vec, start + PER * i0)

                def bias_of(b, i):
                    u = of(b, i) + U * i0
                    L = (i + 1) * P
                    s = i % 2
                    table = bias[:, b, SEQ - L:SEQ]
                    for p in range(2):
                        wait_apart(dve, score, 2 * u + p + 1)
                        dve.tensor_tensor_reduce(out=pr[:, s, p, 0:L], in0=pS[:, p, 0:L], in1=table, scale=1.0, scalar=-3.0e38,
                                                 op0=ALU.add, op1=ALU.max, accum_out=mx[:, s, p:p + 1]).then_inc(biased, 1)
                    dve.wait_ge(biased, 2 * u + 4)
                    dve.tensor_scalar(nb[:, s], mx[:, s], -DH ** -0.5, None, ALU.mult).then_inc(negmax, 1)

                def mix_of(b, i):
                    u = of(b, i) + U * i0
                    L = (i + 1) * P
                    s = i % 2
                    dve.wait_ge(exped, 2 * u + 2)
                    v.step(dve.reciprocal(ri[:, s], sm[:, s]))
                    v.step(dve.tensor_tensor(ri[:, s, 1:2], ri[:, s, 1:2], lam[:, 5:6], ALU.mult))
                    dve.wait_ge(turned, u + 1)
                    v.step(dve.tensor_scalar(at[:, 0:L], pr[:, s, 0, 0:L], ri[:, s, 0:1], None, ALU.mult))
                    dve.scalar_tensor_tensor(out=at[:, 0:L], in0=pr[:, s, 1, 0:L], scalar=ri[:, s, 1:2], in1=at[:, 0:L],
                                             op0=ALU.mult, op1=ALU.add).then_inc(mixed, 1)

                def keep(b, i):
                    u = of(b, i) + U * i0
                    dve.wait_ge(pv, u + U + 1)
                    dve.tensor_copy(kept[:, of(b, i)], pO[:, 0]).then_inc(kept_done, 1)

                def norm_of(g):
                    dve.wait_ge(rstd, i0 + 1)
                    dve.wait_ge(turned_o, U // G * i0 + g + 1)
                    units = slice(g * G, (g + 1) * G)
                    dve.tensor_tensor(on[:, g % 2], kept[:, units], nrm[:, 2, units].unsqueeze(2).to_broadcast([P, G, DV]), ALU.mult).then_inc(normed, 1)

                def low_of(g):
                    dve.wait_ge(hi, U // G * i0 + g + 1)
                    per = NT // G
                    at_ = (slice(None), bass.ds(2 * i0 + g // per, 1), slice(g % per * G * P, (g % per + 1) * G * P))
                    dve.scalar_tensor_tensor(out=m.oTL[at_].rearrange("p a n -> p (a n)"), in0=pQ[:].rearrange("p j n -> p (j n)"), scalar=m.cols[:, 0:1],
                                             in1=m.oTH[at_].bitcast(F32).rearrange("p a n -> p (a n)"), op0=ALU.mult, op1=ALU.subtract).then_inc(lo, 1)

                seq = [(b, i) for b in range(2) for i in range(NT)]
                for n in range(U + 1):
                    if n >= 1:
                        mix_of(*seq[n - 1])
                    if n >= 2:
                        keep(*seq[n - 2])
                    if n < U:
                        bias_of(*seq[n])
                keep(*seq[U - 1])
                for g in range(U // G + 1):
                    if g < U // G:
                        norm_of(g)
                    if g >= 1:
                        low_of(g - 1)
                v.step(dve.tensor_scalar(bias[:], bias[:], 2.0 ** (-16.0 / HEADS), None, ALU.mult))
                assert v.n == PER, v.n

            PER = 3 * U + 1
            head_pairs(dve, body)

        @block.scalar
        def _(act):
            act.wait_ge(lam_done, 1)
            act.activation(lam[:, 2:4], lam[:, 0:2], ACT.Exp).then_inc(lame_done, 1)
            act.sem_inc(aT_done, 1)
            act.sem_inc(turned, 1)
            act.sem_inc(turned_o, 2)

            def body(i0):
                def exp_of(b, i):
                    u = of(b, i) + U * i0
                    L = (i + 1) * P
                    s = i % 2
                    act.wait_ge(negmax, u + 1)
                    for p in range(2):
                        act.activation(pr[:, s, p, 0:L], pr[:, s, p, 0:L], ACT.Exp, bias=nb[:, s, p:p + 1], scale=DH ** -0.5,
                                       accum_out=sm[:, s, p:p + 1]).then_inc(exped, 1)

                def copy_of(b, i):
                    u = of(b, i) + U * i0
                    act.wait_ge(turned, u + 2)
                    act.wait_ge(pv, u + U)
                    act.activation(aT[:, 0:(i + 1) * P], pT[:, 0:(i + 1) * P], ACT.Copy).then_inc(aT_done, 1)

                def square_of(b, i):
                    u = of(b, i) + U * i0
                    act.wait_ge(kept_done, u + 2)
                    act.wait_ge(sumsq, u + 1)
                    act.activation(sq[:], kept[:, of(b, i)], ACT.Square, accum_out=nrm[:, 0, of(b, i):of(b, i) + 1]).then_inc(sumsq, 1)

                def high_of(g):
                    act.wait_ge(turned_o, U // G * i0 + g + 3)
                    per = NT // G
                    to = m.oTH[:, bass.ds(2 * i0 + g // per, 1), g % per * G * P:(g % per + 1) * G * P].rearrange("p a n -> p (a n)")
                    act.activation(to, pQ[:].rearrange("p j n -> p (j n)"), ACT.Copy, scale=m.cols[:, 0:1]).then_inc(hi, 1)

                seq = [(b, i) for b in range(2) for i in range(NT)]
                for n in range(U + 1):
                    if n >= 1:
                        copy_of(*seq[n - 1])
                    if n < U:
                        exp_of(*seq[n])
                    if n >= 2:
                        square_of(*seq[n - 2])
                square_of(*seq[U - 1])
                act.wait_ge(sumsq, U * i0 + U + 1)
                act.activation(nrm[:, 1], nrm[:, 0], ACT.Ln, scale=1.0 / DV, bias=m.eps[:, 0:1]).then_inc(logd, 1)
                act.wait_ge(logd, i0 + 1)
                act.activation(nrm[:, 2], nrm[:, 1], ACT.Exp, scale=-0.5).then_inc(rstd, 1)
                for g in range(U // G):
                    high_of(g)

            act.sem_inc(sumsq, 1)
            head_pairs(act, body)


def phase_merge(nc, m):
    sem, sb = m.sem, m.scoped
    with ExitStack() as ctx:
        raw = sb(ctx, "wb_raw", [P, 2, 2, HEADS, P], F32)
        wH = sb(ctx, "wb_hi", [P, 2, 2 * HEADS, P], F32R)
        wL = sb(ctx, "wb_lo", [P, 2, 2 * HEADS, P], F32R)
        gate = sb(ctx, "gate_in", [P, 2, 2, SEQ], F32)
        tmp = sb(ctx, "merge_tmp", [P, 2, N], F32)
        mg = sb(ctx, "merge_out", [P, 2, N], F32)
        ps = m.psum(ctx, "ps3", [P, 2, 2, N])
        raw_in = [sem(f"b_raw_in{i}") for i in range(2)]
        gate_in = [sem(f"b_gate_in{i}") for i in range(2)]
        whi = sem("b_whi")
        wlo = sem("b_wlo")
        unit = sem("b_unit")
        scaled = sem("b_scaled")
        summed = sem("b_summed")
        hi = sem("b_hi")
        lo = sem("b_lo")
        block = ctx.enter_context(nc.Block())

        def tiles(eng, body):
            with eng.Fori(0, KT // 2) as i:
                for b in range(2):
                    body(2 * i + b, b)

        def tiles_ahead(eng, weights, rest):
            weights(0, 0)
            with eng.Fori(0, KT // 2 - 1) as i:
                for b in range(2):
                    weights(2 * i + b + 1, 1 - b)
                    rest(2 * i + b, b)
            weights(KT - 1, 1)
            rest(KT - 2, 0)
            rest(KT - 1, 1)

        @block.sync
        def _(sp):
            sp.sem_inc(wlo, 2)
            sp.sem_inc(lo, 4)

            def body(q, b):
                sp.wait_ge(wlo, q + 1)
                cols = bass.ds(q * P, P)
                for j, w in enumerate((m.w_branch_diff, m.w_branch_gla)):
                    sp.dma_start(raw[:, b, j], w[0].rearrange("(k p) n -> p k n", p=P)[:, :, cols]).then_inc(raw_in[b], 16)
                sp.wait_ge(lo, 2 * q + 2)
                for j in range(2):
                    sp.dma_start(gate[:, b, j], m.gatesT.rearrange("(j a) r n -> j (a r) n", j=2)[j, cols, :]).then_inc(gate_in[b], 16)

            tiles(sp, body)

        @block.scalar
        def _(act):
            act.sem_inc(unit, 4)

            def weights(q, b):
                act.wait_ge(raw_in[b], 16 * (q - b) + 32)
                act.wait_ge(unit, 2 * q + 2)
                act.activation(wH[:, b].rearrange("p k n -> p (k n)"), raw[:, b].rearrange("p j k n -> p (j k n)"), ACT.Copy).then_inc(whi, 1)

            def rest(q, b):
                for half in range(2):
                    u = 2 * q + half
                    act.wait_ge(summed, u + 1)
                    act.activation(m.mTH[:, bass.ds(q, 1), half * N:(half + 1) * N].rearrange("p a n -> p (a n)"), mg[:, half], ACT.Copy).then_inc(hi, 1)

            tiles_ahead(act, weights, rest)

        @block.vector
        def _(dve):
            def weights(q, b):
                dve.wait_ge(whi, q + 1)
                dve.tensor_tensor(wL[:, b].rearrange("p k n -> p (k n)"), raw[:, b].rearrange("p j k n -> p (j k n)"),
                                  wH[:, b].bitcast(F32).rearrange("p k n -> p (k n)"), ALU.subtract).then_inc(wlo, 1)

            def rest(q, b):
                dve.wait_ge(gate_in[b], 16 * (q - b) + 32)
                for half in range(2):
                    u = 2 * q + half
                    cols = slice(half * N, (half + 1) * N)
                    dve.wait_ge(unit, u + 5)
                    for j in range(2):
                        dve.tensor_tensor(tmp[:, j], ps[:, half, j], gate[:, b, j, cols], ALU.mult).then_inc(scaled, 1)
                    dve.wait_ge(scaled, 2 * u + 6)
                    dve.tensor_tensor(mg[:, half], tmp[:, 0], tmp[:, 1], ALU.add).then_inc(summed, 1)
                    dve.wait_ge(hi, u + 1)
                    to = (slice(None), bass.ds(q, 1), cols)
                    dve.tensor_tensor(m.mTL[to].rearrange("p a n -> p (a n)"), mg[:, half], m.mTH[to].bitcast(F32).rearrange("p a n -> p (a n)"), ALU.subtract).then_inc(lo, 1)

            tiles_ahead(dve, weights, rest)

        @block.tensor
        def _(pe):
            pe.sem_inc(scaled, 4)

            def body(q, b):
                pe.wait_ge(wlo, q + 3)
                for half in range(2):
                    u = 2 * q + half
                    pe.wait_ge(scaled, 2 * u + 2)
                    cols = slice(half * N, (half + 1) * N)
                    for j in range(2):
                        for k in range(HEADS):
                            kk = j * HEADS + k
                            ins = three(pe, ps[:, half, j], (wH[:, b, kk], wL[:, b, kk]), (m.oTH[:, kk, cols], m.oTL[:, kk, cols]), k == 0, k == HEADS - 1)
                    ins.then_inc(unit, 1)

            tiles(pe, body)


def phase_out(nc, m):
    sem, sb = m.sem, m.scoped
    with ExitStack() as ctx:
        raw = sb(ctx, "wo_raw", [P, 4, D], F32)
        wH = sb(ctx, "wo_hi", [P, KT, D], F32R)
        wL = sb(ctx, "wo_lo", [P, KT, D], F32R)
        xt = sb(ctx, "o_x", [P, 2, D], F32)
        x2 = sb(ctx, "o_x2", [P, 2, D], F32)
        h2 = sb(ctx, "o_h2", [P, 2, D], F32)
        h2T = sb(ctx, "o_h2T", [P, D], F32)
        sq = sb(ctx, "o_sq", [P, D], F32)
        nrm = sb(ctx, "o_nrm", [P, NT, 4], F32)
        wr = sb(ctx, "o_wr", [P, KT, NE], F32)
        br = sb(ctx, "o_br", [P, NE], F32)
        ps = m.psum(ctx, "ps4", [P, 2, D])
        pT = m.psum(ctx, "pT4", [P, D])
        pL = m.psum(ctx, "pL4", [P, N])
        once_in = sem("o_once_in")
        raw_in = [sem(f"o_raw_in{i}") for i in range(4)]
        x_in = [sem(f"o_x_in{i}") for i in range(2)]
        whi = sem("o_whi")
        wlo = sem("o_wlo")
        unit = sem("o_unit")
        resid = sem("o_resid")
        added = sem("o_added")
        sumsq = sem("o_sumsq")
        logd = sem("o_logd")
        rstd = sem("o_rstd")
        norm = sem("o_norm")
        h2_done = sem("o_h2_done")
        turned = sem("o_turned")
        h2T_done = sem("o_h2T_done")
        logit = sem("o_logit")
        logit_out = sem("o_logit_out")
        stored = [sem(f"o_stored{i}") for i in range(2)]
        block = ctx.enter_context(nc.Block())

        @block.sync
        def _(sp):
            for k in range(KT):
                if k >= 4:
                    sp.wait_ge(wlo, k - 3)
                sp.dma_start(raw[:, k % 4], m.w_out[0, k * P:(k + 1) * P, :]).then_inc(raw_in[k % 4], 16)
            for k in range(2):
                sp.dma_start(xt[:, k], m.x[0, k * P:(k + 1) * P, :]).then_inc(x_in[k], 16)
            sp.dma_start(wr[:], m.w_router[0].rearrange("(k p) n -> p k n", p=P)).then_inc(once_in, 16)
            sp.dma_start(br[:], m.b_router.to_broadcast([P, NE])).then_inc(once_in, 16)
            for t in range(NT):
                rows = slice(t * P, (t + 1) * P)
                sp.wait_ge(added, t + 1)
                sp.dma_start(m.x2[rows, :], x2[:, t % 2]).then_inc(stored[t % 2], 16)
                if t + 2 < NT:
                    sp.dma_start(xt[:, t % 2], m.x[0, (t + 2) * P:(t + 3) * P, :]).then_inc(x_in[t % 2], 16)
                sp.wait_ge(h2_done, t + 1)
                sp.dma_start(m.h2[rows, :], h2[:, t % 2]).then_inc(stored[t % 2], 16)
            for b in range(2):
                sp.wait_ge(stored[b], 32 * (NT // 2))

        @block.scalar
        def _(act):
            for k in range(KT):
                act.wait_ge(raw_in[k % 4], 16 * (k // 4 + 1))
                act.activation(wH[:, k], raw[:, k % 4], ACT.Copy).then_inc(whi, 1)
            for t in range(NT):
                act.wait_ge(added, t + 1)
                act.activation(sq[:], x2[:, t % 2], ACT.Square, accum_out=nrm[:, t, 0:1]).then_inc(sumsq, 1)
                act.wait_ge(sumsq, t + 1)
                act.activation(nrm[:, t, 1:2], nrm[:, t, 0:1], ACT.Ln, scale=1.0 / D, bias=m.eps[:, 0:1]).then_inc(logd, 1)
                act.wait_ge(logd, t + 1)
                act.activation(nrm[:, t, 2:3], nrm[:, t, 1:2], ACT.Exp, scale=-0.5).then_inc(rstd, 1)
                act.wait_ge(turned, t + 1)
                if t:
                    act.wait_ge(logit, t)
                act.activation(h2T[:], pT[:], ACT.Copy).then_inc(h2T_done, 1)

        @block.vector
        def _(dve):
            for k in range(KT):
                dve.wait_ge(whi, k + 1)
                dve.tensor_tensor(wL[:, k], raw[:, k % 4], wH[:, k].bitcast(F32), ALU.subtract).then_inc(wlo, 1)
            dve.wait_ge(once_in, 32)
            for t in range(NT):
                b = t % 2
                dve.wait_ge(unit, t + 1)
                dve.wait_ge(x_in[b], 16 * (t // 2 + 1))
                if t >= 2:
                    dve.wait_ge(stored[b], 32 * (t // 2))
                dve.tensor_tensor(x2[:, b], ps[:, b], m.mod[:, 2 * D:3 * D], ALU.mult).then_inc(resid, 1)
                dve.wait_ge(resid, t + 1)
                dve.tensor_tensor(x2[:, b], x2[:, b], xt[:, b], ALU.add).then_inc(added, 1)
                dve.wait_ge(rstd, t + 1)
                dve.scalar_tensor_tensor(out=h2[:, b], in0=x2[:, b], scalar=nrm[:, t, 2:3], in1=m.mod[:, 4 * D:5 * D], op0=ALU.mult, op1=ALU.mult).then_inc(norm, 1)
                dve.wait_ge(norm, t + 1)
                dve.tensor_tensor(h2[:, b], h2[:, b], m.mod[:, 3 * D:4 * D], ALU.add).then_inc(h2_done, 1)
                dve.wait_ge(logit, t + 1)
                dve.tensor_tensor(m.logits[:, t], pL[:, 0:NE], br[:], ALU.add).then_inc(logit_out, 1)

        @block.tensor
        def _(pe):
            def product(t):
                if t >= 2:
                    pe.wait_ge(resid, t - 1)
                rows = slice(t * P, (t + 1) * P)
                for half in range(2):
                    cols = slice(half * N, (half + 1) * N)
                    for k in range(KT):
                        if t == 0 and half == 0:
                            pe.wait_ge(wlo, k + 1)
                        ins = three(pe, ps[:, t % 2, cols], (m.mTH[:, k, rows], m.mTL[:, k, rows]), (wH[:, k, cols], wL[:, k, cols]), k == 0, k == KT - 1)
                ins.then_inc(unit, 1)

            def route(t):
                pe.wait_ge(h2_done, t + 1)
                if t:
                    pe.wait_ge(h2T_done, t)
                    pe.wait_ge(logit_out, t)
                for k in range(KT):
                    ins = pe.transpose(pT[:, k * P:(k + 1) * P], h2[:, t % 2, k * P:(k + 1) * P], m.ident[:])
                ins.then_inc(turned, 1)
                pe.wait_ge(h2T_done, t + 1)
                if t == 0:
                    pe.wait_ge(once_in, 32)
                for k in range(KT):
                    ins = pe.matmul(pL[:, 0:NE], h2T[:, k * P:(k + 1) * P], wr[:, k], start=(k == 0), stop=(k == KT - 1))
                ins.then_inc(logit, 1)

            for t in range(NT + 1):
                if t < NT:
                    product(t)
                if t:
                    route(t - 1)


def phase_route(nc, m):
    sem, sb = m.sem, m.scoped
    ROWS = MAX_ROUNDS + 2
    with ExitStack() as ctx:
        top = sb(ctx, "r_top", [P, NT, 8], F32)
        idx = sb(ctx, "r_idx", [P, NT, 8], U32)
        idf = sb(ctx, "r_idf", [P, NT, 8], F32)
        sh = sb(ctx, "r_sh", [P, NT, TOPK], F32)
        tot = sb(ctx, "r_tot", [P, NT], F32)
        eidi = sb(ctx, "r_eidi", [P, NE], I32)
        eid = sb(ctx, "r_eid", [P, NE], F32)
        hot = sb(ctx, "r_hot", [P, TOPK, NT, NE], F32)
        mask = sb(ctx, "r_mask", [P, NT, NE], F32)
        before = sb(ctx, "r_before", [P, P], F32)
        ones = sb(ctx, "r_ones", [P, P], F32)
        rank = sb(ctx, "r_rank", [P, NT, NE], F32)
        tmp = sb(ctx, "r_tmp", [P, TOPK, NT, NE], F32)
        slot = sb(ctx, "r_slot", [P, TOPK, NT], F32)
        slotu = sb(ctx, "r_slotu", [P, TOPK, NT], U32)
        entry = sb(ctx, "r_entry", [P, TOPK, NT, 2], I32)
        pads = sb(ctx, "r_pads", [P, NE * LIST // P, 2], I32)
        cnt = sb(ctx, "r_cnt", [NE, 8], F32)
        cnti = sb(ctx, "r_cnti", [NE, 4], I32)
        rid = sb(ctx, "r_rid", [NE, ROWS], F32)
        ridi = sb(ctx, "r_ridi", [NE, ROWS], I32)
        pidi = sb(ctx, "r_pidi", [NE, 1], I32)
        pid = sb(ctx, "r_pid", [NE, 1], F32)
        rh = sb(ctx, "r_rh", [NE, 2, ROWS], F32)
        rv = sb(ctx, "r_rv", [NE, 4, ROWS], F32)
        row = sb(ctx, "r_row", [1, 4, ROWS], F32)
        row2 = sb(ctx, "r_row2", [1, 8, ROWS], F32)
        pr = m.psum(ctx, "pr5", [P, NT, NE])
        pc = m.psum(ctx, "pc5", [P, 4, P])
        pw = m.psum(ctx, "pw5", [P, N])
        ptab = m.psum(ctx, "pt5", [P, N])
        vec = sem("r_vec")
        pad_set = sem("r_pad_set")
        pool_set = sem("r_pool_set")
        cast = sem("r_cast")
        exped = sem("r_exped")
        shifted = sem("r_shifted")
        masked = sem("r_masked")
        ranked = sem("r_ranked")
        ranks_out = sem("r_ranks_out")
        counted = sem("r_counted")
        cum_in = sem("r_cum_in")
        cummed = sem("r_cummed")
        rows_in = sem("r_rows_in")
        rows_out = sem("r_rows_out")
        weighed = sem("r_weighed")
        wc_out = sem("r_wc_out")
        slots = sem("r_slots")
        ahead_in = sem("r_ahead_in")
        padded = sem("r_padded")
        listed = sem("r_listed")
        block = ctx.enter_context(nc.Block())

        @block.sync
        def _(sp):
            for c in range(2):
                for half in range(2):
                    load_gu(m, sp, 0, c, c, half, ahead_in)
                load_dn(m, sp, 0, c, c, ahead_in)
            load_bias(m, sp, 0, 0, 0, ahead_in)
            sp.wait_ge(ahead_in, 2 * (2 * 32 + 16) + 16)

        @block.gpsimd
        def _(pool):
            c = Count(pool, pool_set)
            c.step(pool.memset(pads[:, :, 0:1], 0))
            pool.memset(pads[:, :, 1:2], NO_ROW).then_inc(pad_set, 1)
            pool.wait_ge(pad_set, 1)
            pool.dma_start(m.lists.rearrange("(p n) c -> p n c", p=P), pads[:]).then_inc(padded, 16)
            c.step(pool.iota(eidi[:], [[1, NE]], base=0, channel_multiplier=0))
            c.step(pool.iota(ridi[:], [[1, ROWS]], base=0, channel_multiplier=0))
            c.step(pool.iota(pidi[:], [[0, 1]], base=0, channel_multiplier=1))
            c.step(pool.iota(entry[:, :, :, 0], [[0, TOPK], [P, NT]], base=0, channel_multiplier=1))
            c.step(pool.iota(entry[:, :, :, 1], [[1, TOPK], [P * TOPK, NT]], base=0, channel_multiplier=TOPK))
            c.step(pool.memset(ones[:], 1.0))
            c.step(pool.memset(before[:], 1.0))
            c.step(pool.affine_select(out=before[:], in_=before[:], compare_op=ALU.is_gt, fill=0.0, base=0, pattern=[[1, P]], channel_multiplier=-1))
            pool.wait_ge(slots, 1)
            pool.wait_ge(padded, 16)
            for k in range(TOPK):
                for t in range(NT):
                    pool.indirect_dma_start(out=m.lists[:, :], out_offset=bass.IndirectOffsetOnAxis(ap=slotu[:, k, t:t + 1], axis=0),
                                            in_=entry[:, k, t, :], in_offset=None).then_inc(listed, 16)
            pool.wait_ge(listed, 16 * TOPK * NT)

        @block.scalar
        def _(act):
            act.wait_ge(shifted, 1)
            act.activation(sh[:], sh[:], ACT.Exp).then_inc(exped, 1)

        @block.tensor
        def _(pe):
            pe.wait_ge(pool_set, 9)
            pe.wait_ge(masked, 1)
            for t in range(NT):
                for s in range(t):
                    pe.matmul(pr[:, t], ones[:], mask[:, s], start=(s == 0), stop=False)
                ins = pe.matmul(pr[:, t], before[:], mask[:, t], start=(t == 0), stop=True)
            ins.then_inc(ranked, 1)
            for t in range(NT):
                ins = pe.matmul(pc[0:NE, 0, 0:1], mask[:, t], ones[:, 0:1], start=(t == 0), stop=(t == NT - 1))
            ins.then_inc(counted, 1)
            pe.wait_ge(cum_in, 1)
            pe.matmul(pw[0:NE, 0:4], before[0:NE, 0:NE], cnt[:, 0:4], start=True, stop=True).then_inc(cummed, 1)
            pe.wait_ge(rows_in, 1)
            for j in range(4):
                ins = pe.matmul(ptab[0:1, j * ROWS:(j + 1) * ROWS], ones[0:NE, 0:1], rv[:, j], start=True, stop=True)
            pe.matmul(ptab[0:1, 4 * ROWS:4 * ROWS + 1], ones[0:NE, 0:1], cnt[:, 0:1], start=True, stop=True).then_inc(rows_out, 1)
            for t in range(NT):
                pe.wait_ge(weighed, t + 1)
                pe.transpose(pc[0:NE, 1], tmp[:, 0, t], m.ident[:]).then_inc(wc_out, 1)

        @block.vector
        def _(dve):
            v = Count(dve, vec)
            dve.wait_ge(pool_set, 9)
            v.step(dve.tensor_copy(eid[:], eidi[:]))
            v.step(dve.tensor_copy(rid[:], ridi[:]))
            v.step(dve.tensor_copy(pid[:], pidi[:]))
            for t in range(NT):
                v.step(dve.max(top[:, t], m.logits[:, t]))
                v.step(dve.max_index(idx[:, t], top[:, t], m.logits[:, t]))
            v.step(dve.tensor_copy(idf[:], idx[:]))
            for t in range(NT):
                ins = dve.tensor_scalar(sh[:, t], top[:, t, 0:TOPK], top[:, t, 0:1], None, ALU.subtract)
            ins.then_inc(shifted, 1)
            for k in range(TOPK):
                for t in range(NT):
                    v.inc(dve.tensor_scalar(hot[:, k, t], eid[:], idf[:, t, k:k + 1], None, ALU.is_equal))
            v.wait()
            v.step(dve.tensor_tensor(mask[:], hot[:, 0], hot[:, 1], ALU.add))
            v.step(dve.tensor_tensor(mask[:], mask[:], hot[:, 2], ALU.add))
            dve.tensor_tensor(mask[:], mask[:], hot[:, 3], ALU.add).then_inc(masked, 1)
            dve.wait_ge(exped, 1)
            v.step(dve.reduce_sum(tot[:], sh[:], axis=AX))
            v.step(dve.reciprocal(tot[:], tot[:]))
            for t in range(NT):
                v.inc(dve.tensor_scalar(m.wtop[:, t], sh[:, t], tot[:, t:t + 1], None, ALU.mult))
            dve.wait_ge(counted, 1)
            c = cnt
            v.step(dve.tensor_scalar(c[:, 4:5], pc[0:NE, 0, 0:1], 1.0, None, ALU.max))
            v.step(dve.tensor_scalar(c[:, 5:6], c[:, 4:5], GROUP / 2 - 0.5, 1.0 / GROUP, ALU.add, ALU.mult))
            v.step(dve.tensor_scalar(c[:, 6:7], c[:, 4:5], P / 2 - 0.5, 1.0 / P, ALU.add, ALU.mult))
            v.step(dve.tensor_copy(cnti[:, 0:2], c[:, 5:7]))
            v.step(dve.tensor_copy(c[:, 0:2], cnti[:, 0:2]))
            v.step(dve.tensor_copy(c[:, 2:4], cnti[:, 0:2]))
            dve.sem_inc(cum_in, 1)
            dve.wait_ge(cummed, 1)
            v.step(dve.tensor_copy(c[:, 4:6], pw[0:NE, 0:2]))
            v.step(dve.tensor_tensor(c[:, 6:7], c[:, 4:5], c[:, 0:1], ALU.add))
            v.step(dve.tensor_scalar(rh[:, 0], rid[:], c[:, 4:5], None, ALU.is_ge))
            v.step(dve.tensor_scalar(rh[:, 1], rid[:], c[:, 6:7], None, ALU.is_lt))
            v.step(dve.tensor_tensor(rh[:, 0], rh[:, 0], rh[:, 1], ALU.mult))
            v.step(dve.tensor_scalar(rh[:, 1], rid[:], c[:, 4:5], None, ALU.subtract))
            v.step(dve.tensor_scalar(rv[:, 0], rh[:, 0], pid[:, 0:1], None, ALU.mult))
            v.step(dve.tensor_tensor(rv[:, 1], rh[:, 0], rh[:, 1], ALU.mult))
            v.step(dve.tensor_scalar(rv[:, 2], rh[:, 0], c[:, 1:2], None, ALU.mult))
            v.step(dve.tensor_scalar(rv[:, 3], rh[:, 0], c[:, 5:6], None, ALU.mult))
            dve.sem_inc(rows_in, 1)
            dve.wait_ge(rows_out, 1)
            v.step(dve.tensor_copy(row[:].rearrange("p a n -> p (a n)"), ptab[0:1, 0:4 * ROWS]))
            v.step(dve.tensor_copy(row2[:, 0], row[:, 0]))
            v.step(dve.tensor_scalar(row2[:, 4], row[:, 1], float(GROUP), None, ALU.mult))
            v.step(dve.scalar_tensor_tensor(out=row2[:, 1], in0=row[:, 0], scalar=float(LIST), in1=row2[:, 4], op0=ALU.mult, op1=ALU.add))
            v.step(dve.scalar_tensor_tensor(out=row2[:, 5], in0=row[:, 1], scalar=-2.0, in1=row[:, 2], op0=ALU.mult, op1=ALU.add))
            v.step(dve.tensor_scalar(row2[:, 2], row2[:, 5], 2.0, None, ALU.is_ge))
            v.step(dve.scalar_tensor_tensor(out=row2[:, 6], in0=row[:, 1], scalar=2.0, in1=row[:, 3], op0=ALU.mult, op1=ALU.add))
            v.step(dve.tensor_scalar(row2[:, 3], row2[:, 6], 4.0, None, ALU.mult))
            for j in range(4):
                v.inc(dve.tensor_copy(m.table[:, :, j], row2[:, j]))
            v.step(dve.tensor_copy(m.rounds[:], ptab[0:1, 4 * ROWS:4 * ROWS + 1]))
            dve.wait_ge(ranked, 1)
            v.step(dve.tensor_copy(rank[:], pr[:]))
            for k in range(TOPK):
                v.inc(dve.tensor_tensor(tmp[:, k], hot[:, k], rank[:], ALU.mult))
            v.wait()
            for k in range(TOPK):
                v.inc(dve.reduce_sum(slot[:, k], tmp[:, k], axis=AX))
            v.wait()
            for k in range(TOPK):
                v.inc(dve.scalar_tensor_tensor(out=slot[:, k], in0=idf[:, :, k], scalar=float(LIST), in1=slot[:, k], op0=ALU.mult, op1=ALU.add))
            v.wait()
            dve.tensor_copy(slotu[:], slot[:]).then_inc(slots, 1)
            for t in range(NT):
                v.inc(dve.tensor_scalar(tmp[:, 0, t], hot[:, 0, t], m.wtop[:, t, 0:1], None, ALU.mult))
            v.wait()
            for k in range(1, TOPK):
                for t in range(NT):
                    ins = dve.scalar_tensor_tensor(out=tmp[:, 0, t], in0=hot[:, k, t], scalar=m.wtop[:, t, k:k + 1], in1=tmp[:, 0, t], op0=ALU.mult, op1=ALU.add)
                    v.inc(ins)
                v.wait()
            dve.sem_inc(weighed, 1)
            for t in range(NT):
                dve.wait_ge(wc_out, t + 1)
                dve.tensor_copy(m.wcT[:, t], pc[0:NE, 1]).then_inc(weighed, 1)


def load_gu(m, sp, e, c, b, half, done):
    w = m.w_gate_up[0].rearrange("e (k p) (g n) -> e p k g n", p=P, g=2)
    k = slice(half * (KT // 2), (half + 1) * (KT // 2))
    for g in range(2):
        src = w[bass.ds(e, 1), :, k, g, c * FC:(c + 1) * FC].rearrange("a p k n -> p (a k) n")
        sp.dma_start(m.gu_raw[:, b, k, g], src).then_inc(done, 16)


def load_dn(m, sp, e, c, b, done):
    w = m.w_down[0].rearrange("e (k p) n -> e p k n", p=P)
    kd = FC // P
    sp.dma_start(m.dn_raw[:, b], w[bass.ds(e, 1), :, c * kd:(c + 1) * kd, :].rearrange("a p k n -> p (a k) n")).then_inc(done, 16)


def load_bias(m, sp, e, c, b, done):
    w = m.b_gate_up[0].rearrange("e (g n) -> e g n", g=2)
    sp.dma_start(m.gu_bias[:, b], w[bass.ds(e, 1), :, c * FC:(c + 1) * FC].to_broadcast([P, 2, FC])).then_inc(done, 16)


def phase_experts(nc, m):
    sem, sb = m.sem, m.scoped
    KD = FC // P
    QG = 4
    with ExitStack() as ctx:
        gu_raw, dn_raw, bias = m.gu_raw, m.dn_raw, m.gu_bias
        gu_hi = sb(ctx, "e_gu_hi", [P, 2, KT, 2 * FC], F32R)
        gu_lo = sb(ctx, "e_gu_lo", [P, 2, KT, 2 * FC], F32R)
        dn_hi = sb(ctx, "e_dn_hi", [P, 2, KD, D], F32R)
        dn_lo = sb(ctx, "e_dn_lo", [P, 2, KD, D], F32R)
        rows = sb(ctx, "e_rows", [P, SLOTS, 2], I32)
        dest = sb(ctx, "e_dest", [P, 2, SLOTS], I32)
        xg = sb(ctx, "e_xg", [P, SLOTS, D], F32)
        xT = sb(ctx, "e_xT", [P, SLOTS, KT, P], F32)
        x_hi = sb(ctx, "e_x_hi", [P, SLOTS, KT, P], F32R)
        x_lo = sb(ctx, "e_x_lo", [P, SLOTS, KT, P], F32R)
        gb = sb(ctx, "e_gb", [P, 2, FC], F32)
        sg = sb(ctx, "e_sg", [P, FC], F32)
        av = sb(ctx, "e_act", [P, FC], F32)
        a_hi = sb(ctx, "e_a_hi", [P, KD, P], F32R)
        a_lo = sb(ctx, "e_a_lo", [P, KD, P], F32R)
        ys = sb(ctx, "e_y", [P, D], F32)
        warm = sb(ctx, "e_warm", [P, 1], F32)
        p_gu = m.psum(ctx, "e_pgu", [P, 2, 2, FC])
        p_dn = m.psum(ctx, "e_pdn", [P, SLOTS, D])
        p_at = m.psum(ctx, "e_pat", [P, N])
        p_xt = m.psum(ctx, "e_pxt", [P, N])

        gu_in = [[sem(f"e_gu_in{i}{half}") for half in range(2)] for i in range(2)]
        dn_in = [sem(f"e_dn_in{i}") for i in range(2)]
        bias_in = [sem(f"e_bias_in{i}") for i in range(2)]
        gu_hi_done = sem("e_gu_hi_done")
        gu_lo_done = sem("e_gu_lo_done")
        dn_hi_done = sem("e_dn_hi_done")
        dn_lo_done = sem("e_dn_lo_done")
        hidden = sem("e_hidden")
        x_half_used = sem("e_x_half_used")
        with_bias = sem("e_with_bias")
        clamped = sem("e_clamped")
        up_clamped = sem("e_up_clamped")
        sigm = sem("e_sigmoid")
        gated = sem("e_gated")
        activated = sem("e_activated")
        a_turned = sem("e_a_turned")
        a_hi_done = sem("e_a_hi_done")
        a_lo_done = sem("e_a_lo_done")
        dn_done = sem("e_dn_done")
        x_hi_done = sem("e_x_hi_done")
        x_lo_done = sem("e_x_lo_done")
        x1_hi_done = sem("e_x1_hi_done")
        x1_lo_done = sem("e_x1_lo_done")
        gathered = [sem(f"e_gathered{i}") for i in range(SLOTS)]
        x_turned = sem("e_x_turned")
        xT_done = sem("e_xT_done")
        rows_in = sem("e_rows_in")
        dest_kept = sem("e_dest_kept")
        y_out = sem("e_y_out")
        scattered = sem("e_scattered")
        block = ctx.enter_context(nc.Block())

        def entry(eng, r, j, top):
            return eng.value_load(m.table[0:1, bass.ds(r, 1), j:j + 1].rearrange("p a b -> p (a b)"), min_val=0, max_val=top)

        def expert_of(eng, r):
            return entry(eng, r, 0, NE - 1)

        def rounds(eng, body):
            n = eng.value_load(m.rounds[0:1, 0:1], min_val=1, max_val=MAX_ROUNDS)
            with eng.Fori(0, n) as r:
                U = eng.snap(entry(eng, r, 3, 4 * (MAX_ROUNDS * SLOTS)))
                two = entry(eng, r, 2, 1)
                with eng.If(two > 0):
                    body(r, U, True)
                with eng.Else():
                    body(r, U, False)
            return eng.snap(entry(eng, n - 1, 3, 4 * (MAX_ROUNDS * SLOTS)) + 4 + 4 * entry(eng, n - 1, 2, 1)), n

        def units(two):
            slots = (1, 0) if two else (0,)
            seq = [(c, s) for c in range(CH) for s in slots]
            for l, (c, s) in enumerate(seq):
                yield l, c, s, s == 0, seq[l - 1]

        def after_first(eng, r, l, body):
            if l == 0:
                with eng.If(r > 0):
                    body()
            else:
                body()

        @block.sync
        def _(sp):
            def gu(e, c, b, half):
                load_gu(m, sp, e, c, b, half, gu_in[b][half])

            def dn(e, c, b):
                load_dn(m, sp, e, c, b, dn_in[b])

            def bs(e, c, b):
                load_bias(m, sp, e, c, b, bias_in[b])

            for b in range(2):
                for half in range(2):
                    sp.sem_inc(gu_in[b][half], 32)
                sp.sem_inc(dn_in[b], 16)
            sp.sem_inc(bias_in[0], 16)
            for half in range(2):
                wait_apart(sp, gu_lo_done, (half + 1) * QG // 2)
                gu(0, 2, 0, half)

            def body(r, U, two):
                here, there = expert_of(sp, r), expert_of(sp, r + 1)
                q4 = sp.snap(4 * r)
                for c in range(CH):
                    wait_apart(sp, with_bias, U + c * (1 + two) + 2)
                    bs(here if c < 3 else there, (c + 1) % CH, (c + 1) % 2)
                    for half in range(2):
                        wait_apart(sp, gu_lo_done, QG * q4 + QG * (c + 1) + (half + 1) * QG // 2)
                        gu(here if c == 0 else there, (c + 3) % CH, (c + 1) % 2, half)
                    wait_apart(sp, dn_lo_done, KD * q4 + KD * (c + 1))
                    dn(here if c < 2 else there, (c + 2) % CH, c % 2)

            rounds(sp, body)
            n = sp.value_load(m.rounds[0:1, 0:1], min_val=1, max_val=MAX_ROUNDS)
            for half in range(2):
                wait_apart(sp, gu_in[0][half], 64 * n + 64)
                wait_apart(sp, gu_in[1][half], 64 * n + 32)
            for b in range(2):
                wait_apart(sp, dn_in[b], 32 * n + 16)
            wait_apart(sp, bias_in[0], 32 * n + 16)
            wait_apart(sp, bias_in[1], 32 * n)

        @block.gpsimd
        def _(pool):
            def fetch(r):
                at = entry(pool, r, 1, NE * LIST - GROUP)
                pool.dma_start(rows[:], m.lists[bass.ds(at, GROUP), :].rearrange("(s p) c -> p s c", p=P)).then_inc(rows_in, 16)

            def gather(s):
                pool.indirect_dma_start(out=xg[:, s], out_offset=None, in_=m.h2[:, :],
                                        in_offset=bass.IndirectOffsetOnAxis(ap=rows[:, s, 0:1].bitcast(U32), axis=0)).then_inc(gathered[s], 16)

            def scatter(s, blocks):
                wait_apart(pool, y_out, blocks + 2)
                pool.indirect_dma_start(out=m.y4[:, :], out_offset=bass.IndirectOffsetOnAxis(ap=dest[:, 0, s:s + 1].bitcast(U32), axis=0),
                                        in_=ys[:], in_offset=None, bounds_check=SEQ * TOPK - 1, oob_is_err=False).then_inc(scattered, 16)

            pool.dma_start(rows[:], m.lists[0:GROUP, :].rearrange("(s p) c -> p s c", p=P)).then_inc(scattered, 16)
            wait_apart(pool, scattered, 16)
            fetch(0)
            wait_apart(pool, rows_in, 16)
            gather(1)
            gather(0)
            for s in range(SLOTS):
                wait_apart(pool, gathered[s], 16)
            pool.tensor_copy(dest[:, 1], rows[:, :, 1]).then_inc(dest_kept, 1)
            wait_apart(pool, dest_kept, 1)
            fetch(1)

            def body(r, U, two):
                B = pool.snap(U // 4)
                wait_apart(pool, rows_in, 16 * r + 32)
                wait_apart(pool, x_turned, 4 * r + 4)
                gather(1)
                gather(0)
                with pool.If(r > 0):
                    scatter(0, B)
                    wait_apart(pool, scattered, 16 * B + 16)
                pool.tensor_copy(dest[:, 0], dest[:, 1]).then_inc(dest_kept, 1)
                for s in range(SLOTS):
                    wait_apart(pool, gathered[s], 16 * r + 32)
                wait_apart(pool, dest_kept, 2 * r + 2)
                pool.tensor_copy(dest[:, 1], rows[:, :, 1]).then_inc(dest_kept, 1)
                wait_apart(pool, dest_kept, 2 * r + 3)
                fetch(r + 2)
                if two:
                    scatter(1, B + 1)

            total, n = rounds(pool, body)
            B = pool.snap(total // 4)
            scatter(0, B)
            wait_apart(pool, scattered, 16 * B + 16)
            for s in range(SLOTS):
                wait_apart(pool, gathered[s], 16 * n + 16)
            wait_apart(pool, rows_in, 16 * n + 32)

        @block.tensor
        def _(pe):
            pe.sem_inc(hidden, 2)
            pe.sem_inc(x_half_used, 1)
            pe.sem_inc(dn_done, 2)
            pe.sem_inc(y_out, 2)

            def turn_x(r, i):
                count = 4 * r + i
                if i % 2 == 0:
                    pe.wait_ge(gathered[1 - i // 2], 16 * r + 16)
                pe.wait_ge(xT_done, count + 1)
                for k in range(4):
                    kk = 4 * (i % 2) + k
                    ins = pe.transpose(p_xt[:, k * P:(k + 1) * P], xg[:, 1 - i // 2, kk * P:(kk + 1) * P], m.ident[:])
                ins.then_inc(x_turned, 1)

            def turn_a(n):
                pe.wait_ge(activated, n + 1)
                pe.wait_ge(a_lo_done, n + 1)
                for k in range(KD):
                    ins = pe.transpose(p_at[:, k * P:(k + 1) * P], av[:, k * P:(k + 1) * P], m.ident[:])
                ins.then_inc(a_turned, 1)

            def down(n, q, blocks, c, s):
                pe.wait_ge(a_lo_done, n + 2)
                pe.wait_ge(dn_lo_done, KD * q + KD)
                if c == 0:
                    pe.wait_ge(y_out, blocks)
                for half in range(2):
                    cols = slice(half * N, (half + 1) * N)
                    for k in range(KD):
                        ins = three(pe, p_dn[:, s, cols], (a_hi[:, k], a_lo[:, k]), (dn_hi[:, c % 2, k, cols], dn_lo[:, c % 2, k, cols]),
                                    c == 0 and k == 0, c == CH - 1 and k == KD - 1)
                ins.then_inc(dn_done, 1)

            for i in range(4):
                turn_x(0, i)

            def body(r, U, two):
                B = pe.snap(U // 4)
                q4 = pe.snap(4 * r)
                for l, c, s, last, (pc, ps) in units(two):
                    n = U + l
                    pe.wait_ge(with_bias, n + 1)
                    if c == 0 and s == 1:
                        pe.wait_ge(x1_lo_done, r + 1)
                    for k in range(KT):
                        if c == 0 and s == 0 and k % (KT // 2) == 0:
                            pe.wait_ge(x_lo_done, 2 * r + 2 * k // KT + 1)
                        if k == (FIRST_K if l else 3):
                            after_first(pe, r, l, lambda: turn_a(n - 1))
                        if k == FIRST_K and s == 0 and c >= 2:
                            turn_x(r + 1, 2 * c - 3)
                        if (s == 1 or not two) and k % 2 == 0:
                            pe.wait_ge(gu_lo_done, QG * q4 + QG * c + k // 2 + 1)
                        ins = three(pe, p_gu[:, l % 2].rearrange("p g n -> p (g n)"), (x_hi[:, s, k], x_lo[:, s, k]),
                                    (gu_hi[:, c % 2, k], gu_lo[:, c % 2, k]), k == 0, k == KT - 1)
                        if c == CH - 1 and last and k == KT // 2 - 1:
                            ins.then_inc(x_half_used, 1)
                    ins.then_inc(hidden, 1)
                    after_first(pe, r, l, lambda: down(n - 1, q4 + (pc if l else -1), B + 2, pc, ps))
                    if s == 0 and c in (1, 2):
                        turn_x(r + 1, 2 * c - 2)

            total, n = rounds(pe, body)
            turn_a(total - 1)
            down(total - 1, 4 * n - 1, 0, CH - 1, 0)

        @block.scalar
        def _(act):
            def gu_piece(r, c, j):
                b = c % 2
                if j % 2 == 0:
                    act.wait_ge(gu_in[b][j // 2], 64 * r + 32 * (c // 2) + 32)
                act.activation(gu_hi[:, b, 2 * j:2 * j + 2], gu_raw[:, b, 2 * j:2 * j + 2].rearrange("p k g n -> p k (g n)"), ACT.Copy).then_inc(gu_hi_done, 1)

            def dn_piece(r, c, j):
                b = c % 2
                if j == 0:
                    act.wait_ge(dn_in[b], 32 * r + 16 * (c // 2) + 16)
                act.activation(dn_hi[:, b, j], dn_raw[:, b, j], ACT.Copy).then_inc(dn_hi_done, 1)

            def stage_x(r, i):
                count = 4 * r + i
                act.wait_ge(x_turned, count + 1)
                act.activation(xT[:, 1 - i // 2, 4 * (i % 2):4 * (i % 2) + 4].rearrange("p k n -> p (k n)"), p_xt[:], ACT.Copy).then_inc(xT_done, 1)

            def sigmoid(n):
                act.wait_ge(clamped, n + 1)
                act.activation(sg[:], gb[:, 0], ACT.Sigmoid, scale=ALPHA).then_inc(sigm, 1)

            def high_x(r, half):
                act.wait_ge(xT_done, 4 * r + 4 + half)
                k = slice(half * (KT // 2), (half + 1) * (KT // 2))
                act.activation(x_hi[:, 0, k], xT[:, 0, k], ACT.Copy).then_inc(x_hi_done, 1)

            def high_x1(r):
                act.wait_ge(xT_done, 4 * r + 3)
                act.activation(x_hi[:, 1], xT[:, 1], ACT.Copy).then_inc(x1_hi_done, 1)

            def high_a(n):
                act.wait_ge(a_turned, n + 1)
                act.wait_ge(dn_done, n + 2)
                act.activation(a_hi[:].rearrange("p k n -> p (k n)"), p_at[:, 0:FC], ACT.Copy).then_inc(a_hi_done, 1)

            def evacuate(n, s, blocks):
                act.wait_ge(dn_done, n + 3)
                act.wait_ge(scattered, 16 * blocks + 16)
                act.activation(ys[:], p_dn[:, s], ACT.Copy).then_inc(y_out, 1)

            act.sem_inc(xT_done, 1)
            for j in range(QG):
                gu_piece(0, 0, j)
            for i in range(4):
                stage_x(0, i)
            high_x1(0)
            high_x(0, 0)
            high_x(0, 1)

            def body(r, U, two):
                B = act.snap(U // 4)
                act.activation(warm[:], m.eps[:], ACT.Sigmoid)
                for l, c, s, last, (pc, ps) in units(two):
                    n = U + l
                    nc_, nr = ((c + 1) % CH, r + (c == CH - 1))
                    if not two:
                        todo = [("g", 0), ("g", 1), ("g", 2), ("g", 3), ("d", 0), ("d", 1)]
                    elif s == 1:
                        todo = [("g", 0), ("d", 0), ("d", 1)]
                    else:
                        todo = [("g", 1), ("g", 2), ("g", 3)]
                    if s == 1 or not two:
                        act.wait_ge(hidden, n + 2)

                    def piece():
                        if todo:
                            kind, j = todo.pop(0)
                            if kind == "d":
                                if j == 0:
                                    act.wait_ge(dn_done, n + 1)
                                dn_piece(r, c, j)
                            else:
                                gu_piece(nr, nc_, j)

                    piece()
                    if l:
                        sigmoid(n - 1)
                        piece()
                        piece()
                    after_first(act, r, l, lambda: high_a(n - 1))
                    if s == 0 and c >= 2:
                        stage_x(r + 1, 2 * c - 3)
                    if (c, s) == ((CH - 1, 0) if two else (CH - 2, 0)):
                        high_x1(r + 1)
                    if (c, s) == (CH - 1, 0):
                        act.wait_ge(x_half_used, r + 2)
                        high_x(r + 1, 0)
                        piece()
                        act.wait_ge(hidden, n + 3)
                        high_x(r + 1, 1)
                        sigmoid(n)
                    if l == 1:
                        after_first(act, r, 0, lambda: evacuate(n - 2, 0, B - 1))
                    while todo:
                        piece()
                    if s == 0 and c in (1, 2):
                        if c == 1:
                            act.wait_ge(x1_lo_done, r + 1)
                        stage_x(r + 1, 2 * c - 2)
                if two:
                    evacuate(n - 1, 1, B)

            total, n = rounds(act, body)
            high_a(total - 1)
            evacuate(total - 1, 0, act.snap(total // 4) - 1)

        @block.vector
        def _(dve):
            def gu_piece(count, c, j):
                b = c % 2
                dve.wait_ge(gu_hi_done, count + 1)
                dve.tensor_tensor(gu_lo[:, b, 2 * j:2 * j + 2], gu_raw[:, b, 2 * j:2 * j + 2].rearrange("p k g n -> p k (g n)"),
                                  gu_hi[:, b, 2 * j:2 * j + 2].bitcast(F32), ALU.subtract).then_inc(gu_lo_done, 1)

            def dn_piece(count, c, j):
                b = c % 2
                dve.wait_ge(dn_hi_done, count + 1)
                dve.tensor_tensor(dn_lo[:, b, j], dn_raw[:, b, j], dn_hi[:, b, j].bitcast(F32), ALU.subtract).then_inc(dn_lo_done, 1)

            def with_biases(n, c, parity, in_count):
                dve.wait_ge(hidden, n + 3)
                dve.wait_ge(bias_in[c % 2], in_count)
                dve.tensor_tensor(gb[:], p_gu[:, parity], bias[:, c % 2], ALU.add).then_inc(with_bias, 1)
                dve.wait_ge(with_bias, n + 3)
                dve.tensor_scalar(gb[:, 0], gb[:, 0], LIMIT, None, ALU.min).then_inc(clamped, 1)
                dve.tensor_scalar(gb[:, 1], gb[:, 1], -LIMIT, LIMIT, ALU.max, ALU.min).then_inc(up_clamped, 1)

            def activate(n):
                dve.wait_ge(sigm, n + 1)
                dve.tensor_tensor(sg[:], gb[:, 0], sg[:], ALU.mult).then_inc(gated, 1)
                dve.wait_ge(gated, n + 1)
                dve.wait_ge(up_clamped, n + 1)
                dve.scalar_tensor_tensor(out=av[:], in0=gb[:, 1], scalar=1.0, in1=sg[:], op0=ALU.add, op1=ALU.mult).then_inc(activated, 1)

            def low_x1(r):
                dve.wait_ge(x1_hi_done, r + 1)
                dve.tensor_tensor(x_lo[:, 1], xT[:, 1], x_hi[:, 1].bitcast(F32), ALU.subtract).then_inc(x1_lo_done, 1)

            def low_x(r, half):
                k = slice(half * (KT // 2), (half + 1) * (KT // 2))
                dve.wait_ge(x_hi_done, 2 * r + half + 1)
                dve.tensor_tensor(x_lo[:, 0, k], xT[:, 0, k], x_hi[:, 0, k].bitcast(F32), ALU.subtract).then_inc(x_lo_done, 1)

            def low_a(n):
                dve.wait_ge(a_hi_done, n + 1)
                dve.tensor_tensor(a_lo[:].rearrange("p k n -> p (k n)"), p_at[:, 0:FC], a_hi[:].rearrange("p k n -> p (k n)").bitcast(F32),
                                  ALU.subtract).then_inc(a_lo_done, 1)

            dve.sem_inc(with_bias, 2)
            dve.sem_inc(a_lo_done, 1)
            for j in range(QG):
                gu_piece(j, 0, j)
            low_x1(0)
            low_x(0, 0)
            low_x(0, 1)

            def body(r, U, two):
                for l, c, s, last, (pc, ps) in units(two):
                    n = U + l
                    if not two:
                        todo = [("g", 0), ("g", 1), ("g", 2), ("g", 3), ("d", 0), ("d", 1)]
                    elif s == 1:
                        todo = [("g", 0), ("d", 0), ("d", 1)]
                    else:
                        todo = [("g", 1), ("g", 2), ("g", 3)]

                    def piece():
                        if todo:
                            kind, j = todo.pop(0)
                            if kind == "d":
                                dn_piece(8 * r + KD * c + j, c, j)
                            else:
                                gu_piece(16 * r + QG * (c + 1) + j, c + 1, j)

                    if l:
                        with_biases(n - 1, pc, (l - 1) % 2, 32 * r + 16 * (pc // 2) + 16)
                    piece()
                    if l:
                        activate(n - 1)
                        piece()
                    after_first(dve, r, l, lambda: low_a(n - 1))
                    if (c, s) == ((CH - 1, 0) if two else (CH - 2, 0)):
                        low_x1(r + 1)
                    if (c, s) == (CH - 1, 0):
                        low_x(r + 1, 0)
                        with_biases(n, c, l % 2, 32 * r + 32)
                        low_x(r + 1, 1)
                        activate(n)
                    while todo:
                        piece()

            total, n = rounds(dve, body)
            low_a(total - 1)


def phase_combine(nc, m):
    sem, sb = m.sem, m.scoped
    with ExitStack() as ctx:
        y = sb(ctx, "c_y", [P, 2, TOPK, D], F32)
        x2 = sb(ctx, "c_x2", [P, 2, D], F32)
        bd = sb(ctx, "c_bd", [NE, D], F32)
        gf = sb(ctx, "c_gf", [P, D], F32)
        acc = sb(ctx, "c_acc", [P, 2, D], F32)
        res = sb(ctx, "c_res", [P, 2, D], F32)
        sq = sb(ctx, "c_sq", [P, D], F32)
        nrm = sb(ctx, "c_nrm", [P, NT, 4], F32)
        ps = m.psum(ctx, "ps7", [P, 2, D])
        once_in = sem("c_once_in")
        y_in = [sem(f"c_y_in{i}") for i in range(2)]
        biased = sem("c_biased")
        weighed = sem("c_weighed")
        summed = sem("c_summed")
        gated = sem("c_gated")
        x3 = sem("c_x3")
        sumsq = sem("c_sumsq")
        logd = sem("c_logd")
        rstd = sem("c_rstd")
        done = sem("c_done")
        out_done = [sem(f"c_out{i}") for i in range(2)]
        block = ctx.enter_context(nc.Block())

        @block.sync
        def _(sp):
            sp.dma_start(bd[:], m.b_down[0]).then_inc(once_in, 16)
            sp.dma_start(gf[:], m.final_g.rearrange("(a d) -> a d", a=1).to_broadcast([P, D])).then_inc(once_in, 16)
            for t in range(NT):
                b = t % 2
                if t >= 2:
                    sp.wait_ge(x3, t - 1)
                sp.dma_start(y[:, b], m.y4.rearrange("(t p k) n -> t p k n", p=P, k=TOPK)[t]).then_inc(y_in[b], 16)
                sp.dma_start(x2[:, b], m.x2[t * P:(t + 1) * P, :]).then_inc(y_in[b], 16)

        @block.tensor
        def _(pe):
            pe.wait_ge(once_in, 32)
            for t in range(NT):
                if t >= 2:
                    pe.wait_ge(weighed, TOPK * (t - 2) + 1)
                for half in range(2):
                    cols = slice(half * N, (half + 1) * N)
                    ins = pe.matmul(ps[:, t % 2, cols], m.wcT[:, t], bd[:, cols], start=True, stop=True)
                ins.then_inc(biased, 1)

        @block.vector
        def _(dve):
            def scale(t):
                b = t % 2
                dve.wait_ge(rstd, t + 1)
                if t >= 2:
                    dve.wait_ge(out_done[b], 16 * (t // 2))
                dve.scalar_tensor_tensor(out=res[:, b], in0=acc[:, b], scalar=nrm[:, t, 2:3], in1=gf[:], op0=ALU.mult, op1=ALU.mult).then_inc(done, 1)

            dve.wait_ge(once_in, 32)
            for t in range(NT):
                b = t % 2
                dve.wait_ge(y_in[b], 32 * (t // 2 + 1))
                dve.wait_ge(biased, t + 1)
                if t >= 2:
                    dve.wait_ge(done, t - 1)
                for k in range(TOPK):
                    if k:
                        dve.wait_ge(weighed, TOPK * t + k)
                    dve.scalar_tensor_tensor(out=acc[:, b], in0=y[:, b, k], scalar=m.wtop[:, t, k:k + 1], in1=acc[:, b] if k else ps[:, b],
                                             op0=ALU.mult, op1=ALU.add).then_inc(weighed, 1)
                dve.wait_ge(weighed, TOPK * (t + 1))
                dve.tensor_tensor(acc[:, b], acc[:, b], m.gate2[:], ALU.mult).then_inc(gated, 1)
                dve.wait_ge(gated, t + 1)
                dve.tensor_tensor(acc[:, b], acc[:, b], x2[:, b], ALU.add).then_inc(x3, 1)
                if t:
                    scale(t - 1)
            scale(NT - 1)

        @block.scalar
        def _(act):
            for t in range(NT):
                b = t % 2
                act.wait_ge(x3, t + 1)
                act.activation(sq[:], acc[:, b], ACT.Square, accum_out=nrm[:, t, 0:1]).then_inc(sumsq, 1)
                act.wait_ge(sumsq, t + 1)
                act.activation(nrm[:, t, 1:2], nrm[:, t, 0:1], ACT.Ln, scale=1.0 / D, bias=m.eps[:, 0:1]).then_inc(logd, 1)
                act.wait_ge(logd, t + 1)
                act.activation(nrm[:, t, 2:3], nrm[:, t, 1:2], ACT.Exp, scale=-0.5).then_inc(rstd, 1)
                act.wait_ge(done, t + 1)
                act.dma_start(m.out[0, t * P:(t + 1) * P, :], res[:, b]).then_inc(out_done[b], 16)
            for b in range(2):
                act.wait_ge(out_done[b], 16 * (NT // 2))


def build(nc, x, c, w_ada, b_ada, norm1_g, w_in, lambda_q1, lambda_k1, lambda_q2, lambda_k2, diff_norm_g, w_alpha_up, b_alpha,
          gla_norm_g, w_branch_diff, w_branch_gla, w_out, norm2_g, w_router, b_router, w_gate_up, b_gate_up, w_down, b_down,
          final_norm_g, out):
    with ExitStack() as ctx:
        m = Memory()
        m.x, m.c_, m.w_ada, m.b_ada, m.norm1_g, m.w_in = x, c, w_ada, b_ada, norm1_g, w_in
        m.lambda_q1, m.lambda_k1, m.lambda_q2, m.lambda_k2 = lambda_q1, lambda_k1, lambda_q2, lambda_k2
        m.diff_norm_g, m.w_alpha_up, m.b_alpha, m.gla_norm_g = diff_norm_g, w_alpha_up, b_alpha, gla_norm_g
        m.w_branch_diff, m.w_branch_gla, m.w_out, m.norm2_g = w_branch_diff, w_branch_gla, w_out, norm2_g
        m.w_router, m.b_router, m.w_gate_up, m.b_gate_up = w_router, b_router, w_gate_up, b_gate_up
        m.w_down, m.b_down, m.final_g, m.out = w_down, b_down, final_norm_g, out

        def dram(name, shape, dt=F32):
            return nc.dram_tensor(name, shape, dt, kind="Internal").ap()

        m.by_token = dram("proj_by_token", [4, SEQ, N])
        m.qkT = dram("qk_transposed", [2, N, SEQ])
        m.gatesT = dram("gates_transposed", [4, N, SEQ])
        m.lrT = dram("low_rank_transposed", [RANK, SEQ])
        m.x2 = dram("residual", [SEQ, D])
        m.h2 = dram("ffn_input", [SEQ, D])
        m.lists = dram("expert_lists", [NE * LIST, 2], I32)
        m.y4 = dram("expert_rows", [SEQ * TOPK, D])

        PASSED[:] = [nc.alloc_semaphore("passed")]
        phase_sems = []

        def sem(name):
            phase_sems.append(nc.alloc_semaphore(name))
            return phase_sems[-1]

        def end_phase():
            nc.clear_and_free_semaphores(phase_sems)
            phase_sems.clear()
            nc.all_engine_barrier()

        m.sem = sem
        m.scoped = lambda c, name, shape, dt: c.enter_context(nc.sbuf_tensor(name, shape, dt))
        m.psum = lambda c, name, shape: c.enter_context(nc.psum_tensor(name, shape, F32))
        sb = lambda name, shape, dt: m.scoped(ctx, name, shape, dt)
        m.gate2 = sb("gate2", [P, D], F32)
        m.ident = sb("ident", [P, P], F32)
        m.eps = sb("eps", [P, 1], F32)
        m.cols = sb("norm_cols", [P, 2], F32)
        m.logits = sb("logits", [P, NT, NE], F32)
        m.wtop = sb("top_weights", [P, NT, TOPK], F32)
        m.wcT = sb("weights_transposed", [NE, NT, P], F32)
        m.table = sb("rounds", [1, MAX_ROUNDS + 2, 4], I32)
        m.rounds = sb("round_count", [1, 1], I32)

        vectors = ExitStack()
        m.mod = m.scoped(vectors, "mod", [P, 5 * D], F32)
        with ExitStack() as scope:
            m.hTH = m.scoped(scope, "hT_hi", [P, KT, SEQ], F32R)
            m.hTL = m.scoped(scope, "hT_lo", [P, KT, SEQ], F32R)
            phase_modulate(nc, m)
            end_phase()
            phase_project(nc, m)
            end_phase()
        with ExitStack() as merged:
            with ExitStack() as scope:
                m.oTH = scope.enter_context(nc.sbuf_tensor("oT_hi", [P, 2 * HEADS, SEQ], F32R, side="right"))
                m.oTL = scope.enter_context(nc.sbuf_tensor("oT_lo", [P, 2 * HEADS, SEQ], F32R, side="right"))
                phase_gla(nc, m)
                end_phase()
                phase_attention(nc, m)
                end_phase()
                m.mTH = m.scoped(merged, "mergedT_hi", [P, KT, SEQ], F32R)
                m.mTL = m.scoped(merged, "mergedT_lo", [P, KT, SEQ], F32R)
                phase_merge(nc, m)
                end_phase()
            phase_out(nc, m)
            end_phase()
        vectors.close()
        with ExitStack() as raw:
            m.gu_raw = m.scoped(raw, "gu_raw", [P, 2, KT, 2, FC], F32)
            m.dn_raw = m.scoped(raw, "dn_raw", [P, 2, FC // P, D], F32)
            m.gu_bias = m.scoped(raw, "gu_bias", [P, 2, 2, FC], F32)
            phase_route(nc, m)
            end_phase()
            phase_experts(nc, m)
            end_phase()
        phase_combine(nc, m)


_INS = ["x", "c", "w_ada", "b_ada", "norm1_g", "w_in", "lambda_q1", "lambda_k1", "lambda_q2", "lambda_k2", "diff_norm_g",
        "w_alpha_up", "b_alpha", "gla_norm_g", "w_branch_diff", "w_branch_gla", "w_out", "norm2_g", "w_router", "b_router",
        "w_gate_up", "b_gate_up", "w_down", "b_down", "final_norm_g"]


def kernel(**inputs):
    import numpy as _np
    import concourse.bacc as _bacc
    from concourse import mybir as _mybir
    from concourse.bass_utils import run_bass_kernel_spmd as _run

    nc = _bacc.Bacc("TRN2", target_bir_lowering=False, num_devices=1)
    arrays, args = {}, []
    for name in _INS:
        a = _np.ascontiguousarray(inputs[name])
        arrays[f"in_{name}_dram"] = a
        args.append(nc.dram_tensor(f"in_{name}_dram", a.shape, _mybir.dt.from_np(a.dtype), kind="ExternalInput").ap())
    args.append(nc.dram_tensor("out_0_dram", (1, SEQ, D), _mybir.dt.float32, kind="ExternalOutput").ap())
    build(nc, *args)
    r = _run(nc, [arrays], core_ids=[0])
    return r.results[0]["out_0_dram"]
```
